# Optimizing a Trainium2 kernel written in Bass

```python
import math
import jax, jax.numpy as jnp
from jax import lax
import numpy as np

D_MODEL = 1024
BATCH = 1
SEQ = 512
DEPTH = 1
DEC_BATCH = 1
DEC_SEQ = 512
PAST_LEN = 128

ATT_HEADS = 16
ATT_KV_HEADS = 4
ATT_REP = ATT_HEADS // ATT_KV_HEADS
HEAD_DIM = 64
ATT_WIDTH = ATT_HEADS * HEAD_DIM
KV_WIDTH = ATT_KV_HEADS * HEAD_DIM
WINDOW = 128
BLOCK = 128
SSM_INNER = 2 * D_MODEL
SSM_HEAD_DIM = 64
SSM_HEADS = SSM_INNER // SSM_HEAD_DIM
SSM_GROUPS = 4
SSM_REP = SSM_HEADS // SSM_GROUPS
SSM_STATE = 128
SSM_GN = SSM_GROUPS * SSM_STATE
CONV_WIDTH = 5
CONV_DIM = SSM_INNER + 2 * SSM_GN
CHUNK = 128
N_BRANCH = 2
N_IN = ATT_WIDTH + 2 * KV_WIDTH + SSM_INNER + CONV_DIM + 2 * SSM_HEADS + N_BRANCH * D_MODEL
MEM_TOKENS = 256
X_HEADS = 4
X_HEAD_DIM = D_MODEL // X_HEADS
X_WIDTH = X_HEADS * X_HEAD_DIM
FFN_HIDDEN = -(-8 * D_MODEL // (3 * 256)) * 256
EPS = 1e-6

kernel_name = "hybrid_bidir_swa_ssd_encoder"

def rms_norm(x, g):
    x32 = x.astype(jnp.float32)
    y = x32 * lax.rsqrt(jnp.mean(x32 * x32, axis=-1, keepdims=True) + EPS)
    return (y * g.astype(jnp.float32)).astype(x.dtype)

def alibi_slopes(n_heads):
    return jnp.exp2(-8.0 * jnp.arange(1, n_heads + 1, dtype=jnp.float32) / n_heads)

def windowed_gqa(q, k, v, sink):
    b, L, _ = q.shape
    nb = L // BLOCK
    qb = q.reshape(b, nb, BLOCK, ATT_KV_HEADS, ATT_REP, HEAD_DIM)
    pad = ((0, 0), (BLOCK, BLOCK), (0, 0))
    kp = jnp.pad(k, pad).reshape(b, nb + 2, BLOCK, ATT_KV_HEADS, HEAD_DIM)
    vp = jnp.pad(v, pad).reshape(b, nb + 2, BLOCK, ATT_KV_HEADS, HEAD_DIM)
    kb = jnp.concatenate([kp[:, :-2], kp[:, 1:-1], kp[:, 2:]], axis=2)
    vb = jnp.concatenate([vp[:, :-2], vp[:, 1:-1], vp[:, 2:]], axis=2)
    s = jnp.einsum('bnqgrd,bnkgd->bngrqk', qb, kb).astype(jnp.float32) * (HEAD_DIM ** -0.5)
    blk = jnp.arange(nb)[:, None] * BLOCK
    qpos = blk + jnp.arange(BLOCK)[None, :]
    kpos = blk - BLOCK + jnp.arange(3 * BLOCK)[None, :]
    dist = jnp.abs(qpos[:, :, None] - kpos[:, None, :])
    valid = (dist <= WINDOW) & ((kpos >= 0) & (kpos < L))[:, None, :]
    slopes = alibi_slopes(ATT_HEADS).reshape(ATT_KV_HEADS, ATT_REP)
    bias = -slopes[None, :, :, None, None] * dist[:, None, None].astype(jnp.float32)
    s = jnp.where(valid[:, None, None], s + bias, -jnp.inf)
    sink_b = sink.astype(jnp.float32).reshape(ATT_KV_HEADS, ATT_REP)[None, None, :, :, None, None]
    m = jnp.maximum(jnp.max(s, axis=-1, keepdims=True), sink_b)
    p = jnp.exp(s - m)
    denom = jnp.sum(p, axis=-1, keepdims=True) + jnp.exp(sink_b - m)
    probs = (p / denom).astype(v.dtype)
    o = jnp.einsum('bngrqk,bnkgd->bnqgrd', probs, vb)
    return o.reshape(b, L, ATT_WIDTH)

def ssd_chunked(x, dt, a, bm, cm):
    b, L = x.shape[:2]
    nc = L // CHUNK
    x = x.reshape(b, nc, CHUNK, SSM_GROUPS, SSM_REP, SSM_HEAD_DIM)
    dt = dt.reshape(b, nc, CHUNK, SSM_GROUPS, SSM_REP)
    bm = bm.reshape(b, nc, CHUNK, SSM_GROUPS, SSM_STATE)
    cm = cm.reshape(b, nc, CHUNK, SSM_GROUPS, SSM_STATE)
    acum = jnp.cumsum(jnp.moveaxis(dt * a, 2, -1), axis=-1)
    xdt = x * dt[..., None]
    lower = jnp.tril(jnp.ones((CHUNK, CHUNK), dtype=bool))
    seg = acum[..., :, None] - acum[..., None, :]
    decay = jnp.exp(jnp.where(lower, seg, -jnp.inf))
    cb = jnp.einsum('bclgn,bcsgn->bcgls', cm, bm)
    y_diag = jnp.einsum('bcgrls,bcsgrp->bclgrp', cb[:, :, :, None] * decay, xdt)
    decay_states = jnp.exp(acum[..., -1:] - acum)
    states = jnp.einsum('bcsgn,bcgrs,bcsgrp->bcgrpn', bm, decay_states, xdt)
    chunk_decay = jnp.exp(acum[..., -1])

    def step(carry, inp):
        st, dec = inp
        return carry * dec[..., None, None] + st, carry

    init = jnp.zeros((b, SSM_GROUPS, SSM_REP, SSM_HEAD_DIM, SSM_STATE), jnp.float32)
    _, s_in = lax.scan(step, init, (jnp.moveaxis(states, 1, 0), jnp.moveaxis(chunk_decay, 1, 0)))
    s_in = jnp.moveaxis(s_in, 0, 1)
    y_off = jnp.einsum('bclgn,bcgrpn,bcgrl->bclgrp', cm, s_in, jnp.exp(acum))
    return (y_diag + y_off).reshape(b, L, SSM_GROUPS, SSM_REP, SSM_HEAD_DIM)

def ssd_branch(xbc, z, dt_raw, conv_w, conv_b, a_log, dt_bias, d_skip, ssm_norm):
    b, L, _ = xbc.shape
    xbc = lax.conv_general_dilated(
        xbc, conv_w[:, None, :].astype(xbc.dtype), (1,),
        [(CONV_WIDTH // 2, CONV_WIDTH // 2)],
        dimension_numbers=('NWC', 'WIO', 'NWC'), feature_group_count=CONV_DIM)
    xbc = jax.nn.silu(xbc + conv_b.astype(xbc.dtype)).astype(jnp.float32)
    gr = (SSM_GROUPS, SSM_REP)
    xs = xbc[..., :SSM_INNER].reshape(b, L, SSM_GROUPS, SSM_REP, SSM_HEAD_DIM)
    bm = xbc[..., SSM_INNER:SSM_INNER + SSM_GN].reshape(b, L, SSM_GROUPS, SSM_STATE)
    cm = xbc[..., SSM_INNER + SSM_GN:].reshape(b, L, SSM_GROUPS, SSM_STATE)
    dt = jax.nn.softplus(dt_raw.astype(jnp.float32).reshape(b, L, 2, SSM_HEADS)
                         + dt_bias.astype(jnp.float32))
    a = -jnp.exp(a_log.astype(jnp.float32))
    flip = lambda t: jnp.flip(t, axis=1)
    y_fwd = ssd_chunked(xs, dt[:, :, 0].reshape(b, L, *gr), a[0].reshape(gr), bm, cm)
    y_bwd = flip(ssd_chunked(flip(xs), flip(dt[:, :, 1]).reshape(b, L, *gr), a[1].reshape(gr),
                             flip(bm), flip(cm)))
    y = y_fwd + y_bwd + d_skip.astype(jnp.float32).reshape(gr)[..., None] * xs
    y = y.reshape(b, L, SSM_INNER) * jax.nn.silu(z.astype(jnp.float32))
    return rms_norm(y, ssm_norm).astype(z.dtype)

def mixer_block(x, norm_mix, w_in, conv_w, conv_b, attn_sink, a_log, dt_bias, d_skip,
                ssm_norm, w_br_attn, w_br_ssm, w_out):
    b, L, _ = x.shape
    u = rms_norm(x, norm_mix)
    proj = u @ w_in
    sizes = [ATT_WIDTH, KV_WIDTH, KV_WIDTH, SSM_INNER, CONV_DIM, 2 * SSM_HEADS, N_BRANCH * D_MODEL]
    cuts = [int(c) for c in np.cumsum(sizes)[:-1]]
    q, k, v, z, xbc, dt_raw, gate_raw = jnp.split(proj, cuts, axis=-1)
    y_attn = windowed_gqa(q, k, v, attn_sink) @ w_br_attn
    y_ssm = ssd_branch(xbc, z, dt_raw, conv_w, conv_b, a_log, dt_bias, d_skip, ssm_norm) @ w_br_ssm
    gates = jax.nn.sigmoid(gate_raw.astype(jnp.float32)).astype(x.dtype)
    merged = gates[..., :D_MODEL] * y_attn + gates[..., D_MODEL:] * y_ssm
    return merged @ w_out

def cross_attention(x, mem, norm_cross, norm_mem, w_q, w_kv, w_o):
    b, L, _ = x.shape
    M = mem.shape[1]
    u = rms_norm(x, norm_cross)
    mn = rms_norm(mem, norm_mem)
    q = (u @ w_q).reshape(b, L, X_HEADS, X_HEAD_DIM)
    kv = (mn @ w_kv).reshape(b, M, 2, X_HEADS, X_HEAD_DIM)
    k, v = kv[:, :, 0], kv[:, :, 1]
    s = jnp.einsum('bqhd,bkhd->bhqk', q, k).astype(jnp.float32) * (X_HEAD_DIM ** -0.5)
    p = jax.nn.softmax(s, axis=-1).astype(v.dtype)
    o = jnp.einsum('bhqk,bkhd->bqhd', p, v).reshape(b, L, X_WIDTH)
    return o @ w_o

def swiglu_ffn(x, norm_ffn, w_gate_up, w_down):
    u = rms_norm(x, norm_ffn)
    gu = u @ w_gate_up
    return (jax.nn.silu(gu[..., :FFN_HIDDEN]) * gu[..., FFN_HIDDEN:]) @ w_down

def trunk(x, mem, params):
    (norm_mix, w_in, conv_w, conv_b, attn_sink, a_log, dt_bias, d_skip, ssm_norm,
     w_br_attn, w_br_ssm, w_out, norm_cross, norm_mem, w_q_cross, w_kv_cross, w_o_cross,
     norm_ffn, w_gate_up, w_down, norm_final) = params
    for l in range(DEPTH):
        x = x + mixer_block(x, norm_mix[l], w_in[l], conv_w[l], conv_b[l], attn_sink[l], a_log[l],
                            dt_bias[l], d_skip[l], ssm_norm[l], w_br_attn[l], w_br_ssm[l], w_out[l])
        x = x + cross_attention(x, mem, norm_cross[l], norm_mem[l], w_q_cross[l], w_kv_cross[l],
                                w_o_cross[l])
        x = x + swiglu_ffn(x, norm_ffn[l], w_gate_up[l], w_down[l])
    return rms_norm(x, norm_final)

def setup_inputs(seed: int = 0) -> dict:
    key = jax.random.key(seed)
    ks = jax.random.split(key, 32)
    f32 = jnp.float32

    def nrm(k, shape, fan_in):
        return jax.random.normal(k, shape, f32) * (fan_in ** -0.5)

    def gain(k, shape):
        return 1.0 + 0.01 * jax.random.normal(k, shape, f32)

    u = jax.random.uniform(ks[8], (DEPTH, 2, SSM_HEADS), f32)
    dt0 = jnp.exp(u * (math.log(0.1) - math.log(0.001)) + math.log(0.001))
    dt_bias = dt0 + jnp.log(-jnp.expm1(-dt0))
    a_log = jnp.log(jax.random.uniform(ks[9], (DEPTH, 2, SSM_HEADS), f32, 1.0, 16.0))
    return {
        "x_prompt": jax.random.normal(ks[0], (BATCH, SEQ, D_MODEL), f32),
        "x_sample": jax.random.normal(ks[1], (DEC_BATCH, DEC_SEQ, D_MODEL), f32),
        "mem_prompt": jax.random.normal(ks[2], (BATCH, MEM_TOKENS, D_MODEL), f32),
        "mem_sample": jax.random.normal(ks[3], (DEC_BATCH, MEM_TOKENS, D_MODEL), f32),
        "norm_mix": gain(ks[4], (DEPTH, D_MODEL)),
        "w_in": nrm(ks[5], (DEPTH, D_MODEL, N_IN), D_MODEL),
        "conv_w": nrm(ks[6], (DEPTH, CONV_WIDTH, CONV_DIM), CONV_WIDTH),
        "conv_b": 0.01 * jax.random.normal(ks[7], (DEPTH, CONV_DIM), f32),
        "attn_sink": jax.random.normal(ks[10], (DEPTH, ATT_HEADS), f32),
        "a_log": a_log,
        "dt_bias": dt_bias,
        "d_skip": 1.0 + 0.1 * jax.random.normal(ks[11], (DEPTH, SSM_HEADS), f32),
        "ssm_norm": gain(ks[12], (DEPTH, SSM_INNER)),
        "w_br_attn": nrm(ks[13], (DEPTH, ATT_WIDTH, D_MODEL), ATT_WIDTH),
        "w_br_ssm": nrm(ks[14], (DEPTH, SSM_INNER, D_MODEL), SSM_INNER),
        "w_out": nrm(ks[15], (DEPTH, D_MODEL, D_MODEL), D_MODEL),
        "norm_cross": gain(ks[16], (DEPTH, D_MODEL)),
        "norm_mem": gain(ks[17], (DEPTH, D_MODEL)),
        "w_q_cross": nrm(ks[18], (DEPTH, D_MODEL, X_WIDTH), D_MODEL),
        "w_kv_cross": nrm(ks[19], (DEPTH, D_MODEL, 2 * X_WIDTH), D_MODEL),
        "w_o_cross": nrm(ks[20], (DEPTH, X_WIDTH, D_MODEL), X_WIDTH),
        "norm_ffn": gain(ks[21], (DEPTH, D_MODEL)),
        "w_gate_up": nrm(ks[22], (DEPTH, D_MODEL, 2 * FFN_HIDDEN), D_MODEL),
        "w_down": nrm(ks[23], (DEPTH, FFN_HIDDEN, D_MODEL), FFN_HIDDEN),
        "norm_final": gain(ks[24], (D_MODEL,)),
    }

def reference(x_prompt, x_sample, mem_prompt, mem_sample, norm_mix, w_in, conv_w, conv_b,
              attn_sink, a_log, dt_bias, d_skip, ssm_norm, w_br_attn, w_br_ssm, w_out,
              norm_cross, norm_mem, w_q_cross, w_kv_cross, w_o_cross, norm_ffn, w_gate_up,
              w_down, norm_final):
    params = (norm_mix, w_in, conv_w, conv_b, attn_sink, a_log, dt_bias, d_skip, ssm_norm,
              w_br_attn, w_br_ssm, w_out, norm_cross, norm_mem, w_q_cross, w_kv_cross, w_o_cross,
              norm_ffn, w_gate_up, w_down, norm_final)
    y_prompt = trunk(x_prompt, mem_prompt, params)
    y_sample = trunk(x_sample, mem_sample, params)
    return (y_prompt, y_sample)


_drawn_inputs = setup_inputs


def setup_inputs(seed=0):
    import zlib

    import numpy as np

    out = dict(_drawn_inputs(seed))
    spreads = {}
    factors = {'norm_mix': 6.94,
     'conv_b': 6.516,
     'attn_sink': 3.302,
     'ssm_norm': 8.0,
     'norm_cross': 8.0,
     'norm_mem': 8.0,
     'norm_ffn': 8.0,
     'norm_final': 5.7}
    for name, (base, spread) in spreads.items():
        noise = np.random.default_rng([zlib.crc32(name.encode()), seed]).standard_normal(out[name].shape)
        drawn = base * np.exp(spread * noise) if base else spread * noise
        out[name] = __import__('jax').numpy.asarray(drawn.astype(out[name].dtype))
    for name, factor in factors.items():
        out[name] = (out[name] * factor).astype(out[name].dtype)
    return out
```

```python
from contextlib import ExitStack

import numpy as np
import concourse.bass as bass
from concourse import mybir

F32 = mybir.dt.float32
F32R = mybir.dt.float32r
ACT = mybir.ActivationFunctionType
ALU = mybir.AluOpType
AX = mybir.AxisListType

P = 128
NSEQ = 2
SEQ = 512
TOK = NSEQ * SEQ
TT = TOK // P
D = 1024
KT = D // P
EPS = 1e-6
HEADS, KVH, HD = 16, 4, 64
BLOCKS = SEQ // P
GROUPS, GH, NSTATE = 4, 8, 128
SSMH = GROUPS * GH
GW = GH * 64
XT = GW // P
CT = XT + 2
TAPS = 5
HALO = TAPS // 2
MEM = 256
MT = NSEQ * MEM // P
XHD = 256
XH = D // XHD
HID = 2816
HT = HID // P
FAR = 1e35
BANK = 512

Q0, K0, V0, Z0, C0 = 0, 8, 10, 12, 28
GATE0 = C0 + GROUPS * CT
NPROJ = GATE0 + 16

U_PROJ = 0
U_WB = U_PROJ + NPROJ
U_WA = U_WB + 16
U_OUT = U_WA + 8
U_KV = U_OUT + 8
U_Q = U_KV + 16
U_O = U_Q + 8
U_FFN = U_O + 8
NUNITS = U_FFN + 3 * HT

CON_ID, CON_ONES, CON_UP, CON_LOW = 0, 128, 256, 384
CON_SEL, CON_NSEL, CON_DIST = 512, 576, 640
NCON = CON_DIST + 3 * P
G_MIX, G_CROSS, G_MEM, G_FFN, G_SSM = 0, 8, 16, 24, 32
NG = 48
R_ALOG, R_DTB, R_SKIP, R_SINK, R_FINAL = 0, 64, 128, 160, 176
NR = R_FINAL + D


def constants():
    i = np.arange(P)
    c = np.zeros((P, NCON), np.float32)
    c[:, CON_ID:CON_ID + P] = np.eye(P)
    c[:, CON_ONES:CON_ONES + P] = 1.0
    c[:, CON_UP:CON_UP + P] = i[:, None] <= i[None, :]
    c[:, CON_LOW:CON_LOW + P] = i[:, None] >= i[None, :]
    sel = (i[:, None] % 64 == np.arange(64)[None, :]).astype(np.float32)
    c[:, CON_SEL:CON_SEL + 64] = sel
    c[:, CON_NSEL:CON_NSEL + 64] = -sel
    k = np.arange(3 * P) - P
    dist = np.abs(i[:, None] - k[None, :]).astype(np.float32)
    c[:, CON_DIST:] = np.where(dist <= 128, dist, FAR)
    return c


class Core:

    def semaphore(self, name):
        self.stage_sems.append(self.nc.alloc_semaphore(name=name))
        return self.stage_sems[-1]

    def recycle(self):
        self.nc.clear_and_free_semaphores(self.stage_sems)
        self.stage_sems = []
        self.nc.all_engine_barrier()


def open_core(nc, ctx, dram):
    m = Core()
    m.nc, m.dram, m.stage_sems = nc, dram, []

    def sb(name, shape, dt=F32):
        return ctx.enter_context(nc.sbuf_tensor(name, shape, dt))

    m.con = sb("con", [P, NCON])
    m.gains = sb("gains", [P, NG])
    m.rows = sb("rows", [P, NR])
    m.w_raw = sb("w_raw", [P, 2, 1024])
    m.w_hi = sb("w_hi", [P, 2, 1024], F32R)
    m.w_lo = sb("w_lo", [P, 2, 1024], F32R)
    m.ps = ctx.enter_context(nc.psum_tensor("ps", [P, 8, BANK], F32))
    m.w_landed = [nc.alloc_semaphore(name=f"w_landed{r}") for r in range(2)]
    m.w_hi_ready = nc.alloc_semaphore(name="w_hi_ready")
    m.w_lo_ready = nc.alloc_semaphore(name="w_lo_ready")
    m.w_used = nc.alloc_semaphore(name="w_used")
    return m



def load_unit(sp, m, r, rows):
    sp.dma_start(m.w_raw[:, r], rows).then_inc(m.w_landed[r], 16)


def stream_weights(sp, m, first, n):
    end = min(first + n + 2, NUNITS)
    pairs = (end - first - 2) // 2
    if pairs <= 0:
        return
    w = m.dram["w_all"]
    with sp.Fori(0, pairs) as i:
        for r in range(2):
            row = sp.snap(i * (2 * P) + (first + 2 + r) * P)
            sp.wait_ge(m.w_lo_ready, i * 2 + (first + 1 + r))
            load_unit(sp, m, r, w[bass.ds(row, P), :])


def split_hi(act, m, r, landed, used):
    act.wait_ge(m.w_landed[r], landed)
    if used is not None:
        act.wait_ge(m.w_used, used)
    act.activation(m.w_hi[:, r], m.w_raw[:, r], ACT.Copy).then_inc(m.w_hi_ready, 1)


def split_lo(dve, m, r, hi_ready):
    dve.wait_ge(m.w_hi_ready, hi_ready)
    dve.tensor_tensor(m.w_lo[:, r], m.w_raw[:, r], m.w_hi[:, r].bitcast(F32),
                      ALU.subtract).then_inc(m.w_lo_ready, 1)


class Units:

    def __init__(self, m, first):
        self.m, self.first = m, first

    def hi(self, act, at, r, first=False):
        u = self.first + at
        split_hi(act, self.m, r, ring_landed(self.first, at, r), None if first else u - 1)

    def lo(self, dve, at, r):
        split_lo(dve, self.m, r, self.first + at + 1)

    def products_done(self, eng, at):
        eng.wait_ge(self.m.w_used, self.first + at + 1)

    def wait(self, pe, at):
        pe.wait_ge(self.m.w_lo_ready, self.first + at + 1)


def ring_landed(first, at, r):
    return (at - r) * 8 + (first // 2 + 1) * 16


def products(pe, out, pairs, last_of_group=True, first_of_group=True):
    n = len(pairs)
    for k, ((l_hi, l_lo), (r_hi, r_lo)) in enumerate(pairs):
        for q, (a, b) in enumerate(((l_hi, r_hi), (l_hi, r_lo), (l_lo, r_hi))):
            mm = pe.matmul(out, a, b, start=first_of_group and k == 0 and q == 0,
                           stop=last_of_group and k == n - 1 and q == 2)
    return mm


def wslice(m, r, a, b):
    return m.w_hi[:, r, a:b], m.w_lo[:, r, a:b]



def prep_stage(m):
    nc, d = m.nc, m.dram
    with ExitStack() as ctx:
        landed = m.semaphore("const_landed")
        block = ctx.enter_context(nc.Block())

        @block.sync
        def _(sp):
            sp.dma_start(m.con[:], d["con"]).then_inc(landed, 16)
            sp.dma_start(m.gains[:], d["gains"]).then_inc(landed, 16)
            sp.dma_start(m.rows[:], d["rows"].partition_broadcast(P)).then_inc(landed, 16)
            for r in range(2):
                load_unit(sp, m, r, d["w_all"][r * P:(r + 1) * P, :])
            sp.wait_ge(landed, 48)


def norm_stage(m, name, source, gain, hi, lo, tiles, source_is_dram):
    nc = m.nc
    wide = tiles // 4
    with ExitStack() as ctx:
        sem = lambda n: m.semaphore(f"{name}_{n}")
        x = ctx.enter_context(nc.sbuf_tensor(f"{name}_x", [P, tiles, D], F32)) if source_is_dram else source
        xn = ctx.enter_context(nc.sbuf_tensor(f"{name}_xn", [P, tiles, D], F32))
        ss = ctx.enter_context(nc.sbuf_tensor(f"{name}_ss", [P, 3, tiles], F32))
        landed = [sem(f"landed{t}") for t in range(tiles)] if source_is_dram else []
        squared, mean, root, rstd, scaled = sem("squared"), sem("mean"), sem("root"), sem("rstd"), sem("scaled")
        turned, hi_done, lo_done = sem("turned"), sem("hi_done"), sem("lo_done")
        block = ctx.enter_context(nc.Block())
        groups = [(n, j) for n in range(wide) for j in range(KT)]

        if source_is_dram:
            @block.sync
            def _(sp):
                for t in range(tiles):
                    sp.dma_start(x[:, t], source[t * P:(t + 1) * P, :]).then_inc(landed[t], 16)

        @block.scalar
        def _(act):
            for t in range(tiles):
                if source_is_dram:
                    act.wait_ge(landed[t], 16)
                act.activation(xn[:, t], x[:, t], ACT.Square, accum_out=ss[:, 0, t:t + 1]).then_inc(squared, 1)
            act.wait_ge(mean, 1)
            act.activation(ss[:, 2], ss[:, 1], ACT.Sqrt).then_inc(root, 1)
            for i, (n, j) in enumerate(groups):
                act.wait_ge(turned, i + 1)
                act.activation(hi[:, j, n * BANK:(n + 1) * BANK], m.ps[:, 4 + i % 4], ACT.Copy,
                               scale=m.gains[:, gain + j:gain + j + 1]).then_inc(hi_done, 1)

        @block.vector
        def _(dve):
            dve.wait_ge(squared, tiles)
            dve.tensor_scalar(ss[:, 1], ss[:, 0], 1.0 / D, EPS, ALU.mult, ALU.add).then_inc(mean, 1)
            dve.wait_ge(root, 1)
            dve.reciprocal(ss[:, 0], ss[:, 2]).then_inc(rstd, 1)
            dve.wait_ge(rstd, 1)
            for t in range(tiles):
                dve.tensor_scalar(xn[:, t], x[:, t], ss[:, 0, t:t + 1], None, ALU.mult).then_inc(scaled, 1)
            for i, (n, j) in enumerate(groups):
                dve.wait_ge(hi_done, i + 1)
                dve.scalar_tensor_tensor(lo[:, j, n * BANK:(n + 1) * BANK], m.ps[:, 4 + i % 4],
                                         m.gains[:, gain + j:gain + j + 1],
                                         hi[:, j, n * BANK:(n + 1) * BANK].bitcast(F32),
                                         ALU.mult, ALU.subtract).then_inc(lo_done, 1)

        @block.tensor
        def _(pe):
            ident = m.con[:, CON_ID:CON_ID + P]
            for i, (n, j) in enumerate(groups):
                if j == 0:
                    pe.wait_ge(scaled, 4 * (n + 1))
                if i >= 4:
                    pe.wait_ge(lo_done, i - 3)
                for t in range(4):
                    mm = pe.transpose(m.ps[:, 4 + i % 4, t * P:(t + 1) * P],
                                      xn[:, 4 * n + t, j * P:(j + 1) * P], ident)
                mm.then_inc(turned, 1)


def projection_stage(m, u_hi, u_lo, dt_raw):
    nc, d = m.nc, m.dram
    segments = [(8, ACT.Copy, HD ** -0.5), (4, ACT.Copy, 1.0), (16, ACT.Silu, 1.0),
                (GROUPS * CT, ACT.Copy, 1.0), (16, ACT.Sigmoid, 1.0)]
    with ExitStack() as ctx:
        sem = lambda n: m.semaphore(f"proj_{n}")
        out = ctx.enter_context(nc.sbuf_tensor("proj_out", [P, 2, TOK], F32))
        w_dt = ctx.enter_context(nc.sbuf_tensor("w_dt", [P, KT * 64], F32))
        w_dt_hi = ctx.enter_context(nc.sbuf_tensor("w_dt_hi", [P, KT * 64], F32R))
        w_dt_lo = ctx.enter_context(nc.sbuf_tensor("w_dt_lo", [P, KT * 64], F32R))
        drained = sem("drained")
        stored = [sem(f"stored{r}") for r in range(2)]
        dt_landed, dt_hi, dt_lo, dt_done, dt_out = sem("dt_landed"), sem("dt_hi"), sem("dt_lo"), sem("dt_done"), sem("dt_out")
        block = ctx.enter_context(nc.Block())
        units = Units(m, U_PROJ)

        @block.sync
        def _(sp):
            sp.dma_start(w_dt[:], d["w_dt"]).then_inc(dt_landed, 16)
            stream_weights(sp, m, U_PROJ, NPROJ)

        @block.scalar
        def _(act):
            act.wait_ge(dt_landed, 16)
            act.activation(w_dt_hi[:], w_dt[:], ACT.Copy).then_inc(dt_hi, 1)

            def evacuate(at, r, func, scale, peel):
                row = act.snap(at * P) if not isinstance(at, int) else at * P
                if not peel:
                    act.wait_ge(stored[r], (at - r) * 8)
                units.products_done(act, at)
                act.activation(out[:, r], m.ps[:, 2 * r:2 * r + 2].rearrange("p a b -> p (a b)"), func,
                               scale=scale).then_inc(drained, 1)
                act.wait_ge(drained, at + 1)
                act.dma_start(d["proj"][bass.ds(row, P), :], out[:, r]).then_inc(stored[r], 16)

            t0 = 0
            for s, (n, func, scale) in enumerate(segments):
                def pair(at, first_unit, peel, last):
                    if first_unit:
                        units.hi(act, at, 0, first=True)
                    units.hi(act, at + 1, 1, first=first_unit)
                    evacuate(at, 0, func, scale, peel)
                    if not last:
                        units.hi(act, at + 2, 0)
                    evacuate(at + 1, 1, func, scale, peel)
                final = s == len(segments) - 1
                head = 1 if s == 0 else 0
                if head:
                    pair(t0, True, True, False)
                body = n // 2 - head - (1 if final else 0)
                with act.Fori(0, body) as i:
                    pair(i * 2 + (t0 + 2 * head), False, False, False)
                if final:
                    pair(t0 + n - 2, False, False, True)
                t0 += n
            for r in range(2):
                act.wait_ge(stored[r], NPROJ * 8)

        @block.vector
        def _(dve):
            dve.wait_ge(dt_hi, 1)
            dve.tensor_tensor(w_dt_lo[:], w_dt[:], w_dt_hi[:].bitcast(F32), ALU.subtract).then_inc(dt_lo, 1)
            with dve.Fori(0, NPROJ // 2) as i:
                for r in range(2):
                    units.lo(dve, i * 2 + r, r)
            dve.wait_ge(dt_done, 1)
            dve.tensor_copy(dt_raw[:].rearrange("p a b -> p (a b)"), m.ps[:, 7]).then_inc(dt_out, 1)

        @block.tensor
        def _(pe):
            pe.wait_ge(dt_lo, 1)
            for t in range(TT):
                s = slice(t * P, (t + 1) * P)
                mm = products(pe, m.ps[:, 7, t * 64:(t + 1) * 64],
                              [((u_hi[:, k, s], u_lo[:, k, s]),
                                (w_dt_hi[:, k * 64:(k + 1) * 64], w_dt_lo[:, k * 64:(k + 1) * 64]))
                               for k in range(KT)])
            mm.then_inc(dt_done, 1)

            def tile(at, r, peel):
                units.wait(pe, at)
                if not peel:
                    pe.wait_ge(drained, at - 1)
                for n in range(2):
                    s = slice(n * BANK, (n + 1) * BANK)
                    mm = products(pe, m.ps[:, 2 * r + n],
                                  [(wslice(m, r, k * P, (k + 1) * P), (u_hi[:, k, s], u_lo[:, k, s]))
                                   for k in range(KT)])
                mm.then_inc(m.w_used, 1)

            for r in range(2):
                tile(r, r, True)
            with pe.Fori(1, NPROJ // 2) as i:
                for r in range(2):
                    tile(i * 2 + r, r, False)


def step_stage(m, dt_raw, dt, a2, exp_a, w_in, dec, hl):
    nc = m.nc
    with ExitStack() as ctx:
        sem = lambda n: m.semaphore(f"step_{n}")
        tmp = [ctx.enter_context(nc.sbuf_tensor(f"step_t{i}", [P, TT, 64], F32)) for i in range(4)]
        neg_a = ctx.enter_context(nc.sbuf_tensor("neg_a", [P, 64], F32))
        dve_step, act_step, pe_step = sem("dve"), sem("act"), sem("pe")
        block = ctx.enter_context(nc.Block())
        flat = lambda ap: ap.rearrange("p a b -> p (a b)")
        bias = m.rows[:, R_DTB:R_DTB + 64].unsqueeze(1).to_broadcast([P, TT, 64])
        TERMS = 9

        n_dve = 0

        @block.vector
        def _(dve):
            nonlocal n_dve
            count = [0]

            def chain(ins):
                count[0] += 1
                ins.then_inc(dve_step, 1)
                dve.wait_ge(dve_step, count[0])

            x, mag, z, z2 = tmp
            chain(dve.tensor_tensor(x[:], dt_raw[:], bias, ALU.add))
            chain(dve.tensor_scalar(mag[:], x[:], -1.0, None, ALU.mult))
            chain(dve.tensor_tensor(mag[:], mag[:], x[:], ALU.min))
            dve.wait_ge(act_step, 1)
            chain(dve.tensor_scalar(z[:], mag[:], 2.0, None, ALU.add))
            chain(dve.reciprocal(z[:], z[:]))
            chain(dve.tensor_tensor(z[:], z[:], mag[:], ALU.mult))
            chain(dve.tensor_tensor(z2[:], z[:], z[:], ALU.mult))
            chain(dve.tensor_scalar(mag[:], z2[:], 2.0 / (2 * TERMS - 1), 2.0 / (2 * TERMS - 3), ALU.mult, ALU.add))
            for t in range(TERMS - 3, -1, -1):
                chain(dve.tensor_tensor(mag[:], mag[:], z2[:], ALU.mult))
                chain(dve.tensor_scalar(mag[:], mag[:], 2.0 / (2 * t + 1), None, ALU.add))
            chain(dve.tensor_tensor(mag[:], mag[:], z[:], ALU.mult))
            chain(dve.scalar_tensor_tensor(dt[:], x[:], 0.0, mag[:], ALU.max, ALU.add))
            dve.wait_ge(act_step, 2)
            chain(dve.tensor_scalar(neg_a[:], neg_a[:], -1.0, None, ALU.mult))
            dta = tmp[0]
            chain(dve.tensor_tensor(dta[:], dt[:], neg_a[:].unsqueeze(1).to_broadcast([P, TT, 64]), ALU.mult))
            n_dve = count[0]
            dve.wait_ge(pe_step, 1)
            for dup in range(2):
                for way in range(2):
                    src = m.ps[:, 4 + way, 0:TT * 32].rearrange("p (a b) -> p a b", a=TT)
                    chain(dve.tensor_copy(a2[:, :, dup, way * 32:way * 32 + 32], src))
            dve.wait_ge(pe_step, 2)
            tot = m.ps[:, 6].rearrange("p (a b) -> p a b", a=TT)
            chain(dve.tensor_tensor(tmp[1][:], tot, a2[:, :, 0, :], ALU.subtract))
            dve.wait_ge(act_step, 5)
            chain(dve.tensor_tensor(w_in[:], tmp[2][:], dt[:], ALU.mult))
            dve.wait_ge(pe_step, 3)
            both = m.ps[:, 0:2].rearrange("p a b -> p (a b)")
            chain(dve.tensor_copy(hl[:], both))
            chain(dve.tensor_tensor(hl[64:128, :], both[64:128], hl[64:128, :].bitcast(F32), ALU.subtract))

        @block.scalar
        def _(act):
            act.wait_ge(dve_step, 3)
            act.activation(tmp[1][:], tmp[1][:], ACT.Exp).then_inc(act_step, 1)
            act.activation(neg_a[:], m.rows[:, R_ALOG:R_ALOG + 64], ACT.Exp).then_inc(act_step, 1)
            act.wait_ge(dve_step, n_dve + 4)
            act.activation(exp_a[:], a2[:, :, 0, :], ACT.Exp).then_inc(act_step, 1)
            act.wait_ge(dve_step, n_dve + 5)
            act.activation(dec[:], m.ps[:, 6].rearrange("p (a b) -> p a b", a=TT), ACT.Exp).then_inc(act_step, 1)
            act.activation(tmp[2][:], tmp[1][:], ACT.Exp).then_inc(act_step, 1)

        @block.tensor
        def _(pe):
            dta = tmp[0]
            pe.wait_ge(dve_step, n_dve)
            for way, tri in ((0, CON_UP), (1, CON_LOW)):
                mm = pe.matmul(m.ps[:, 4 + way, 0:TT * 32], m.con[:, tri:tri + P],
                               dta[:, :, way * 32:way * 32 + 32], start=True, stop=True)
            mm.then_inc(pe_step, 1)
            pe.matmul(m.ps[:, 6], m.con[:, CON_ONES:CON_ONES + P], flat(dta[:]), start=True,
                      stop=True).then_inc(pe_step, 1)
            pe.wait_ge(dve_step, n_dve + 4)
            for c in range(TT):
                mm = pe.transpose(m.ps[:, c // 4, (c % 4) * P:(c % 4 + 1) * P], flat(a2[:, c]),
                                  m.con[:, CON_ID:CON_ID + P])
            mm.then_inc(pe_step, 1)


def bc(ap, n):
    return ap.unsqueeze(len(ap.shape)).to_broadcast([*ap.shape, n])


def ssd_stage(m, st4, hl):
    nc, d = m.nc, m.dram
    DT, EXPA, WIN, DEC = range(4)
    STEPS = 2 * TT
    NS = 12
    order = [(q, way, k) for q in range(NSEQ) for way in range(2) for k in range(BLOCKS - 1)]
    gives = lambda q, way, k: q * BLOCKS + (k if way == 0 else BLOCKS - 1 - k)
    index = {(way, gives(q, way, k) + (1 if way == 0 else -1)): n for n, (q, way, k) in enumerate(order)}
    with ExitStack() as ctx:
        sem = lambda n: m.semaphore(f"ssd_{n}")
        sb = lambda n, s, t=F32: ctx.enter_context(nc.sbuf_tensor(n, s, t))
        xpad = sb("xpad", [P, CT, NSEQ, SEQ + 2 * HALO])
        taps = sb("taps", [P, CT * (TAPS + 1)])
        conv = sb("conv", [P, CT, NSEQ, SEQ])
        xs = sb("xs", [P, TT, GW])
        b_tm = sb("b_tm", [P, TT, NSTATE])
        states = sb("states", [P, NS, GW])
        grp = sb("grp", [P, 4 * TT, 2, GH])
        skip = sb("skip", [P, GH])
        sel = sb("sel", [P, 2, GH, P], F32R)
        neg_sel = sb("neg_sel", [P, 2, GH, P], F32R)
        zy = sb("zy", [P, XT, TOK])
        xw = sb("xw", [P, 2, GW])
        fs = sb("fs", [P, 2, BANK])
        e = sb("e", [P, 2, BANK])
        tl = sb("tl", [P, 2, BANK])
        tu = sb("tu", [P, 2, BANK])
        cb = sb("cb", [P, 2, 2, P])
        y = sb("y", [P, 2, GW])
        off = sb("off", [P, 2, GW])
        flat_conv = lambda i: conv[:, i].rearrange("p a b -> p (a b)")
        bm_t, cm_t = flat_conv(XT), flat_conv(XT + 1)
        grp4 = grp[:].rearrange("p (a b) c d -> p a b c d", a=4)

        taps_landed, x_landed, z_landed = sem("taps_landed"), sem("x_landed"), sem("z_landed")
        pads, grp_ready, conv_step, conv_done = sem("pads"), sem("grp_ready"), sem("conv_step"), sem("conv_done")
        turned, tm_ready, sel_ready = sem("turned"), sem("tm_ready"), sem("sel_ready")
        xw_ready, st_done, decayed, st_ready = sem("xw_ready"), sem("st_done"), sem("decayed"), sem("st_ready")
        cb_done, cb_ready = sem("cb_done"), sem("cb_ready")
        f_done, b_done, f_copied, min_done, e_ready = sem("f_done"), sem("b_done"), sem("f_copied"), sem("min_done"), sem("e_ready")
        masked, t_sum, m_ready = sem("masked"), sem("t_sum"), sem("m_ready")
        y_done, skipped, y_read = sem("y_done"), sem("skipped"), sem("y_read")
        off_done, off_read, off_added = sem("off_done"), sem("off_read"), sem("off_added")
        y_turned, yz_ready, y_stored = sem("y_turned"), sem("yz_ready"), sem("y_stored")
        block = ctx.enter_context(nc.Block())

        offs = [[(way, index[way, c]) for way in range(2) if (way, c) in index] for c in range(TT)]
        off_before = [sum(len(o) for o in offs[:c]) for c in range(TT)]

        @block.sync
        def _(sp):
            def group(g, first):
                at = sp.snap if not first else int
                t_row, x_row = at(g * P), at(g * (CT * P) + C0 * P)
                z_row, y_row = at(g * (XT * P) + Z0 * P), at(g * (XT * P))
                if first:
                    sp.wait_ge(pads, 1)
                else:
                    sp.wait_ge(conv_step, g * (CT * TAPS))
                sp.dma_start(taps[:], d["taps"][bass.ds(t_row, P), :]).then_inc(taps_landed, 16)
                for i in range(CT):
                    src = d["proj"][bass.ds(x_row, CT * P), :][i * P:(i + 1) * P, :]
                    sp.dma_start(xpad[:, i, :, HALO:HALO + SEQ],
                                 src.rearrange("p (a b) -> p a b", a=NSEQ)).then_inc(x_landed, 16)
                if not first:
                    sp.wait_ge(y_stored, g * 16)
                sp.dma_start(zy[:], d["proj"][bass.ds(z_row, XT * P), :]
                             .rearrange("(a p) t -> p a t", p=P)).then_inc(z_landed, 16)
                sp.wait_ge(yz_ready, g * TT + TT)
                sp.dma_start(d["yt"][bass.ds(y_row, XT * P), :].rearrange("(a p) t -> p a t", p=P),
                             zy[:]).then_inc(y_stored, 16)
            group(0, True)
            with sp.Fori(1, GROUPS) as g:
                group(g, False)
            sp.wait_ge(y_stored, GROUPS * 16)

        @block.vector
        def _(dve):
            with dve.Fori(0, GROUPS) as g:
                col = dve.snap(g * GH)
                src = st4[:].rearrange("p a b (w h) -> p (a b) w h", w=2)[:, :, :, bass.ds(col, GH)]
                dve.tensor_scalar(grp[:], src, 1.0, None, ALU.mult).then_inc(grp_ready, 1)
                dve.tensor_scalar(skip[:], m.rows[:, R_SKIP:R_SKIP + SSMH][:, bass.ds(col, GH)], 1.0, None,
                                  ALU.mult).then_inc(grp_ready, 1)
                dve.wait_ge(taps_landed, g * 16 + 16)
                dve.wait_ge(x_landed, g * (16 * CT) + 16 * CT)
                dve.wait_ge(pads, 1)
                for t in range(TAPS):
                    for i in range(CT):
                        w = taps[:, i * (TAPS + 1) + t:i * (TAPS + 1) + t + 1]
                        src = xpad[:, i, :, t:t + SEQ]
                        if t == 0:
                            ins = dve.tensor_scalar(conv[:, i], src, w, None, ALU.mult)
                        else:
                            dve.wait_ge(conv_step, g * (CT * TAPS) + ((t - 1) * CT + i + 1))
                            ins = dve.scalar_tensor_tensor(conv[:, i], src, w, conv[:, i], ALU.mult, ALU.add)
                        ins.then_inc(conv_step, 1)
                for way in range(2):
                    for con, dst in ((CON_SEL, sel), (CON_NSEL, neg_sel)):
                        src = m.con[:, con + 32 * way:con + 32 * way + 32][:, bass.ds(col, GH)]
                        dve.tensor_scalar(dst[:, way], bc(src, P), 1.0, None, ALU.mult).then_inc(sel_ready, 1)
                for n, (q, way, k) in enumerate(order):
                    dve.wait_ge(st_done, g * NS + n + 1)
                    if k == 0:
                        dve.tensor_copy(states[:, n], m.ps[:, 6 + n % 2]).then_inc(st_ready, 1)
                    else:
                        c = gives(q, way, k)
                        s3 = states[:, n].rearrange("p (h w) -> p h w", h=GH)
                        before = states[:, n - 1].rearrange("p (h w) -> p h w", h=GH)
                        dve.wait_ge(st_ready, g * NS + n)
                        dve.tensor_tensor(s3, before, bc(grp4[:, DEC, c, way], 64), ALU.mult).then_inc(decayed, 1)
                        dve.wait_ge(decayed, g * 8 + (n - n // 3))
                        dve.tensor_tensor(states[:, n], states[:, n], m.ps[:, 6 + n % 2],
                                          ALU.add).then_inc(st_ready, 1)

                def finish_chunk(c):
                    s = c % 2
                    dve.wait_ge(skipped, g * TT + c + 1)
                    dve.wait_ge(y_done, g * STEPS + 2 * c + 2)
                    dve.tensor_tensor(y[:, s], y[:, s], m.ps[:, 6], ALU.add).then_inc(y_read, 1)
                    for n, (way, _) in enumerate(offs[c]):
                        at = off_before[c] + n
                        dve.wait_ge(off_done, g * NS + at + 1)
                        if at >= 1:
                            dve.wait_ge(off_added, g * NS + at)
                        dve.tensor_tensor(off[:, at % 2].rearrange("p (h w) -> p h w", h=GH),
                                          m.ps[:, 1 + way].rearrange("p (h w) -> p h w", h=GH),
                                          bc(grp4[:, EXPA, c, way], 64), ALU.mult).then_inc(off_read, 1)
                        dve.wait_ge(off_read, g * NS + at + 1)
                        dve.wait_ge(y_read, g * TT + c + 1)
                        dve.tensor_tensor(y[:, s], y[:, s], off[:, at % 2], ALU.add).then_inc(off_added, 1)

                def gate_chunk(c):
                    if c == 0:
                        dve.wait_ge(z_landed, g * 16 + 16)
                    dve.wait_ge(y_turned, g * TT + c + 1)
                    dst = zy[:, :, c * P:(c + 1) * P]
                    dve.tensor_tensor(dst, dst, m.ps[:, 3].rearrange("p (a b) -> p a b", a=XT),
                                      ALU.mult).then_inc(yz_ready, 1)

                for k in range(STEPS + 7):
                    if k < STEPS:
                        c, h = divmod(k, 2)
                        if h == 0:
                            dve.wait_ge(cb_done, g * TT + c + 1)
                            for way, tri in ((0, CON_UP), (1, CON_LOW)):
                                dve.tensor_tensor(cb[:, c % 2, way], m.ps[:, 0, 0:P], m.con[:, tri:tri + P],
                                                  ALU.mult).then_inc(cb_ready, 1)
                        dve.wait_ge(b_done, g * STEPS + k + 1)
                        dve.wait_ge(f_copied, g * STEPS + k + 1)
                        dve.tensor_tensor(fs[:, k % 2], fs[:, k % 2], m.ps[:, 5], ALU.min).then_inc(min_done, 1)
                    if 1 <= k <= STEPS:
                        j = k - 1
                        dve.wait_ge(masked, g * (2 * STEPS) + 2 * j + 2)
                        dve.tensor_tensor(tu[:, j % 2], tu[:, j % 2], tl[:, j % 2], ALU.add).then_inc(t_sum, 1)
                        dve.wait_ge(e_ready, g * STEPS + j + 1)
                        dve.wait_ge(t_sum, g * STEPS + j + 1)
                        dve.tensor_tensor(tu[:, j % 2], tu[:, j % 2], e[:, j % 2], ALU.mult).then_inc(m_ready, 1)
                    if k >= 4 and k % 2 == 0 and (k - 4) // 2 < TT:
                        finish_chunk((k - 4) // 2)
                    if k >= 6 and k % 2 == 0 and (k - 6) // 2 < TT:
                        gate_chunk((k - 6) // 2)

        @block.scalar
        def _(act):
            with act.Fori(0, GROUPS) as g:
                for i in range(CT):
                    act.wait_ge(conv_step, g * (CT * TAPS) + (CT * (TAPS - 1) + i + 1))
                    act.activation(flat_conv(i), flat_conv(i), ACT.Silu,
                                   bias=taps[:, i * (TAPS + 1) + TAPS:(i + 1) * (TAPS + 1)]).then_inc(conv_done, 1)
                for n in range(TT + 2):
                    act.wait_ge(turned, g * (TT + 2) + n + 1)
                    dst = b_tm[:, 4 * n:4 * n + 4].rearrange("p a b -> p (a b)") if n < 2 else xs[:, n - 2]
                    act.activation(dst, m.ps[:, n % 4], ACT.Copy).then_inc(tm_ready, 1)
                for k in range(STEPS + 1):
                    if k < STEPS:
                        act.wait_ge(f_done, g * STEPS + k + 1)
                        if k >= 2:
                            act.wait_ge(e_ready, g * STEPS + k - 1)
                        act.activation(fs[:, k % 2], m.ps[:, 4], ACT.Copy).then_inc(f_copied, 1)
                    if k >= 1:
                        j = k - 1
                        act.wait_ge(min_done, g * STEPS + j + 1)
                        if j >= 2:
                            act.wait_ge(m_ready, g * STEPS + j - 1)
                        act.activation(e[:, j % 2], fs[:, j % 2], ACT.Exp).then_inc(e_ready, 1)

        @block.gpsimd
        def _(pool):
            pool.memset(xpad[:], 0.0).then_inc(pads, 1)
            with pool.Fori(0, GROUPS) as g:
                pool.wait_ge(grp_ready, g * 2 + 2)
                for n, (q, way, k) in enumerate(order):
                    c = gives(q, way, k)
                    pool.wait_ge(tm_ready, g * (TT + 2) + c + 3)
                    if n >= 2:
                        pool.wait_ge(st_done, g * NS + n - 1)
                    x3 = xs[:, c].rearrange("p (h w) -> p h w", h=GH)
                    pool.tensor_tensor(xw[:, n % 2].rearrange("p (h w) -> p h w", h=GH), x3,
                                       bc(grp4[:, WIN, c, way], 64), ALU.mult).then_inc(xw_ready, 1)
                for k in range(STEPS):
                    c, h = divmod(k, 2)
                    if h == 0:
                        if c >= 2:
                            pool.wait_ge(y_turned, g * TT + c - 1)
                        x3 = xs[:, c].rearrange("p (h w) -> p h w", h=GH)
                        pool.tensor_tensor(y[:, c % 2].rearrange("p (h w) -> p h w", h=GH), x3, bc(skip[:], 64),
                                           ALU.mult).then_inc(skipped, 1)
                        pool.wait_ge(cb_ready, g * (2 * TT) + 2 * c + 2)
                    if k >= 2:
                        pool.wait_ge(y_done, g * STEPS + k - 1)
                    for way, dst in ((1, tl), (0, tu)):
                        one = cb[:, c % 2, way].unsqueeze(1).to_broadcast([P, 4, P])
                        pool.tensor_tensor(dst[:, k % 2].rearrange("p (a b) -> p a b", a=4), one,
                                           bc(grp4[:, DT, c, way, 4 * h:4 * h + 4], P),
                                           ALU.mult).then_inc(masked, 1)

        @block.tensor
        def _(pe):
            ident = m.con[:, CON_ID:CON_ID + P]
            with pe.Fori(0, GROUPS) as g:
                pe.wait_ge(conv_done, g * CT + CT)
                for n in range(TT + 2):
                    if n >= 4:
                        pe.wait_ge(tm_ready, g * (TT + 2) + n - 3)
                    for i in range(4):
                        src = bm_t[:, (4 * n + i) * P:(4 * n + i + 1) * P] if n < 2 else \
                            flat_conv(i)[:, (n - 2) * P:(n - 1) * P]
                        mm = pe.transpose(m.ps[:, n % 4, i * P:(i + 1) * P], src, ident)
                    mm.then_inc(turned, 1)
                for n, (q, way, k) in enumerate(order):
                    pe.wait_ge(xw_ready, g * NS + n + 1)
                    if n >= 2:
                        pe.wait_ge(st_ready, g * NS + n - 1)
                    pe.matmul(m.ps[:, 6 + n % 2], b_tm[:, gives(q, way, k)], xw[:, n % 2], start=True,
                              stop=True).then_inc(st_done, 1)
                pe.wait_ge(sel_ready, g * 4 + 4)
                pe.wait_ge(st_ready, g * NS + NS)
                pe.wait_ge(tm_ready, g * (TT + 2) + TT + 2)
                for k in range(STEPS + 7):
                    if k < STEPS:
                        c, h = divmod(k, 2)
                        chunk = slice(c * P, (c + 1) * P)
                        if h == 0:
                            if c >= 1:
                                pe.wait_ge(cb_ready, g * (2 * TT) + 2 * c)
                            pe.matmul(m.ps[:, 0, 0:P], bm_t[:, chunk], cm_t[:, chunk], start=True,
                                      stop=True).then_inc(cb_done, 1)
                        for way, bank, done, read in ((0, 4, f_done, f_copied), (1, 5, b_done, min_done)):
                            if k >= 1:
                                pe.wait_ge(read, g * STEPS + k)
                            pe.matmul(m.ps[:, bank], hl[:, chunk], neg_sel[:, way, 4 * h:4 * h + 4],
                                      start=True, stop=True)
                            for i in range(4):
                                mm = pe.matmul(m.ps[:, bank, i * P:(i + 1) * P], sel[:, way, 4 * h + i],
                                               hl[:, chunk], start=False, stop=True, skip_group_check=True)
                            mm.then_inc(done, 1)
                    if 2 <= k < STEPS + 2:
                        j = k - 2
                        c, h = divmod(j, 2)
                        chunk = slice(c * P, (c + 1) * P)
                        pe.wait_ge(m_ready, g * STEPS + j + 1)
                        if h == 0:
                            if c >= 1:
                                pe.wait_ge(y_read, g * TT + c)
                            for n, (way, state) in enumerate(offs[c]):
                                if off_before[c] + n >= 1:
                                    pe.wait_ge(off_read, g * NS + off_before[c])
                                pe.matmul(m.ps[:, 1 + way], cm_t[:, chunk], states[:, state], start=True,
                                          stop=True).then_inc(off_done, 1)
                        for i in range(4):
                            hh = 4 * h + i
                            mm = pe.matmul(m.ps[:, 6, hh * 64:(hh + 1) * 64], tu[:, j % 2, i * P:(i + 1) * P],
                                           xs[:, c, hh * 64:(hh + 1) * 64], start=True, stop=True)
                        mm.then_inc(y_done, 1)
                    if k >= 5 and k % 2 == 1 and (k - 5) // 2 < TT:
                        c = (k - 5) // 2
                        last_off = off_before[c] + len(offs[c])
                        pe.wait_ge(off_added, g * NS + last_off)
                        if c >= 1:
                            pe.wait_ge(yz_ready, g * TT + c)
                        for i in range(4):
                            mm = pe.transpose(m.ps[:, 3, i * P:(i + 1) * P], y[:, c % 2, i * P:(i + 1) * P], ident)
                        mm.then_inc(y_turned, 1)



def attention_stage(m):
    nc, d = m.nc, m.dram
    spans = [(max(b - 1, 0), min(b + 1, BLOCKS - 1) - max(b - 1, 0) + 1, P if b == 0 else 0) for b in range(BLOCKS)]
    slopes = [2.0 ** (-8.0 * (h + 1) / HEADS) for h in range(HEADS)]
    turns = [HEADS * n // 4 for _, n, _ in spans]
    turns_before = [sum(turns[:b]) for b in range(BLOCKS)]
    NTURN = sum(turns)
    rep = HEADS // KVH
    with ExitStack() as ctx:
        sem = lambda n: m.semaphore(f"att_{n}")
        sb = lambda n, s, t=F32: ctx.enter_context(nc.sbuf_tensor(n, s, t))
        qs = sb("qs", [P, HEADS // 2, SEQ])
        kd = sb("kd", [P, KVH, SEQ])
        vt = sb("vt", [P, 2, SEQ])
        v = sb("v", [P, BLOCKS, KVH * HD])
        s_sb = sb("s_sb", [P, 2, HEADS, 3 * P])
        pt = sb("pt", [P, HEADS * 3, P])
        o = sb("o", [P, 2, BANK])
        ot = sb("ot_sb", [P, KT, SEQ])
        st = sb("att_st", [P, 2, 6, HEADS])
        landed, s_done, s_read = sem("landed"), sem("s_done"), sem("s_read")
        stat, m_ready, p_ready, sink_e, den = sem("stat"), sem("m_ready"), sem("p_ready"), sem("sink_e"), sem("den")
        v_turned, v_ready, p_turned, pt_ready = sem("v_turned"), sem("v_ready"), sem("p_turned"), sem("pt_ready")
        o_done, o_ready, o_turned, ot_ready, stored = sem("o_done"), sem("o_ready"), sem("o_turned"), sem("ot_ready"), sem("stored")
        block = ctx.enter_context(nc.Block())
        MAX, NMAX, SINK, ESINK, SUM, RSUM = range(6)
        sink = m.rows[:, R_SINK:R_SINK + HEADS]

        @block.sync
        def _(sp):
            for s in range(NSEQ):
                col = s * SEQ
                rows = lambda tile, n: d["proj"][tile * P:(tile + n) * P, col:col + SEQ]
                if s:
                    sp.wait_ge(stored, s * 16)
                sp.dma_start(qs[:], rows(Q0, 8).rearrange("(a p) t -> p a t", p=P)).then_inc(landed, 16)
                for half in range(2):
                    sp.dma_start(kd[half * 64:(half + 1) * 64], rows(K0, 2).rearrange("(a p) t -> p a t", p=HD)).then_inc(landed, 16)
                sp.dma_start(vt[:], rows(V0, 2).rearrange("(a p) t -> p a t", p=P)).then_inc(landed, 16)
                sp.wait_ge(ot_ready, s * (2 * BLOCKS) + 2 * BLOCKS)
                sp.dma_start(d["ot"].rearrange("(a p) t -> p a t", p=P)[:, :, col:col + SEQ], ot[:]).then_inc(stored, 16)
            sp.wait_ge(stored, NSEQ * 16)

        @block.tensor
        def _(pe):
            ident = m.con[:, CON_ID:CON_ID + P]
            with pe.Fori(0, NSEQ) as s:
                blk = lambda b: s * BLOCKS + b
                pe.wait_ge(landed, s * 64 + 64)
                for n in range(2):
                    for i in range(4):
                        kb, ft = divmod(4 * n + i, 2)
                        mm = pe.transpose(m.ps[:, 6 + n, i * P:(i + 1) * P], vt[:, ft, kb * P:(kb + 1) * P], ident)
                    mm.then_inc(v_turned, 1)

                def scores(b):
                    k0, nk, _ = spans[b]
                    for h in range(HEADS):
                        if b or h >= 4:
                            pe.wait_ge(s_read, s * (BLOCKS * HEADS) + (b * HEADS + h - 3))
                        half = slice((h % 2) * 64, (h % 2) * 64 + 64)
                        pe.matmul(m.ps[:, h % 4, 0:nk * P], qs[half, h // 2, b * P:(b + 1) * P],
                                  kd[half, h // rep, k0 * P:(k0 + nk) * P], start=True, stop=True).then_inc(s_done, 1)

                scores(0)
                for b in range(BLOCKS):
                    k0, nk, _ = spans[b]
                    if b + 1 < BLOCKS:
                        scores(b + 1)
                    for t in range(turns[b]):
                        last_head = (4 * t + 3) // nk
                        pe.wait_ge(p_ready, s * (BLOCKS * HEADS) + (b * HEADS + last_head + 1))
                        n = turns_before[b] + t
                        if n >= 2:
                            pe.wait_ge(pt_ready, s * NTURN + (n - 1))
                        for i in range(4):
                            h, kb = divmod(4 * t + i, nk)
                            mm = pe.transpose(m.ps[:, 4 + n % 2, i * P:(i + 1) * P],
                                              s_sb[:, b % 2, h, kb * P:(kb + 1) * P], ident)
                        mm.then_inc(p_turned, 1)
                    if b == 0:
                        pe.wait_ge(v_ready, s * 2 + 2)
                    else:
                        pe.wait_ge(ot_ready, s * (2 * BLOCKS) + 2 * b)
                    pe.wait_ge(pt_ready, s * NTURN + (turns_before[b] + turns[b]))
                    for h in range(HEADS):
                        g = h // rep
                        for kb in range(nk):
                            mm = pe.matmul(m.ps[:, 6 + h // 8, (h % 8) * 64:(h % 8 + 1) * 64], pt[:, h * nk + kb],
                                           v[:, k0 + kb, g * HD:(g + 1) * HD], start=kb == 0, stop=kb == nk - 1)
                        if h % 8 == 7:
                            mm.then_inc(o_done, 1)
                    for n in range(2):
                        pe.wait_ge(o_ready, s * (2 * BLOCKS) + (2 * b + n + 1))
                        for i in range(4):
                            mm = pe.transpose(m.ps[:, 6 + n, i * P:(i + 1) * P], o[:, n, i * P:(i + 1) * P], ident)
                        mm.then_inc(o_turned, 1)

        @block.vector
        def _(dve):
            with dve.Fori(0, NSEQ) as s:
                def read_scores(b):
                    _, nk, c0 = spans[b]
                    if b >= 2:
                        dve.wait_ge(p_turned, s * NTURN + turns_before[b - 1])
                    for h in range(HEADS):
                        dve.wait_ge(s_done, s * (BLOCKS * HEADS) + (b * HEADS + h + 1))
                        dve.scalar_tensor_tensor(s_sb[:, b % 2, h, 0:nk * P],
                                                 m.con[:, CON_DIST + c0:CON_DIST + c0 + nk * P], -slopes[h],
                                                 m.ps[:, h % 4, 0:nk * P], ALU.mult, ALU.add).then_inc(s_read, 1)
                    t = st[:, b % 2]
                    dve.wait_ge(s_read, s * (BLOCKS * HEADS) + (b + 1) * HEADS)
                    dve.tensor_reduce(t[:, MAX], s_sb[:, b % 2, :, 0:nk * P], AX.X, ALU.max).then_inc(stat, 1)
                    dve.wait_ge(stat, s * (2 * BLOCKS) + (2 * b + 1))
                    dve.tensor_tensor(t[:, MAX], t[:, MAX], sink, ALU.max).then_inc(stat, 1)
                    dve.wait_ge(stat, s * (2 * BLOCKS) + (2 * b + 2))
                    dve.tensor_scalar(t[:, NMAX], t[:, MAX], -1.0, None, ALU.mult).then_inc(m_ready, 1)
                    dve.tensor_tensor(t[:, SINK], sink, t[:, MAX], ALU.subtract).then_inc(m_ready, 1)

                read_scores(0)
                for n in range(2):
                    dve.wait_ge(v_turned, s * 2 + n + 1)
                    dve.tensor_copy(v[:, 2 * n:2 * n + 2].rearrange("p a b -> p (a b)"), m.ps[:, 6 + n]).then_inc(v_ready, 1)
                for b in range(BLOCKS):
                    if b + 1 < BLOCKS:
                        read_scores(b + 1)
                    t = st[:, b % 2]
                    dve.wait_ge(sink_e, s * BLOCKS + b + 1)
                    dve.wait_ge(p_ready, s * (BLOCKS * HEADS) + (b + 1) * HEADS)
                    dve.tensor_tensor(t[:, SUM], t[:, SUM], t[:, ESINK], ALU.add).then_inc(den, 1)
                    dve.wait_ge(den, s * (2 * BLOCKS) + (2 * b + 1))
                    dve.reciprocal(t[:, RSUM], t[:, SUM]).then_inc(den, 1)
                    dve.wait_ge(den, s * (2 * BLOCKS) + (2 * b + 2))
                    for n in range(2):
                        dve.wait_ge(o_done, s * (2 * BLOCKS) + (2 * b + n + 1))
                        dve.tensor_tensor(o[:, n].rearrange("p (h w) -> p h w", h=8),
                                          m.ps[:, 6 + n].rearrange("p (h w) -> p h w", h=8),
                                          bc(t[:, RSUM, n * 8:(n + 1) * 8], HD), ALU.mult).then_inc(o_ready, 1)

        @block.scalar
        def _(act):
            with act.Fori(0, NSEQ) as s:
                def exponent(b, h):
                    _, nk, _ = spans[b]
                    t = st[:, b % 2]
                    if h == 0:
                        act.wait_ge(m_ready, s * (2 * BLOCKS) + (2 * b + 2))
                        act.activation(t[:, ESINK], t[:, SINK], ACT.Exp).then_inc(sink_e, 1)
                    p = s_sb[:, b % 2, h, 0:nk * P]
                    act.activation(p, p, ACT.Exp, bias=t[:, NMAX, h:h + 1],
                                   accum_out=t[:, SUM, h:h + 1]).then_inc(p_ready, 1)

                for h in range(HEADS):
                    exponent(0, h)
                for b in range(BLOCKS):
                    for i in range(max(HEADS, turns[b])):
                        if i < turns[b]:
                            n = turns_before[b] + i
                            act.wait_ge(p_turned, s * NTURN + n + 1)
                            if b and i == 0:
                                act.wait_ge(o_done, s * (2 * BLOCKS) + 2 * b)
                            act.activation(pt[:, 4 * i:4 * i + 4].rearrange("p a b -> p (a b)"),
                                           m.ps[:, 4 + n % 2], ACT.Copy).then_inc(pt_ready, 1)
                        if b + 1 < BLOCKS and i < HEADS:
                            exponent(b + 1, i)
                    for n in range(2):
                        act.wait_ge(o_turned, s * (2 * BLOCKS) + (2 * b + n + 1))
                        act.activation(ot[:, 4 * n:4 * n + 4, b * P:(b + 1) * P],
                                       m.ps[:, 6 + n].rearrange("p (a b) -> p a b", a=4), ACT.Copy).then_inc(ot_ready, 1)


def ssm_out_stage(m):
    nc, d = m.nc, m.dram
    NK = 2 * KT
    with ExitStack() as ctx:
        sem = lambda n: m.semaphore(f"wb_{n}")
        sb = lambda n, s, t=F32: ctx.enter_context(nc.sbuf_tensor(n, s, t))
        hi, lo = sb("y_hi", [P, NK, TOK], F32R), sb("y_lo", [P, NK, TOK], F32R)
        stage = sb("y_stage", [P, 2, TOK])
        rms = sb("y_rms", [P, TOK])
        landed = [sem(f"landed{r}") for r in range(2)]
        gate_landed = [sem(f"gate_landed{r}") for r in range(2)]
        hi_done, lo_done, sq_done, sq_used, mean, root, rms_ready = (sem(n) for n in (
            "hi_done", "lo_done", "sq_done", "sq_used", "mean", "root", "rms_ready"))
        scaled, gated = sem("scaled"), sem("gated")
        block = ctx.enter_context(nc.Block())
        units = Units(m, U_WB)
        both = lambda r: m.ps[:, 2 * r:2 * r + 2].rearrange("p a b -> p (a b)")

        @block.sync
        def _(sp):
            for k in range(NK):
                r = k % 2
                if k >= 2:
                    sp.wait_ge(lo_done, k - 1)
                    sp.wait_ge(sq_done, k - 1)
                sp.dma_start(stage[:, r], d["yt"][k * P:(k + 1) * P, :]).then_inc(landed[r], 16)
            sp.wait_ge(lo_done, NK)
            sp.wait_ge(sq_done, NK)
            for r in range(2):
                sp.dma_start(stage[:, r], d["proj"][(GATE0 + 8 + r) * P:(GATE0 + 9 + r) * P, :]).then_inc(gate_landed[r], 16)
            w = d["w_all"]

            def next_units(i, r):
                for s in range(2):
                    row = sp.snap(i * (4 * P) + (U_WB + 2 + 2 * r + s) * P)
                    sp.wait_ge(m.w_lo_ready, i * 4 + (U_WB + 1 + 2 * r + s))
                    load_unit(sp, m, s, w[bass.ds(row, P), :])
            with sp.Fori(0, KT // 2 - 1) as i:
                for r in range(2):
                    next_units(i, r)
                    row = sp.snap(i * (2 * P) + (GATE0 + 8 + 2 + r) * P)
                    sp.wait_ge(gated, i * 2 + r + 1)
                    sp.dma_start(stage[:, r], d["proj"][bass.ds(row, P), :]).then_inc(gate_landed[r], 16)
            with sp.Fori(KT // 2 - 1, KT // 2) as i:
                for r in range(2):
                    next_units(i, r)

        @block.scalar
        def _(act):
            for k in range(NK):
                r = k % 2
                act.wait_ge(landed[r], 16 * (k // 2 + 1))
                act.activation(hi[:, k], stage[:, r], ACT.Copy, scale=m.gains[:, G_SSM + k:G_SSM + k + 1]).then_inc(hi_done, 1)
                if k >= 2:
                    act.wait_ge(sq_used, k - 1)
                act.activation(m.resid[:, r], stage[:, r], ACT.Square).then_inc(sq_done, 1)
            units.hi(act, 0, 0, first=True)
            units.hi(act, 1, 1, first=True)
            act.wait_ge(mean, 1)
            act.activation(rms[:], rms[:], ACT.Sqrt).then_inc(root, 1)
            with act.Fori(1, KT) as i:
                for r in range(2):
                    units.hi(act, i * 2 + r, r)

        @block.vector
        def _(dve):
            for k in range(NK):
                dve.wait_ge(hi_done, k + 1)
                dve.scalar_tensor_tensor(lo[:, k], stage[:, k % 2], m.gains[:, G_SSM + k:G_SSM + k + 1],
                                         hi[:, k].bitcast(F32), ALU.mult, ALU.subtract).then_inc(lo_done, 1)
            units.lo(dve, 0, 0)
            units.lo(dve, 1, 1)
            dve.wait_ge(sq_used, NK)
            dve.tensor_scalar(rms[:], m.ps[:, 4:6].rearrange("p a b -> p (a b)"), 1.0 / (2 * D), EPS,
                              ALU.mult, ALU.add).then_inc(mean, 1)
            dve.wait_ge(root, 1)
            dve.reciprocal(rms[:], rms[:]).then_inc(rms_ready, 1)
            dve.wait_ge(rms_ready, 1)

            def finish(at, r):
                dst = m.resid[:, at] if isinstance(at, int) else m.resid[:, bass.ds(dve.snap(at), 1)].squeeze(1)
                dve.wait_ge(m.w_used, at * 2 + (U_WB + 2))
                dve.tensor_tensor(dst, both(r), rms[:], ALU.mult).then_inc(scaled, 1)
                dve.wait_ge(gate_landed[r], (at - r) * 8 + 16)
                dve.wait_ge(scaled, at + 1)
                dve.tensor_tensor(dst, dst, stage[:, r], ALU.mult).then_inc(gated, 1)

            with dve.Fori(0, KT // 2 - 1) as i:
                for r in range(2):
                    units.lo(dve, i * 4 + 2 * r + 2, 0)
                    units.lo(dve, i * 4 + 2 * r + 3, 1)
                    finish(i * 2 + r, r)
            units.lo(dve, 2 * KT - 2, 0)
            units.lo(dve, 2 * KT - 1, 1)
            finish(KT - 2, 0)
            finish(KT - 1, 1)

        @block.tensor
        def _(pe):
            for k in range(NK):
                pe.wait_ge(sq_done, k + 1)
                for n in range(2):
                    mm = pe.matmul(m.ps[:, 4 + n], m.con[:, CON_ONES:CON_ONES + P],
                                   m.resid[:, k % 2, n * BANK:(n + 1) * BANK], start=k == 0, stop=k == NK - 1)
                mm.then_inc(sq_used, 1)
            pe.wait_ge(lo_done, NK)

            def tile(at, r, peel):
                for s in range(2):
                    units.wait(pe, at * 2 + s)
                    if s == 0 and not peel:
                        pe.wait_ge(scaled, at - 1)
                    for n in range(2):
                        c = slice(n * BANK, (n + 1) * BANK)
                        mm = products(pe, m.ps[:, 2 * r + n],
                                      [(wslice(m, s, k * P, (k + 1) * P), (hi[:, s * KT + k, c], lo[:, s * KT + k, c]))
                                       for k in range(KT)], first_of_group=s == 0, last_of_group=s == 1)
                    mm.then_inc(m.w_used, 1)
            for r in range(2):
                tile(r, r, True)
            with pe.Fori(1, KT // 2) as i:
                for r in range(2):
                    tile(i * 2 + r, r, False)


def attention_out_stage(m, m_hi, m_lo):
    nc, d = m.nc, m.dram
    with ExitStack() as ctx:
        sem = lambda n: m.semaphore(f"wa_{n}")
        sb = lambda n, s, t=F32: ctx.enter_context(nc.sbuf_tensor(n, s, t))
        hi, lo = sb("o_hi", [P, KT, TOK], F32R), sb("o_lo", [P, KT, TOK], F32R)
        stage = sb("o_stage", [P, 2, TOK])
        landed = [sem(f"landed{r}") for r in range(2)]
        gate_landed = [sem(f"gate_landed{r}") for r in range(2)]
        hi_done, lo_done, gated, summed, m_hi_done, merged = (sem(n) for n in (
            "hi_done", "lo_done", "gated", "summed", "m_hi_done", "merged"))
        block = ctx.enter_context(nc.Block())
        units = Units(m, U_WA)
        both = lambda r: m.ps[:, 2 * r:2 * r + 2].rearrange("p a b -> p (a b)")

        @block.sync
        def _(sp):
            for k in range(KT):
                r = k % 2
                if k >= 2:
                    sp.wait_ge(lo_done, k - 1)
                sp.dma_start(stage[:, r], d["ot"][k * P:(k + 1) * P, :]).then_inc(landed[r], 16)
            sp.wait_ge(lo_done, KT)
            for r in range(2):
                sp.dma_start(stage[:, r], d["proj"][(GATE0 + r) * P:(GATE0 + r + 1) * P, :]).then_inc(gate_landed[r], 16)
            w = d["w_all"]
            with sp.Fori(0, KT // 2 - 1) as i:
                for r in range(2):
                    row = sp.snap(i * (2 * P) + (U_WA + 2 + r) * P)
                    g_row = sp.snap(i * (2 * P) + (GATE0 + 2 + r) * P)
                    sp.wait_ge(m.w_lo_ready, i * 2 + (U_WA + 1 + r))
                    load_unit(sp, m, r, w[bass.ds(row, P), :])
                    sp.wait_ge(merged, i * 2 + r + 1)
                    sp.dma_start(stage[:, r], d["proj"][bass.ds(g_row, P), :]).then_inc(gate_landed[r], 16)
            for r in range(2):
                sp.wait_ge(m.w_lo_ready, U_WA + KT - 1 + r)
                load_unit(sp, m, r, w[(U_WA + KT + r) * P:(U_WA + KT + r + 1) * P, :])

        @block.scalar
        def _(act):
            for k in range(KT):
                act.wait_ge(landed[k % 2], 16 * (k // 2 + 1))
                act.activation(hi[:, k], stage[:, k % 2], ACT.Copy).then_inc(hi_done, 1)
            for r in range(2):
                units.hi(act, r, r, first=True)
            with act.Fori(1, KT // 2) as i:
                for r in range(2):
                    units.hi(act, i * 2 + r, r)

        @block.vector
        def _(dve):
            for k in range(KT):
                dve.wait_ge(hi_done, k + 1)
                dve.tensor_tensor(lo[:, k], stage[:, k % 2], hi[:, k].bitcast(F32), ALU.subtract).then_inc(lo_done, 1)
            units.lo(dve, 0, 0)

            def finish(at, r):
                one = (lambda t: t[:, at]) if isinstance(at, int) else (lambda t, j=dve.snap(at): t[:, bass.ds(j, 1)].squeeze(1))
                dve.wait_ge(m.w_used, at + (U_WA + 1))
                dve.wait_ge(gate_landed[r], (at - r) * 8 + 16)
                dve.tensor_tensor(stage[:, r], both(r), stage[:, r], ALU.mult).then_inc(gated, 1)
                dve.wait_ge(gated, at + 1)
                dve.tensor_tensor(one(m.resid), one(m.resid), stage[:, r], ALU.add).then_inc(summed, 1)
                dve.wait_ge(summed, at + 1)
                dve.tensor_scalar(one(m_hi), one(m.resid), 1.0, None, ALU.mult).then_inc(m_hi_done, 1)
                dve.wait_ge(m_hi_done, at + 1)
                dve.tensor_tensor(one(m_lo), one(m.resid), one(m_hi).bitcast(F32), ALU.subtract).then_inc(merged, 1)

            with dve.Fori(0, KT // 2 - 1) as i:
                units.lo(dve, i * 2 + 1, 1)
                finish(i * 2, 0)
                units.lo(dve, i * 2 + 2, 0)
                finish(i * 2 + 1, 1)
            units.lo(dve, KT - 1, 1)
            finish(KT - 2, 0)
            finish(KT - 1, 1)

        @block.tensor
        def _(pe):
            pe.wait_ge(lo_done, KT)

            def tile(at, r, peel):
                units.wait(pe, at)
                if not peel:
                    pe.wait_ge(gated, at - 1)
                for n in range(2):
                    c = slice(n * BANK, (n + 1) * BANK)
                    mm = products(pe, m.ps[:, 2 * r + n],
                                  [(wslice(m, r, k * P, (k + 1) * P), (hi[:, k, c], lo[:, k, c])) for k in range(KT)])
                mm.then_inc(m.w_used, 1)
            for r in range(2):
                tile(r, r, True)
            with pe.Fori(1, KT // 2) as i:
                for r in range(2):
                    tile(i * 2 + r, r, False)


def residual_stage(m, name, first, hi, lo, load_x):
    nc, d = m.nc, m.dram
    n_units = KT
    with ExitStack() as ctx:
        sem = lambda n: m.semaphore(f"{name}_{n}")
        part_done, added, x_landed = sem("part_done"), sem("added"), sem("x_landed")
        block = ctx.enter_context(nc.Block())
        units = Units(m, first)

        @block.sync
        def _(sp):
            if load_x:
                sp.dma_start(m.resid[:], d["x"].rearrange("(a p) c -> p a c", p=P)).then_inc(x_landed, 16)
            stream_weights(sp, m, first, n_units)

        @block.scalar
        def _(act):
            for r in range(2):
                units.hi(act, r, r, first=True)
            with act.Fori(1, n_units // 2) as i:
                for r in range(2):
                    units.hi(act, i * 2 + r, r)

        @block.vector
        def _(dve):
            units.lo(dve, 0, 0)
            if load_x:
                dve.wait_ge(x_landed, 16)

            def add(u):
                col = (u % 2) * BANK
                for g in range(4):
                    wait_part(dve, units, part_done, u, g)
                    dst = m.resid[:, 2 * g:2 * g + 2, col:col + BANK]
                    dve.tensor_tensor(dst, dst, m.ps[:, 2 * (g % 2):2 * (g % 2) + 2], ALU.add).then_inc(added, 1)
            for u in range(n_units):
                if u + 1 < n_units:
                    units.lo(dve, u + 1, (u + 1) % 2)
                add(u)

        @block.tensor
        def _(pe):
            for u in range(n_units):
                units.wait(pe, u)
                parts(pe, m, u % 2, part_done, hi, lo, 2 * (u // 2),
                      lambda g: pe.wait_ge(added, 4 * u + g - 1) if 4 * u + g >= 2 else None)


def wait_part(eng, units, part_done, u, g):
    if g < 3:
        eng.wait_ge(part_done, u * 3 + (g + 1))
    else:
        units.products_done(eng, u)


def parts(pe, m, r, part_done, hi, lo, kt, wait_bank):
    for g in range(4):
        wait_bank(g)
        for t in (2 * g, 2 * g + 1):
            s = slice(t * P, (t + 1) * P)
            mm = products(pe, m.ps[:, 2 * (g % 2) + t % 2],
                          [((hi[:, kt + i, s], lo[:, kt + i, s]), wslice(m, r, i * BANK, (i + 1) * BANK))
                           for i in range(2)])
        mm.then_inc(part_done if g < 3 else m.w_used, 1)


def memory_stage(m, mem_hi, mem_lo, k_t, v_c):
    nc, d = m.nc, m.dram
    with ExitStack() as ctx:
        sem = lambda n: m.semaphore(f"kv_{n}")
        k_read, v_read = sem("k_read"), sem("v_read")
        block = ctx.enter_context(nc.Block())
        units = Units(m, U_KV)

        @block.sync
        def _(sp):
            stream_weights(sp, m, U_KV, 16)

        @block.scalar
        def _(act):
            for r in range(2):
                units.hi(act, r, r, first=True)
            with act.Fori(1, KT) as i:
                for r in range(2):
                    units.hi(act, i * 2 + r, r)

        @block.vector
        def _(dve):
            units.lo(dve, 0, 0)
            with dve.Fori(0, KT // 2) as i:
                for r in range(2):
                    j = dve.snap(i * 2 + r)
                    units.lo(dve, i * 2 + (r + 1), 1 - r)
                    units.products_done(dve, i * 2 + r)
                    dve.tensor_scalar(k_t[:, bass.ds(j, 1)].squeeze(1), m.ps[:, r], 1.0, None, ALU.mult).then_inc(k_read, 1)
            for u in range(KT, 2 * KT):
                if u + 1 < 2 * KT:
                    units.lo(dve, u + 1, (u + 1) % 2)
                if u % 4 == 3:
                    n = (u - KT) // 4
                    units.products_done(dve, u)
                    for t in range(MT):
                        dve.tensor_copy(v_c[:, t, n * BANK:(n + 1) * BANK], m.ps[:, 4 + t]).then_inc(v_read, 1)

        @block.tensor
        def _(pe):
            def k_tile(at, r, peel):
                units.wait(pe, at)
                if not peel:
                    pe.wait_ge(k_read, at - 1)
                mm = products(pe, m.ps[:, r], [(wslice(m, r, k * P, (k + 1) * P), (mem_hi[:, k], mem_lo[:, k]))
                                               for k in range(KT)])
                mm.then_inc(m.w_used, 1)
            for r in range(2):
                k_tile(r, r, True)
            with pe.Fori(1, KT // 2) as i:
                for r in range(2):
                    k_tile(i * 2 + r, r, False)
            for u in range(KT, 2 * KT):
                n, kp = divmod(u - KT, 4)
                units.wait(pe, u)
                if u == KT + 4:
                    pe.wait_ge(v_read, MT)
                for t in range(MT):
                    s = slice(t * P, (t + 1) * P)
                    mm = products(pe, m.ps[:, 4 + t],
                                  [((mem_hi[:, 2 * kp + i, s], mem_lo[:, 2 * kp + i, s]),
                                    wslice(m, u % 2, i * BANK, (i + 1) * BANK)) for i in range(2)],
                                  first_of_group=kp == 0, last_of_group=kp == 3)
                mm.then_inc(m.w_used, 1)


def query_stage(m, u_hi, u_lo, q_t):
    nc, d = m.nc, m.dram
    with ExitStack() as ctx:
        drained = m.semaphore("q_drained")
        block = ctx.enter_context(nc.Block())
        units = Units(m, U_Q)

        @block.sync
        def _(sp):
            stream_weights(sp, m, U_Q, KT)

        @block.scalar
        def _(act):
            for r in range(2):
                units.hi(act, r, r, first=True)
            with act.Fori(1, KT // 2) as i:
                for r in range(2):
                    units.hi(act, i * 2 + r, r)

        @block.vector
        def _(dve):
            units.lo(dve, 0, 0)

            def finish(at, r):
                dst = q_t[:, at] if isinstance(at, int) else q_t[:, bass.ds(dve.snap(at), 1)].squeeze(1)
                units.products_done(dve, at)
                dve.tensor_scalar(dst, m.ps[:, 2 * r:2 * r + 2].rearrange("p a b -> p (a b)"), XHD ** -0.5, None,
                                  ALU.mult).then_inc(drained, 1)
            with dve.Fori(0, KT // 2 - 1) as i:
                units.lo(dve, i * 2 + 1, 1)
                finish(i * 2, 0)
                units.lo(dve, i * 2 + 2, 0)
                finish(i * 2 + 1, 1)
            units.lo(dve, KT - 1, 1)
            finish(KT - 2, 0)
            finish(KT - 1, 1)

        @block.tensor
        def _(pe):
            def tile(at, r, peel):
                units.wait(pe, at)
                if not peel:
                    pe.wait_ge(drained, at - 1)
                for n in range(2):
                    c = slice(n * BANK, (n + 1) * BANK)
                    mm = products(pe, m.ps[:, 2 * r + n],
                                  [(wslice(m, r, k * P, (k + 1) * P), (u_hi[:, k, c], u_lo[:, k, c])) for k in range(KT)])
                mm.then_inc(m.w_used, 1)
            for r in range(2):
                tile(r, r, True)
            with pe.Fori(1, KT // 2) as i:
                for r in range(2):
                    tile(i * 2 + r, r, False)


def cross_stage(m, q_t, k_t, v_c, o_hi, o_lo):
    nc = m.nc
    with ExitStack() as ctx:
        sem = lambda n: m.semaphore(f"cr_{n}")
        sb = lambda n, s, t=F32: ctx.enter_context(nc.sbuf_tensor(n, s, t))
        p = sb("cr_p", [P, 2, XH, MEM])
        pt = sb("cr_pt", [P, 2 * XH, P])
        st = sb("cr_st", [P, 2, 3, XH])
        s_done, neg_max, exp_done, inv, normed, p_turned, pt_ready, o_done, hi_done, lo_done = (sem(n) for n in (
            "s_done", "neg_max", "exp_done", "inv", "normed", "p_turned", "pt_ready", "o_done", "hi_done", "lo_done"))
        block = ctx.enter_context(nc.Block())
        scores = m.ps[:, 4:6].rearrange("p a (h k) -> p (a h) k", h=2)

        @block.tensor
        def _(pe):
            ident = m.con[:, CON_ID:CON_ID + P]

            def score(t):
                s = t // BLOCKS
                if t:
                    pe.wait_ge(exp_done, XH * t)
                for h in range(XH):
                    for i in range(2):
                        mm = pe.matmul(scores[:, h], q_t[:, 2 * h + i, t * P:(t + 1) * P],
                                       k_t[:, 2 * h + i, s * MEM:(s + 1) * MEM], start=i == 0, stop=i == 1)
                mm.then_inc(s_done, 1)
            score(0)
            for t in range(TT):
                s = t // BLOCKS
                if t + 1 < TT:
                    score(t + 1)
                for n in range(2):
                    pe.wait_ge(normed, XH * t + 2 * n + 2)
                    if t:
                        pe.wait_ge(pt_ready, 2 * (t - 1) + n + 1)
                    for i in range(4):
                        h, kb = divmod(4 * n + i, 2)
                        mm = pe.transpose(m.ps[:, 6 + n, i * P:(i + 1) * P], p[:, t % 2, h, kb * P:(kb + 1) * P], ident)
                    mm.then_inc(p_turned, 1)
                if t:
                    pe.wait_ge(lo_done, 2 * t)
                for n in range(2):
                    pe.wait_ge(pt_ready, 2 * t + n + 1)
                    for i in range(4):
                        f = 4 * n + i
                        h = f // 2
                        for kb in range(2):
                            mm = pe.matmul(m.ps[:, n, i * P:(i + 1) * P], v_c[:, 2 * s + kb, f * P:(f + 1) * P],
                                           pt[:, 2 * h + kb], start=kb == 0, stop=kb == 1)
                    mm.then_inc(o_done, 1)

        @block.vector
        def _(dve):
            def maxima(t):
                dve.wait_ge(s_done, t + 1)
                dve.tensor_reduce(st[:, t % 2, 0], scores, AX.X, ALU.max, negate=True).then_inc(neg_max, 1)

            maxima(0)
            for t in range(TT):
                if t + 1 < TT:
                    maxima(t + 1)
                dve.wait_ge(exp_done, XH * (t + 1))
                dve.reciprocal(st[:, t % 2, 2], st[:, t % 2, 1]).then_inc(inv, 1)
                dve.wait_ge(inv, t + 1)
                for h in range(XH):
                    dve.tensor_scalar(p[:, t % 2, h], p[:, t % 2, h], st[:, t % 2, 2, h:h + 1], None,
                                      ALU.mult).then_inc(normed, 1)
                for n in range(2):
                    dve.wait_ge(hi_done, 2 * t + n + 1)
                    dst = (slice(None), slice(4 * n, 4 * n + 4), slice(t * P, (t + 1) * P))
                    dve.tensor_tensor(o_lo[dst], m.ps[:, n].rearrange("p (a b) -> p a b", a=4),
                                      o_hi[dst].bitcast(F32), ALU.subtract).then_inc(lo_done, 1)

        @block.scalar
        def _(act):
            def exponents(t):
                act.wait_ge(neg_max, t + 1)
                if t >= 2:
                    act.wait_ge(p_turned, 2 * (t - 1))
                for h in range(XH):
                    act.activation(p[:, t % 2, h], scores[:, h], ACT.Exp, bias=st[:, t % 2, 0, h:h + 1],
                                   accum_out=st[:, t % 2, 1, h:h + 1]).then_inc(exp_done, 1)
            exponents(0)
            for t in range(TT):
                if t + 1 < TT:
                    exponents(t + 1)
                for n in range(2):
                    act.wait_ge(p_turned, 2 * t + n + 1)
                    if t:
                        act.wait_ge(o_done, 2 * t)
                    act.activation(pt[:, 4 * n:4 * n + 4].rearrange("p a b -> p (a b)"), m.ps[:, 6 + n],
                                   ACT.Copy).then_inc(pt_ready, 1)
                for n in range(2):
                    act.wait_ge(o_done, 2 * t + n + 1)
                    act.activation(o_hi[:, 4 * n:4 * n + 4, t * P:(t + 1) * P],
                                   m.ps[:, n].rearrange("p (a b) -> p a b", a=4), ACT.Copy).then_inc(hi_done, 1)


def ffn_stage(m, u_hi, u_lo):
    nc, d = m.nc, m.dram
    NC = HT // 2
    with ExitStack() as ctx:
        sem = lambda n: m.semaphore(f"ffn_{n}")
        sb = lambda n, s, t=F32: ctx.enter_context(nc.sbuf_tensor(n, s, t))
        g = sb("ffn_g", [P, 2, TOK])
        h_hi, h_lo = sb("h_hi", [P, 2, TOK], F32R), sb("h_lo", [P, 2, TOK], F32R)
        silu, prod, h_hi_done, h_ready, part_done, added = (sem(n) for n in (
            "silu", "prod", "h_hi_done", "h_ready", "part_done", "added"))
        block = ctx.enter_context(nc.Block())
        units = Units(m, U_FFN)
        both = lambda r: m.ps[:, 2 * r:2 * r + 2].rearrange("p a b -> p (a b)")
        at = lambda c, k: (c - 1) * 6 + (4 + k)

        @block.sync
        def _(sp):
            stream_weights(sp, m, U_FFN, 3 * HT)

        @block.scalar
        def _(act):
            def gate(u, c, r, first=False):
                if not first:
                    act.wait_ge(h_ready, c * 2 + (r - 1))
                units.products_done(act, u)
                act.activation(g[:, r], both(r), ACT.Silu).then_inc(silu, 1)

            def hidden(c, r):
                act.wait_ge(prod, c * 2 + (r + 1))
                act.activation(h_hi[:, r], g[:, r], ACT.Copy).then_inc(h_hi_done, 1)

            units.hi(act, 0, 0, first=True)
            units.hi(act, 1, 1, first=True)
            gate(0, 0, 0, True)
            units.hi(act, 2, 0)
            gate(1, 0, 1, True)
            units.hi(act, 3, 1)
            units.hi(act, 4, 0)
            hidden(0, 0)
            units.hi(act, 5, 1)
            hidden(0, 1)
            with act.Fori(1, NC) as c:
                gate(at(c, 0), c, 0)
                units.hi(act, at(c, 2), 0)
                gate(at(c, 1), c, 1)
                units.hi(act, at(c, 3), 1)
                units.hi(act, at(c, 4), 0)
                units.hi(act, at(c, 5), 1)
                units.hi(act, at(c, 6), 0)
                hidden(c, 0)
                units.hi(act, at(c, 7), 1)
                hidden(c, 1)

        @block.vector
        def _(dve):
            def up(u, c, r):
                dve.wait_ge(silu, c * 2 + (r + 1))
                units.products_done(dve, u)
                dve.tensor_tensor(g[:, r], both(r), g[:, r], ALU.mult).then_inc(prod, 1)

            def low(c, r):
                dve.wait_ge(h_hi_done, c * 2 + (r + 1))
                dve.tensor_tensor(h_lo[:, r], g[:, r], h_hi[:, r].bitcast(F32), ALU.subtract).then_inc(h_ready, 1)

            def down(u, d_at, n):
                for k in range(4):
                    if k < 3:
                        dve.wait_ge(part_done, d_at * 3 + (k + 1))
                    else:
                        units.products_done(dve, u)
                    dst = m.resid[:, 2 * k:2 * k + 2, n * BANK:(n + 1) * BANK]
                    dve.tensor_tensor(dst, dst, m.ps[:, 2 * (k % 2):2 * (k % 2) + 2], ALU.add).then_inc(added, 1)

            for u in range(4):
                units.lo(dve, u, u % 2)
            units.lo(dve, 4, 0)
            up(2, 0, 0)
            units.lo(dve, 5, 1)
            up(3, 0, 1)
            low(0, 0)
            low(0, 1)
            with dve.Fori(1, NC) as c:
                units.lo(dve, at(c, 2), 0)
                units.lo(dve, at(c, 3), 1)
                down(at(c, 2), c * 2 - 2, 0)
                units.lo(dve, at(c, 4), 0)
                down(at(c, 3), c * 2 - 1, 1)
                units.lo(dve, at(c, 5), 1)
                units.lo(dve, at(c, 6), 0)
                up(at(c, 4), c, 0)
                units.lo(dve, at(c, 7), 1)
                low(c, 0)
                up(at(c, 5), c, 1)
                low(c, 1)
            down(at(NC, 0), 2 * NC - 2, 0)
            down(at(NC, 1), 2 * NC - 1, 1)

        @block.tensor
        def _(pe):
            def tile(u, r):
                units.wait(pe, u)
                for n in range(2):
                    s = slice(n * BANK, (n + 1) * BANK)
                    mm = products(pe, m.ps[:, 2 * r + n],
                                  [(wslice(m, r, k * P, (k + 1) * P), (u_hi[:, k, s], u_lo[:, k, s])) for k in range(KT)])
                mm.then_inc(m.w_used, 1)

            def down(u, d_at, n, c):
                units.wait(pe, u)

                def bank_free(k):
                    if n == 0 and k < 2:
                        if k == 0:
                            pe.wait_ge(silu, c * 2 + 2)
                    else:
                        pe.wait_ge(added, d_at * 4 + (k - 1))
                parts(pe, m, n, part_done, h_hi, h_lo, 0, bank_free)

            tile(0, 0)
            tile(1, 1)
            pe.wait_ge(silu, 1)
            tile(2, 0)
            pe.wait_ge(silu, 2)
            tile(3, 1)
            with pe.Fori(1, NC) as c:
                pe.wait_ge(prod, c * 2 - 1)
                tile(at(c, 0), 0)
                pe.wait_ge(prod, c * 2)
                tile(at(c, 1), 1)
                pe.wait_ge(h_ready, c * 2)
                down(at(c, 2), c * 2 - 2, 0, c)
                down(at(c, 3), c * 2 - 1, 1, c)
                pe.wait_ge(added, c * 8 - 1)
                tile(at(c, 4), 0)
                pe.wait_ge(added, c * 8)
                tile(at(c, 5), 1)
            pe.wait_ge(h_ready, 2 * NC)
            pe.wait_ge(prod, 2 * NC)
            down(at(NC, 0), 2 * NC - 2, 0, NC - 1)
            down(at(NC, 1), 2 * NC - 1, 1, NC - 1)


def final_stage(m):
    nc, d = m.nc, m.dram
    with ExitStack() as ctx:
        sem = lambda n: m.semaphore(f"fin_{n}")
        sq = ctx.enter_context(nc.sbuf_tensor("fin_sq", [P, 2, D], F32))
        ss = ctx.enter_context(nc.sbuf_tensor("fin_ss", [P, 3, TT], F32))
        squared, mean, root, rstd, ready, stored = (sem(n) for n in ("squared", "mean", "root", "rstd", "ready", "stored"))
        block = ctx.enter_context(nc.Block())

        @block.scalar
        def _(act):
            for t in range(TT):
                if t >= 2:
                    act.wait_ge(squared, t - 1)
                act.activation(sq[:, t % 2], m.resid[:, t], ACT.Square, accum_out=ss[:, 0, t:t + 1]).then_inc(squared, 1)
            act.wait_ge(mean, 1)
            act.activation(ss[:, 2], ss[:, 1], ACT.Sqrt).then_inc(root, 1)

        @block.vector
        def _(dve):
            dve.wait_ge(squared, TT)
            dve.tensor_scalar(ss[:, 1], ss[:, 0], 1.0 / D, EPS, ALU.mult, ALU.add).then_inc(mean, 1)
            dve.wait_ge(root, 1)
            dve.reciprocal(ss[:, 0], ss[:, 2]).then_inc(rstd, 1)
            dve.wait_ge(rstd, 1)
            for t in range(TT):
                dve.scalar_tensor_tensor(m.resid[:, t], m.resid[:, t], ss[:, 0, t:t + 1],
                                         m.rows[:, R_FINAL:R_FINAL + D], ALU.mult, ALU.mult).then_inc(ready, 1)

        @block.sync
        def _(sp):
            for t in range(TT):
                sp.wait_ge(ready, t + 1)
                sp.dma_start(d["y"][t * P:(t + 1) * P, :], m.resid[:, t]).then_inc(stored, 16)
            sp.wait_ge(stored, 16 * TT)


def build(nc, dram):
    with ExitStack() as top:
        m = open_core(nc, top, dram)
        sb = lambda ctx, n, s, t=F32: ctx.enter_context(nc.sbuf_tensor(n, s, t))
        prep_stage(m)
        with ExitStack() as mix:
            st4 = sb(mix, "st4", [P, 4, TT, 64])
            hl = sb(mix, "hl", [P, TOK], F32R)
            with ExitStack() as ctx:
                dt_raw = sb(ctx, "dt_raw", [P, TT, 64])
                a2 = sb(ctx, "a2", [P, TT, 2, 64])
                with ExitStack() as c2:
                    u_hi, u_lo = sb(c2, "u_hi", [P, KT, TOK], F32R), sb(c2, "u_lo", [P, KT, TOK], F32R)
                    norm_stage(m, "mix", dram["x"], G_MIX, u_hi, u_lo, TT, True)
                    projection_stage(m, u_hi, u_lo, dt_raw)
                step_stage(m, dt_raw, st4[:, 0], a2, st4[:, 1], st4[:, 2], st4[:, 3], hl)
            ssd_stage(m, st4, hl)
        attention_stage(m)
        m.resid = sb(top, "resid", [P, TT, D])
        ssm_out_stage(m)
        with ExitStack() as ctx:
            m_hi, m_lo = sb(ctx, "m_hi", [P, KT, TOK], F32R), sb(ctx, "m_lo", [P, KT, TOK], F32R)
            attention_out_stage(m, m_hi, m_lo)
            residual_stage(m, "out", U_OUT, m_hi, m_lo, True)
        m.recycle()
        with ExitStack() as ctx:
            k_t, v_c = sb(ctx, "k_t", [P, KT, NSEQ * MEM]), sb(ctx, "v_c", [P, MT, D])
            with ExitStack() as c2:
                mem_hi, mem_lo = (sb(c2, n, [P, KT, NSEQ * MEM], F32R) for n in ("mem_hi", "mem_lo"))
                norm_stage(m, "mem", dram["mem"], G_MEM, mem_hi, mem_lo, MT, True)
                memory_stage(m, mem_hi, mem_lo, k_t, v_c)
            c_hi, c_lo = sb(ctx, "c_hi", [P, KT, TOK], F32R), sb(ctx, "c_lo", [P, KT, TOK], F32R)
            norm_stage(m, "crs", m.resid, G_CROSS, c_hi, c_lo, TT, False)
            q_t = sb(ctx, "q_t", [P, KT, TOK])
            query_stage(m, c_hi, c_lo, q_t)
            cross_stage(m, q_t, k_t, v_c, c_hi, c_lo)
            residual_stage(m, "wo", U_O, c_hi, c_lo, False)
        with ExitStack() as ctx:
            f_hi, f_lo = sb(ctx, "f_hi", [P, KT, TOK], F32R), sb(ctx, "f_lo", [P, KT, TOK], F32R)
            norm_stage(m, "ffn", m.resid, G_FFN, f_hi, f_lo, TT, False)
            ffn_stage(m, f_hi, f_lo)
        final_stage(m)



def tiles_a(w):
    k, n = w.shape
    return w.reshape(KT, P, n // P, P).transpose(2, 1, 0, 3).reshape(-1, 1024)


def tiles_b(w):
    k, n = w.shape
    return w.reshape(k // (2 * P), 2, P, n // BANK, BANK).transpose(0, 3, 2, 1, 4).reshape(-1, 1024)


def lay_out(i):
    a = {k: np.asarray(v) for k, v in i.items()}
    w = a["w_in"][0]
    c = 1536
    z, xbc, dtw, gates = w[:, c:c + 2048], w[:, c + 2048:c + 5120], w[:, c + 5120:c + 5184], w[:, c + 5184:]
    chans = np.concatenate([np.r_[g * GW:(g + 1) * GW, 2048 + g * P:2048 + (g + 1) * P, 2560 + g * P:2560 + (g + 1) * P]
                            for g in range(GROUPS)])
    kv = a["w_kv_cross"][0]
    v_units = kv[:, 1024:].reshape(4, 2, P, 2, BANK).transpose(3, 0, 2, 1, 4).reshape(-1, 1024)
    gu = a["w_gate_up"][0]
    gate, up = (tiles_a(gu[:, s:s + HID]).reshape(HT // 2, 2 * P, 1024) for s in (0, HID))
    down = tiles_b(a["w_down"][0]).reshape(HT // 2, 2 * P, 1024)
    ffn = [gate[0], up[0]]
    for k in range(1, HT // 2):
        ffn += [gate[k], down[k - 1], up[k]]
    ffn.append(down[-1])
    wb = a["w_br_ssm"][0].reshape(2, KT, P, KT, P).transpose(3, 0, 2, 1, 4).reshape(-1, 1024)
    w_all = np.concatenate([tiles_a(w[:, :c]), tiles_a(z), tiles_a(xbc[:, chans]), tiles_a(gates), wb,
                            tiles_a(a["w_br_attn"][0]), tiles_b(a["w_out"][0]), tiles_a(kv[:, :1024]), v_units,
                            tiles_a(a["w_q_cross"][0]), tiles_b(a["w_o_cross"][0]), *ffn])
    taps = np.concatenate([a["conv_w"][0], a["conv_b"][0][None]])[:, chans]
    taps = taps.reshape(TAPS + 1, GROUPS, CT, P).transpose(1, 3, 2, 0).reshape(GROUPS * P, CT * (TAPS + 1))
    col = lambda n: a[n].reshape(-1, P).T
    return {
        "x": np.concatenate([a["x_prompt"][0], a["x_sample"][0]]),
        "mem": np.concatenate([a["mem_prompt"][0], a["mem_sample"][0]]),
        "w_all": w_all,
        "w_dt": dtw.reshape(KT, P, 64).transpose(1, 0, 2).reshape(P, KT * 64),
        "taps": taps,
        "gains": np.concatenate([col(n) for n in ("norm_mix", "norm_cross", "norm_mem", "norm_ffn", "ssm_norm")], axis=1),
        "rows": np.concatenate([a["a_log"].ravel(), a["dt_bias"].ravel(), a["d_skip"].ravel(), a["attn_sink"].ravel(),
                                a["norm_final"].ravel()]),
        "con": constants(),
    }


def kernel(**inputs):
    import concourse.bacc as bacc
    from concourse.bass_utils import run_bass_kernel_spmd

    arrays = {k: np.ascontiguousarray(v) for k, v in lay_out(inputs).items()}
    nc = bacc.Bacc("TRN2", target_bir_lowering=False, num_devices=1)
    dram = {k: nc.dram_tensor(f"{k}_dram", v.shape, F32, kind="ExternalInput").ap() for k, v in arrays.items()}
    for name, tiles in (("proj", NPROJ), ("yt", 2 * KT), ("ot", KT)):
        dram[name] = nc.dram_tensor(f"{name}_dram", [tiles * P, TOK], F32, kind="Internal").ap()
    dram["y"] = nc.dram_tensor("y_dram", [TOK, D], F32, kind="ExternalOutput").ap()
    build(nc, dram)
    y = run_bass_kernel_spmd(nc, [{f"{k}_dram": v for k, v in arrays.items()}], core_ids=[0]).results[0]["y_dram"]
    return y[:SEQ][None], y[SEQ:][None]
```

```python
from contextlib import ExitStack

import numpy as np
import concourse.bass as bass
from concourse import mybir

F32 = mybir.dt.float32
F32R = mybir.dt.float32r
ACT = mybir.ActivationFunctionType
ALU = mybir.AluOpType
AX = mybir.AxisListType

P = 128
NSEQ = 2
SEQ = 512
TOK = NSEQ * SEQ
TT = TOK // P
D = 1024
KT = D // P
EPS = 1e-6
HEADS, KVH, HD = 16, 4, 64
BLOCKS = SEQ // P
GROUPS, GH, NSTATE = 4, 8, 128
SSMH = GROUPS * GH
GW = GH * 64
XT = GW // P
CT = XT + 2
TAPS = 5
HALO = TAPS // 2
MEM = 256
MT = NSEQ * MEM // P
XHD = 256
XH = D // XHD
HID = 2816
HT = HID // P
FAR = 1e35
BANK = 512

GT = XT + CT
V0, GRP0 = 0, 2
Q0 = GRP0 + GROUPS * GT
K0 = Q0 + 8
GATE0 = K0 + 2
NPROJ = GATE0 + 16
STEPW = 5 * TT * 2 * GH + GH

U_PROJ = 0
U_WB = U_PROJ + NPROJ
U_WA = U_WB + 16
U_OUT = U_WA + 8
U_KV = U_OUT + 8
U_Q = U_KV + 16
U_O = U_Q + 8
U_FFN = U_O + 8
NUNITS = U_FFN + 3 * HT

CON_ID, CON_ONES, CON_UP, CON_LOW = 0, 128, 256, 384
CON_DIST = 512
NCON = CON_DIST + 3 * P
G_MIX, G_CROSS, G_MEM, G_FFN, G_SSM = 0, 8, 16, 24, 32
NG = 48
R_ALOG, R_DTB, R_SKIP, R_SINK = 0, 64, 128, 160
NR = R_SINK + HEADS


def constants():
    i = np.arange(P)
    c = np.zeros((P, NCON), np.float32)
    c[:, CON_ID:CON_ID + P] = np.eye(P)
    c[:, CON_ONES:CON_ONES + P] = 1.0
    c[:, CON_UP:CON_UP + P] = i[:, None] <= i[None, :]
    c[:, CON_LOW:CON_LOW + P] = i[:, None] >= i[None, :]
    k = np.arange(3 * P) - P
    dist = np.abs(i[:, None] - k[None, :]).astype(np.float32)
    c[:, CON_DIST:] = np.where(dist <= 128, dist, FAR)
    return c


class Core:

    def semaphore(self, name):
        self.stage_sems.append(self.nc.alloc_semaphore(name=name))
        return self.stage_sems[-1]

    def recycle(self):
        self.nc.clear_and_free_semaphores(self.stage_sems)
        self.stage_sems = []
        self.nc.all_engine_barrier()


def open_core(nc, ctx, dram):
    m = Core()
    m.nc, m.dram, m.stage_sems = nc, dram, []

    def sb(name, shape, dt=F32):
        return ctx.enter_context(nc.sbuf_tensor(name, shape, dt))

    m.con = sb("con", [P, NCON])
    m.gains = sb("gains", [P, NG])
    m.rows = sb("rows", [P, NR])
    m.w_raw = sb("w_raw", [P, 2, 1024])
    m.w_hi = sb("w_hi", [P, 2, 1024], F32R)
    m.w_lo = sb("w_lo", [P, 2, 1024], F32R)
    m.ps = ctx.enter_context(nc.psum_tensor("ps", [P, 8, BANK], F32))
    m.w_landed = [nc.alloc_semaphore(name=f"w_landed{r}") for r in range(2)]
    m.w_hi_ready = nc.alloc_semaphore(name="w_hi_ready")
    m.w_lo_ready = nc.alloc_semaphore(name="w_lo_ready")
    m.w_used = nc.alloc_semaphore(name="w_used")
    return m



def load_unit(sp, m, r, rows):
    sp.dma_start(m.w_raw[:, r], rows).then_inc(m.w_landed[r], 16)


def stream_weights(sp, m, first, n):
    end = min(first + n + 2, NUNITS)
    pairs = (end - first - 2) // 2
    if pairs <= 0:
        return
    w = m.dram["w_all"]
    with sp.Fori(0, pairs) as i:
        for r in range(2):
            row = sp.snap(i * (2 * P) + (first + 2 + r) * P)
            sp.wait_ge(m.w_lo_ready, i * 2 + (first + 1 + r))
            load_unit(sp, m, r, w[bass.ds(row, P), :])


def split_hi(act, m, r, landed, used):
    act.wait_ge(m.w_landed[r], landed)
    if used is not None:
        act.wait_ge(m.w_used, used)
    act.activation(m.w_hi[:, r], m.w_raw[:, r], ACT.Copy).then_inc(m.w_hi_ready, 1)


def split_lo(dve, m, r, hi_ready):
    dve.wait_ge(m.w_hi_ready, hi_ready)
    dve.tensor_tensor(m.w_lo[:, r], m.w_raw[:, r], m.w_hi[:, r].bitcast(F32),
                      ALU.subtract).then_inc(m.w_lo_ready, 1)


class Units:

    def __init__(self, m, first):
        self.m, self.first = m, first

    def hi(self, act, at, r, first=False):
        u = self.first + at
        split_hi(act, self.m, r, ring_landed(self.first, at, r), None if first else u - 1)

    def lo(self, dve, at, r):
        split_lo(dve, self.m, r, self.first + at + 1)

    def products_done(self, eng, at):
        eng.wait_ge(self.m.w_used, self.first + at + 1)

    def wait(self, pe, at):
        pe.wait_ge(self.m.w_lo_ready, self.first + at + 1)


def ring_landed(first, at, r):
    return (at - r) * 8 + (first // 2 + 1) * 16


def products(pe, out, pairs, last_of_group=True, first_of_group=True):
    n = len(pairs)
    for k, ((l_hi, l_lo), (r_hi, r_lo)) in enumerate(pairs):
        for q, (a, b) in enumerate(((l_hi, r_hi), (l_hi, r_lo), (l_lo, r_hi))):
            mm = pe.matmul(out, a, b, start=first_of_group and k == 0 and q == 0,
                           stop=last_of_group and k == n - 1 and q == 2)
    return mm


def wslice(m, r, a, b):
    return m.w_hi[:, r, a:b], m.w_lo[:, r, a:b]



def prep_stage(m):
    nc, d = m.nc, m.dram
    with ExitStack() as ctx:
        landed = m.semaphore("const_landed")
        block = ctx.enter_context(nc.Block())

        @block.sync
        def _(sp):
            sp.dma_start(m.con[:], d["con"]).then_inc(landed, 16)
            sp.dma_start(m.gains[:], d["gains"]).then_inc(landed, 16)
            sp.dma_start(m.rows[:], d["rows"].partition_broadcast(P)).then_inc(landed, 16)
            for r in range(2):
                load_unit(sp, m, r, d["w_all"][r * P:(r + 1) * P, :])
            sp.wait_ge(landed, 48)


def norm_stage(m, name, source, gain, hi, lo, tiles, source_is_dram):
    nc = m.nc
    wide = tiles // 4
    with ExitStack() as ctx:
        sem = lambda n: m.semaphore(f"{name}_{n}")
        x = ctx.enter_context(nc.sbuf_tensor(f"{name}_x", [P, tiles, D], F32)) if source_is_dram else source
        xn = ctx.enter_context(nc.sbuf_tensor(f"{name}_xn", [P, tiles, D], F32))
        ss = ctx.enter_context(nc.sbuf_tensor(f"{name}_ss", [P, 3, tiles], F32))
        landed = [sem(f"landed{t}") for t in range(tiles)] if source_is_dram else []
        squared, mean, root, rstd, scaled = sem("squared"), sem("mean"), sem("root"), sem("rstd"), sem("scaled")
        turned, hi_done, lo_done = sem("turned"), sem("hi_done"), sem("lo_done")
        block = ctx.enter_context(nc.Block())
        groups = [(n, j) for n in range(wide) for j in range(KT)]

        if source_is_dram:
            @block.sync
            def _(sp):
                for t in range(tiles):
                    sp.dma_start(x[:, t], source[t * P:(t + 1) * P, :]).then_inc(landed[t], 16)

        @block.scalar
        def _(act):
            for t in range(tiles):
                if source_is_dram:
                    act.wait_ge(landed[t], 16)
                act.activation(xn[:, t], x[:, t], ACT.Square, accum_out=ss[:, 0, t:t + 1]).then_inc(squared, 1)
            act.wait_ge(mean, 1)
            act.activation(ss[:, 2], ss[:, 1], ACT.Sqrt).then_inc(root, 1)
            for i, (n, j) in enumerate(groups):
                act.wait_ge(turned, i + 1)
                act.activation(hi[:, j, n * BANK:(n + 1) * BANK], m.ps[:, 4 + i % 4], ACT.Copy,
                               scale=m.gains[:, gain + j:gain + j + 1]).then_inc(hi_done, 1)

        @block.vector
        def _(dve):
            dve.wait_ge(squared, tiles)
            dve.tensor_scalar(ss[:, 1], ss[:, 0], 1.0 / D, EPS, ALU.mult, ALU.add).then_inc(mean, 1)
            dve.wait_ge(root, 1)
            dve.reciprocal(ss[:, 0], ss[:, 2]).then_inc(rstd, 1)
            dve.wait_ge(rstd, 1)
            for t in range(tiles):
                dve.tensor_scalar(xn[:, t], x[:, t], ss[:, 0, t:t + 1], None, ALU.mult).then_inc(scaled, 1)
            for i, (n, j) in enumerate(groups):
                dve.wait_ge(hi_done, i + 1)
                dve.scalar_tensor_tensor(lo[:, j, n * BANK:(n + 1) * BANK], m.ps[:, 4 + i % 4],
                                         m.gains[:, gain + j:gain + j + 1],
                                         hi[:, j, n * BANK:(n + 1) * BANK].bitcast(F32),
                                         ALU.mult, ALU.subtract).then_inc(lo_done, 1)

        @block.tensor
        def _(pe):
            ident = m.con[:, CON_ID:CON_ID + P]
            for i, (n, j) in enumerate(groups):
                if j == 0:
                    pe.wait_ge(scaled, 4 * (n + 1))
                if i >= 4:
                    pe.wait_ge(lo_done, i - 3)
                for t in range(4):
                    mm = pe.transpose(m.ps[:, 4 + i % 4, t * P:(t + 1) * P],
                                      xn[:, 4 * n + t, j * P:(j + 1) * P], ident)
                mm.then_inc(turned, 1)


class Projection:

    def __init__(self, m, ctx):
        self.m = m
        self.out = ctx.enter_context(m.nc.sbuf_tensor("proj_out", [P, 2, TOK], F32))
        self.drained = m.nc.alloc_semaphore(name="proj_drained")
        self.stored = [m.nc.alloc_semaphore(name=f"proj_stored{r}") for r in range(2)]

    def evacuate(self, act, at, r, func, scale=1.0, peel=False):
        row = at * P if isinstance(at, int) else act.snap(at * P)
        if not peel:
            act.wait_ge(self.stored[r], (at - r) * 8)
        act.wait_ge(self.m.w_used, at + 1)
        act.activation(self.out[:, r], self.m.ps[:, 2 * r:2 * r + 2].rearrange("p a b -> p (a b)"), func,
                       scale=scale).then_inc(self.drained, 1)
        act.wait_ge(self.drained, at + 1)
        act.dma_start(self.m.dram["proj"][bass.ds(row, P), :], self.out[:, r]).then_inc(self.stored[r], 16)

    def half(self, pe, u_hi, u_lo, at, r, n, peel=False):
        m = self.m
        if n == 0:
            pe.wait_ge(m.w_lo_ready, at + 1)
            if not peel:
                pe.wait_ge(self.drained, at - 1)
        s = slice(n * BANK, (n + 1) * BANK)
        mm = products(pe, m.ps[:, 2 * r + n],
                      [(wslice(m, r, k * P, (k + 1) * P), (u_hi[:, k, s], u_lo[:, k, s])) for k in range(KT)])
        if n == 1:
            mm.then_inc(m.w_used, 1)


def first_stage(m, pr, u_hi, u_lo):
    nc, d = m.nc, m.dram
    with ExitStack() as ctx:
        sem = lambda n: m.semaphore(f"step_{n}")
        w_dt = ctx.enter_context(nc.sbuf_tensor("w_dt", [P, KT * 64], F32))
        w_dt_hi = ctx.enter_context(nc.sbuf_tensor("w_dt_hi", [P, KT * 64], F32R))
        w_dt_lo = ctx.enter_context(nc.sbuf_tensor("w_dt_lo", [P, KT * 64], F32R))
        dt_landed, dt_hi, dt_lo, dt_done = sem("dt_landed"), sem("dt_hi"), sem("dt_lo"), sem("dt_done")
        units = Units(m, U_PROJ)
        N = GRP0 + GT
        tmp = [ctx.enter_context(nc.sbuf_tensor(f"step_t{i}", [P, TT, 64], F32)) for i in range(4)]
        sums, dt, exp_a, w_in, dec = (ctx.enter_context(nc.sbuf_tensor(f"step_{n}", [P, TT, 64], F32))
                                      for n in ("sums", "dt", "exp_a", "w_in", "dec"))
        rows = ctx.enter_context(nc.sbuf_tensor("sum_rows", [64, TOK], F32))
        by_group = ctx.enter_context(nc.sbuf_tensor("by_group", [P, GROUPS, STEPW], F32))
        neg_a = ctx.enter_context(nc.sbuf_tensor("neg_a", [P, 64], F32))
        dve_step, act_step, pe_step = sem("dve"), sem("act"), sem("pe")
        rows_ready, grouped, stored = sem("rows_ready"), sem("grouped"), sem("stored")
        block = ctx.enter_context(nc.Block())
        flat = lambda ap: ap.rearrange("p a b -> p (a b)")
        bias = m.rows[:, R_DTB:R_DTB + 64].unsqueeze(1).to_broadcast([P, TT, 64])
        TERMS = 9

        n_dve = 0

        @block.vector
        def _(dve):
            nonlocal n_dve
            count = [0]

            def chain(ins):
                count[0] += 1
                ins.then_inc(dve_step, 1)
                dve.wait_ge(dve_step, count[0])

            units.lo(dve, 0, 0)
            dve.wait_ge(dt_hi, 1)
            dve.tensor_tensor(w_dt_lo[:], w_dt[:], w_dt_hi[:].bitcast(F32), ALU.subtract).then_inc(dt_lo, 1)
            units.lo(dve, 1, 1)
            x, mag, z, z2 = tmp
            dve.wait_ge(dt_done, 1)
            chain(dve.tensor_tensor(x[:], m.ps[:, 7].rearrange("p (a b) -> p a b", a=TT), bias, ALU.add))
            chain(dve.tensor_scalar(mag[:], x[:], -1.0, None, ALU.mult))
            chain(dve.tensor_tensor(mag[:], mag[:], x[:], ALU.min))
            dve.wait_ge(act_step, 1)
            chain(dve.tensor_scalar(z[:], mag[:], 2.0, None, ALU.add))
            chain(dve.reciprocal(z[:], z[:]))
            chain(dve.tensor_tensor(z[:], z[:], mag[:], ALU.mult))
            chain(dve.tensor_tensor(z2[:], z[:], z[:], ALU.mult))
            chain(dve.tensor_scalar(mag[:], z2[:], 2.0 / (2 * TERMS - 1), 2.0 / (2 * TERMS - 3), ALU.mult, ALU.add))
            for t in range(TERMS - 3, -1, -1):
                chain(dve.tensor_tensor(mag[:], mag[:], z2[:], ALU.mult))
                chain(dve.tensor_scalar(mag[:], mag[:], 2.0 / (2 * t + 1), None, ALU.add))
            chain(dve.tensor_tensor(mag[:], mag[:], z[:], ALU.mult))
            chain(dve.scalar_tensor_tensor(dt[:], x[:], 0.0, mag[:], ALU.max, ALU.add))
            dve.wait_ge(act_step, 2)
            chain(dve.tensor_scalar(neg_a[:], neg_a[:], -1.0, None, ALU.mult))
            dta = tmp[0]
            chain(dve.tensor_tensor(dta[:], dt[:], neg_a[:].unsqueeze(1).to_broadcast([P, TT, 64]), ALU.mult))
            n_dve = count[0]
            units.lo(dve, 2, 0)
            dve.wait_ge(pe_step, 1)
            for way in range(2):
                src = m.ps[:, 4 + way, 0:TT * 32].rearrange("p (a b) -> p a b", a=TT)
                chain(dve.tensor_copy(sums[:, :, way * 32:way * 32 + 32], src))
            dve.wait_ge(pe_step, 2)
            tot = m.ps[:, 6].rearrange("p (a b) -> p a b", a=TT)
            chain(dve.tensor_tensor(tmp[1][:], tot, sums[:], ALU.subtract))
            units.lo(dve, 3, 1)
            dve.wait_ge(act_step, 5)
            chain(dve.tensor_tensor(w_in[:], tmp[2][:], dt[:], ALU.mult))
            units.lo(dve, 4, 0)
            dve.wait_ge(pe_step, 3)
            dve.tensor_copy(rows[:], m.ps[0:64, 4:6].rearrange("p a b -> p (a b)")).then_inc(rows_ready, 1)
            for g in range(GROUPS):
                for i, src in enumerate((sums, dt, exp_a, w_in, dec)):
                    dve.tensor_copy(by_group[:, g, i * 2 * GH * TT:(i + 1) * 2 * GH * TT]
                                    .rearrange("p (c w h) -> p c w h", c=TT, w=2),
                                    src[:].rearrange("p c (w h) -> p c w h", w=2)[:, :, :, g * GH:(g + 1) * GH]
                                    ).then_inc(grouped, 1)
                dve.tensor_copy(by_group[:, g, STEPW - GH:], m.rows[:, R_SKIP + g * GH:R_SKIP + (g + 1) * GH]
                                ).then_inc(grouped, 1)
                units.lo(dve, 5 + g, (5 + g) % 2)
            for u in range(5 + GROUPS, N):
                units.lo(dve, u, u % 2)

        @block.sync
        def _(sp):
            def load_weights(u):
                sp.wait_ge(m.w_lo_ready, u - 1)
                load_unit(sp, m, u % 2, d["w_all"][u * P:(u + 1) * P, :])

            sp.dma_start(w_dt[:], d["w_dt"]).then_inc(dt_landed, 16)
            for u in range(2, 7):
                load_weights(u)
            sp.wait_ge(rows_ready, 1)
            dst = d["sums"].rearrange("(g c f) (w i t) -> g f w i c t", g=GROUPS, c=TT, w=2, i=4)
            n = 0
            for g in range(GROUPS):
                for f in range(2):
                    for way in range(2):
                        p0 = way * 32 + g * GH + f * 4
                        sp.dma_start(dst[g, f, way], rows[p0:p0 + 4].rearrange("p (c t) -> p c t", c=TT)
                                     ).then_inc(stored, 16)
                        n += 1
            for g in range(GROUPS):
                load_weights(7 + g)
                sp.wait_ge(grouped, 6 * (g + 1))
                sp.dma_start(d["steps"][g * P:(g + 1) * P, :], by_group[:, g]).then_inc(stored, 16)
            for u in range(7 + GROUPS, N + 2):
                load_weights(u)
            sp.wait_ge(stored, 16 * (n + GROUPS))

        @block.scalar
        def _(act):
            def service(j):
                if j + 1 < N:
                    units.hi(act, j + 1, (j + 1) % 2, first=j == 0)
                if j:
                    tile = j - 1
                    pr.evacuate(act, tile, tile % 2, ACT.Silu if GRP0 <= tile < GRP0 + XT else ACT.Copy, peel=tile < 2)

            units.hi(act, 0, 0, first=True)
            act.wait_ge(dt_landed, 16)
            act.activation(w_dt_hi[:], w_dt[:], ACT.Copy).then_inc(dt_hi, 1)
            service(0)
            act.wait_ge(dve_step, 3)
            act.activation(tmp[1][:], tmp[1][:], ACT.Exp).then_inc(act_step, 1)
            act.activation(neg_a[:], m.rows[:, R_ALOG:R_ALOG + 64], ACT.Exp).then_inc(act_step, 1)
            service(1)
            act.wait_ge(dve_step, n_dve + 2)
            act.activation(exp_a[:], sums[:], ACT.Exp).then_inc(act_step, 1)
            act.wait_ge(dve_step, n_dve + 3)
            act.activation(dec[:], m.ps[:, 6].rearrange("p (a b) -> p a b", a=TT), ACT.Exp).then_inc(act_step, 1)
            act.activation(tmp[2][:], tmp[1][:], ACT.Exp).then_inc(act_step, 1)
            for j in range(2, N + 1):
                service(j)
            for r in range(2):
                act.wait_ge(pr.stored[r], N * 8)

        @block.tensor
        def _(pe):
            def project(u):
                for n in range(2):
                    pr.half(pe, u_hi, u_lo, u, u % 2, n, peel=u < 2)

            pe.wait_ge(dt_lo, 1)
            for t in range(TT):
                s = slice(t * P, (t + 1) * P)
                mm = products(pe, m.ps[:, 7, t * 64:(t + 1) * 64],
                              [((u_hi[:, k, s], u_lo[:, k, s]),
                                (w_dt_hi[:, k * 64:(k + 1) * 64], w_dt_lo[:, k * 64:(k + 1) * 64])) for k in range(KT)])
            mm.then_inc(dt_done, 1)
            project(0)
            project(1)
            dta = tmp[0]
            pe.wait_ge(dve_step, n_dve)
            for way, tri in ((0, CON_UP), (1, CON_LOW)):
                mm = pe.matmul(m.ps[:, 4 + way, 0:TT * 32], m.con[:, tri:tri + P],
                               dta[:, :, way * 32:way * 32 + 32], start=True, stop=True)
            mm.then_inc(pe_step, 1)
            pe.matmul(m.ps[:, 6], m.con[:, CON_ONES:CON_ONES + P], flat(dta[:]), start=True,
                      stop=True).then_inc(pe_step, 1)
            project(2)
            pe.wait_ge(dve_step, n_dve + 3)
            for c in range(TT):
                mm = pe.transpose(m.ps[0:64, 4 + c // 4, (c % 4) * P:(c % 4 + 1) * P], sums[:, c],
                                  m.con[:, CON_ID:CON_ID + P])
            mm.then_inc(pe_step, 1)
            project(3)
            with pe.Fori(2, N // 2) as i:
                for r in range(2):
                    for n in range(2):
                        pr.half(pe, u_hi, u_lo, i * 2 + r, r, n)


def bc(ap, n):
    return ap.unsqueeze(len(ap.shape)).to_broadcast([*ap.shape, n])


def ssd_stage(m, pr, u_hi, u_lo):
    nc, d = m.nc, m.dram
    STEPS = 2 * TT
    LAST = STEPS + 5
    NS = 12
    NT = 2 * (XT + 1)
    UG = GRP0 + GT
    order = [(q, way, k) for way in (1, 0) for q in range(NSEQ) for k in range(BLOCKS - 1)]
    gives = lambda n: order[n][0] * BLOCKS + (order[n][2] if order[n][1] == 0 else BLOCKS - 1 - order[n][2])
    index = {(order[n][1], gives(n) + (1 if order[n][1] == 0 else -1)): n for n in range(NS)}
    forward = {gives(n): n for n in range(NS // 2, NS)}
    slot = lambda n: n if n < NS // 2 else NS // 2 + n % 2
    offs = [[(way, index[way, c]) for way in range(2) if (way, c) in index] for c in range(TT)]
    off_before = [sum(len(o) for o in offs[:c]) for c in range(TT)]
    halves = {0: (5, 0), 2: (5, 1), 3: (6, 0), 5: (6, 1), 6: (7, 0), 8: (7, 1), 9: (8, 0), 11: (8, 1), 12: (9, 0), 14: (9, 1)}
    services = {0: 5, 3: 6, 6: 7, 9: 8, 12: 9}
    last_drain = 15
    FB = 3
    MS = 4
    with ExitStack() as ctx:
        sem = lambda n: m.semaphore(f"ssd_{n}")
        sb = lambda n, s, t=F32: ctx.enter_context(nc.sbuf_tensor(n, s, t))
        xpad = sb("xpad", [P, 2, NSEQ, SEQ + 2 * HALO])
        taps = sb("taps", [P, CT * (TAPS + 1)])
        conv = sb("conv", [P, 4, NSEQ, SEQ])
        xs = sb("xs", [P, TT, GW])
        b_tm = sb("b_tm", [P, TT, NSTATE])
        states = sb("states", [P, NS // 2 + 2, GW])
        grp = sb("grp", [P, STEPW])
        xw = sb("xw", [P, 2, GW])
        fb = sb("fb", [P, FB, 2, BANK])
        tl = sb("tl", [P, 2, BANK])
        tu = sb("tu", [P, MS, BANK])
        cb = sb("cb", [P, 2, 2, P])
        y = sb("y", [P, 2, GW])
        off = sb("off", [P, 2, GW])
        zy = sb("zy", [P, 2, XT, P])
        conv_slot = [0, 1, 0, 1, 2, 3]
        flat_conv = lambda i: conv[:, conv_slot[i]].rearrange("p a b -> p (a b)")
        bm_t, cm_t = flat_conv(XT), flat_conv(XT + 1)
        grp5 = grp[:, 0:STEPW - GH].rearrange("p (a c w h) -> p a c w h", a=5, c=TT, w=2)
        SUMS, DT, EXPA, WIN, DEC = (grp5[:, i] for i in range(5))
        skip = grp[:, STEPW - GH:]
        heads = lambda ap: ap.rearrange("p (h w) -> p h w", h=GH)

        taps_landed, grp_landed = sem("taps_landed"), sem("grp_landed")
        x_landed, z_landed, y_stored = ([sem(f"{n}{r}") for r in range(2)] for n in ("x_landed", "z_landed", "y_stored"))
        fb_landed = [sem(f"fb_landed{r}") for r in range(FB)]
        fb_count = lambda k: len(range(k % FB, k + 1, FB))
        fb_total = lambda k: len(range(k % FB, STEPS, FB))
        pads, conv_step, conv_done = sem("pads"), sem("conv_step"), sem("conv_done")
        turned, tm_ready = sem("turned"), sem("tm_ready")
        xw_ready, st_done, decayed, st_ready = sem("xw_ready"), sem("st_done"), sem("decayed"), sem("st_ready")
        cb_done, cb_ready = sem("cb_done"), sem("cb_ready")
        b_shifted, min_done, e_ready = sem("b_shifted"), sem("min_done"), sem("e_ready")
        masked, t_sum, m_ready = sem("masked"), sem("t_sum"), sem("m_ready")
        y_done, skipped, y_read = sem("y_done"), sem("skipped"), sem("y_read")
        off_done, off_read, off_added = sem("off_done"), sem("off_read"), sem("off_added")
        y_turned, yz_ready = sem("y_turned"), sem("yz_ready")
        block = ctx.enter_context(nc.Block())
        units = Units(m, UG)

        def groups(eng, group):
            with eng.Fori(0, GROUPS - 1) as g:
                group(g, False)
            group(GROUPS - 1, True)

        @block.sync
        def _(sp):
            at = lambda v: v if isinstance(v, int) else sp.snap(v)

            def load_weights(g, u):
                row = at(g * (GT * P) + (UG + u) * P)
                sp.wait_ge(m.w_lo_ready, g * GT + (UG + u - 1))
                load_unit(sp, m, u % 2, d["w_all"][bass.ds(row, P), :])

            def load_x(g, i):
                row = at(g * (GT * P) + (GRP0 + XT + i) * P)
                if i < 2:
                    sp.wait_ge(pr.stored[i % 2], g * (GT * 8) + (GRP0 + XT + 2) * 8)
                else:
                    sp.wait_ge(conv_step, g * (CT * TAPS) + (i - 1) * TAPS)
                sp.dma_start(xpad[:, i % 2, :, HALO:HALO + SEQ],
                             d["proj"][bass.ds(row, P), :].rearrange("p (a b) -> p a b", a=NSEQ)).then_inc(x_landed[i % 2], 16)

            def load_taps(g):
                row = at(g * P)
                sp.dma_start(taps[:], d["taps"][bass.ds(row, P), :]).then_inc(taps_landed, 16)

            def load_fb(g, k):
                row = at(g * STEPS + k)
                if k >= FB:
                    sp.wait_ge(m_ready, g * STEPS + (k - FB + 1))
                sp.dma_start(fb[:, k % FB].rearrange("p a b -> p (a b)"),
                             d["sums"][bass.ds(row, 1), :].squeeze(0).partition_broadcast(P)).then_inc(fb_landed[k % FB], 16)

            def load_z(g, c):
                row = at(g * (GT * P) + GRP0 * P)
                if c >= 2 or not isinstance(g, int) or g:
                    sp.wait_ge(y_stored[c % 2], g * (TT * 8) + (c // 2) * 16)
                sp.dma_start(zy[:, c % 2], d["proj"][bass.ds(row, XT * P), c * P:(c + 1) * P]
                             .rearrange("(a p) t -> p a t", p=P)).then_inc(z_landed[c % 2], 16)

            def store_y(g, c):
                row = at(g * (XT * P))
                sp.wait_ge(yz_ready, g * TT + (c + 1))
                sp.dma_start(d["yt"][bass.ds(row, XT * P), c * P:(c + 1) * P].rearrange("(a p) t -> p a t", p=P),
                             zy[:, c % 2]).then_inc(y_stored[c % 2], 16)

            def group(g, last):
                g_row = at(g * P)
                load_weights(g, 3)
                sp.dma_start(grp[:], d["steps"][bass.ds(g_row, P), :]).then_inc(grp_landed, 16)
                load_x(g, 2)
                load_x(g, 3)
                load_weights(g, 4)
                load_x(g, 4)
                load_x(g, 5)
                load_weights(g, 5)
                for k in range(FB):
                    load_fb(g, k)
                load_weights(g, 6)
                load_weights(g, 7)
                for k in range(LAST):
                    if k >= 6 and k % 2 == 0:
                        store_y(g, (k - 6) // 2)
                    if k >= 7 and k % 2 == 1 and (k - 7) // 2 + 2 < TT:
                        load_z(g, (k - 7) // 2 + 2)
                    if k in services and not (last and services[k] == 9):
                        load_weights(g, services[k] + 3)
                    if k + FB < STEPS:
                        load_fb(g, k + FB)
                    if k == LAST - 6 and not last:
                        load_taps(g + 1)
                        load_x(g + 1, 0)
                        load_x(g + 1, 1)
                if not last:
                    load_z(g + 1, 0)
                    load_z(g + 1, 1)

            load_taps(0)
            sp.wait_ge(pads, 1)
            load_x(0, 0)
            load_x(0, 1)
            load_z(0, 0)
            load_z(0, 1)
            load_weights(0, 2)
            groups(sp, group)
            for r in range(2):
                sp.wait_ge(y_stored[r], GROUPS * TT * 8)

        @block.vector
        def _(dve):
            def service(g, j):
                units.lo(dve, g * GT + (j + 1), (j + 1) % 2)

            def convolve(g, i):
                dve.wait_ge(x_landed[i % 2], g * (8 * CT) + 16 * (i // 2 + 1))
                if 2 <= i < XT:
                    dve.wait_ge(turned, g * NT + 2 * (i - 1))
                for t in range(TAPS):
                    w = taps[:, i * (TAPS + 1) + t:i * (TAPS + 1) + t + 1]
                    src, dst = xpad[:, i % 2, :, t:t + SEQ], conv[:, conv_slot[i]]
                    if t == 0:
                        ins = dve.tensor_scalar(dst, src, w, None, ALU.mult)
                    else:
                        dve.wait_ge(conv_step, g * (CT * TAPS) + (i * TAPS + t))
                        ins = dve.scalar_tensor_tensor(dst, src, w, dst, ALU.mult, ALU.add)
                    ins.then_inc(conv_step, 1)

            def state(g, n, bank):
                dve.wait_ge(st_done, g * NS + n + 1)
                if n >= NS // 2 + 2:
                    taker = gives(n - 2) + 1
                    dve.wait_ge(off_done, g * NS + off_before[taker] + 1)
                if order[n][2] == 0:
                    dve.tensor_copy(states[:, slot(n)], m.ps[:, bank]).then_inc(st_ready, 1)
                else:
                    dve.wait_ge(st_ready, g * NS + n)
                    dve.tensor_tensor(heads(states[:, slot(n)]), heads(states[:, slot(n - 1)]),
                                      bc(DEC[:, gives(n), order[n][1]], 64), ALU.mult).then_inc(decayed, 1)
                    dve.wait_ge(decayed, g * 8 + (n - n // 3))
                    dve.tensor_tensor(states[:, slot(n)], states[:, slot(n)], m.ps[:, bank], ALU.add).then_inc(st_ready, 1)

            def mask(g, c):
                dve.wait_ge(cb_done, g * TT + c + 1)
                if c >= 2:
                    dve.wait_ge(masked, g * (2 * STEPS) + 4 * (c - 1))
                for way, tri in ((0, CON_UP), (1, CON_LOW)):
                    dve.tensor_tensor(cb[:, c % 2, way], m.ps[:, 7, 0:P], m.con[:, tri:tri + P],
                                      ALU.mult).then_inc(cb_ready, 1)

            def finish_chunk(g, c):
                s = c % 2
                dve.wait_ge(skipped, g * TT + c + 1)
                dve.wait_ge(y_done, g * STEPS + 2 * c + 2)
                dve.tensor_tensor(y[:, s], y[:, s], m.ps[:, 4], ALU.add).then_inc(y_read, 1)
                for n, (way, _) in enumerate(offs[c]):
                    at = off_before[c] + n
                    if n == 0:
                        dve.wait_ge(off_done, g * NS + at + len(offs[c]))
                    if at >= 2:
                        dve.wait_ge(off_added, g * NS + at - 1)
                    dve.tensor_tensor(heads(off[:, at % 2]), heads(m.ps[:, 5 + way]), bc(EXPA[:, c, way], 64),
                                      ALU.mult).then_inc(off_read, 1)
                for n in range(len(offs[c])):
                    at = off_before[c] + n
                    dve.wait_ge(off_read, g * NS + at + 1)
                    if n == 0:
                        dve.wait_ge(y_read, g * TT + c + 1)
                    else:
                        dve.wait_ge(off_added, g * NS + at)
                    dve.tensor_tensor(y[:, s], y[:, s], off[:, at % 2], ALU.add).then_inc(off_added, 1)

            def group(g, last):
                dve.wait_ge(taps_landed, g * 16 + 16)
                service(g, 0)
                convolve(g, 0)
                convolve(g, 1)
                service(g, 1)
                convolve(g, 2)
                convolve(g, 3)
                service(g, 2)
                convolve(g, 4)
                convolve(g, 5)
                service(g, 3)
                dve.wait_ge(grp_landed, g * 16 + 16)
                state(g, 0, 6)
                state(g, 1, 7)
                service(g, 4)
                for n in range(2, NS // 2):
                    state(g, n, 6 + n % 2)
                mask(g, 0)
                for k in range(LAST):
                    c, h = divmod(k, 2)
                    if k >= 4 and h == 0 and (k - 4) // 2 < TT:
                        finish_chunk(g, (k - 4) // 2)
                    if k < STEPS:
                        dve.wait_ge(b_shifted, g * STEPS + k + 1)
                        for i in range(4):
                            f = fb[:, k % FB, 0, i * P:(i + 1) * P]
                            ins = dve.scalar_tensor_tensor(f, f, SUMS[:, c, 0, 4 * h + i:4 * h + i + 1],
                                                           fb[:, k % FB, 1, i * P:(i + 1) * P], ALU.subtract, ALU.min)
                        ins.then_inc(min_done, 1)
                    if 1 <= k <= STEPS:
                        j = k - 1
                        dve.wait_ge(masked, g * (2 * STEPS) + 2 * j + 2)
                        dve.tensor_tensor(tu[:, j % MS], tu[:, j % MS], tl[:, j % 2], ALU.add).then_inc(t_sum, 1)
                        dve.wait_ge(e_ready, g * STEPS + j + 1)
                        dve.wait_ge(t_sum, g * STEPS + j + 1)
                        dve.tensor_tensor(tu[:, j % MS], tu[:, j % MS], fb[:, j % FB, 0], ALU.mult).then_inc(m_ready, 1)
                    if k >= 6 and h == 0 and (k - 6) // 2 < TT:
                        gated = (k - 6) // 2
                        dve.wait_ge(z_landed[gated % 2], g * (8 * TT) + 16 * (gated // 2 + 1))
                        dve.wait_ge(y_turned, g * TT + gated + 1)
                        dve.tensor_tensor(zy[:, gated % 2], zy[:, gated % 2], m.ps[:, 7].rearrange("p (a b) -> p a b", a=XT),
                                          ALU.mult).then_inc(yz_ready, 1)
                    if h == 0 and c + 1 < TT:
                        mask(g, c + 1)
                    if h == 1 and c in forward:
                        state(g, forward[c], 7)
                    if k in services and not (last and services[k] == 9):
                        service(g, services[k])

            units.lo(dve, 0, 0)
            dve.wait_ge(pads, 1)
            groups(dve, group)

        @block.scalar
        def _(act):
            def drain(g, j, last):
                z = not last and j < XT
                pr.evacuate(act, g * GT + (UG + j), j % 2, ACT.Silu if z else ACT.Copy,
                            scale=HD ** -0.5 if last and j < K0 - Q0 else 1.0)

            def service(g, j, last):
                if not (last and j == 9):
                    units.hi(act, g * GT + (j + 1), (j + 1) % 2)
                if j:
                    drain(g, j - 1, last)

            def silu(g, i):
                act.wait_ge(conv_step, g * (CT * TAPS) + TAPS * (i + 1))
                act.activation(flat_conv(i), flat_conv(i), ACT.Silu,
                               bias=taps[:, i * (TAPS + 1) + TAPS:(i + 1) * (TAPS + 1)]).then_inc(conv_done, 1)

            def copy_turned(g, i):
                for n in range(2):
                    act.wait_ge(turned, g * NT + 2 * i + n + 1)
                    dst = b_tm[:, 4 * n:4 * n + 4] if i == XT else xs[:, 4 * n:4 * n + 4, i * P:(i + 1) * P]
                    act.activation(dst, m.ps[:, 4 + (2 * i + n) % 4].rearrange("p (a b) -> p a b", a=4),
                                   ACT.Copy).then_inc(tm_ready, 1)

            def group(g, last):
                for r in range(2):
                    act.wait_ge(pr.stored[r], g * (GT * 8) + UG * 8)
                service(g, 0, last)
                silu(g, 0)
                silu(g, 1)
                service(g, 1, last)
                copy_turned(g, 0)
                silu(g, 2)
                copy_turned(g, 1)
                silu(g, 3)
                service(g, 2, last)
                copy_turned(g, 2)
                silu(g, 4)
                copy_turned(g, 3)
                service(g, 3, last)
                silu(g, 5)
                copy_turned(g, 4)
                service(g, 4, last)
                for k in range(STEPS):
                    act.wait_ge(min_done, g * STEPS + k + 1)
                    act.activation(fb[:, k % FB, 0], fb[:, k % FB, 0], ACT.Exp).then_inc(e_ready, 1)
                    if k in services:
                        service(g, services[k], last)
                    if k == last_drain:
                        drain(g, 9, last)

            units.hi(act, 0, 0)
            groups(act, group)
            for r in range(2):
                act.wait_ge(pr.stored[r], (UG + GROUPS * GT) * 8)

        @block.gpsimd
        def _(pool):
            def weigh(g, n):
                if n >= 2:
                    pool.wait_ge(st_done, g * NS + n - 1)
                c = gives(n)
                pool.tensor_tensor(heads(xw[:, n % 2]), heads(xs[:, c]), bc(WIN[:, c, order[n][1]], 64),
                                   ALU.mult).then_inc(xw_ready, 1)

            def start_y(g, c):
                if c >= 2:
                    pool.wait_ge(y_turned, g * TT + c - 1)
                pool.tensor_tensor(heads(y[:, c % 2]), heads(xs[:, c]), bc(skip, 64), ALU.mult).then_inc(skipped, 1)

            def group(g, last):
                pool.wait_ge(grp_landed, g * 16 + 16)
                pool.wait_ge(tm_ready, g * NT + 2 * XT)
                for n in range(NS // 2):
                    weigh(g, n)
                for k in range(STEPS):
                    c, h = divmod(k, 2)
                    if h == 0 and c in forward:
                        weigh(g, forward[c])
                    pool.wait_ge(fb_landed[k % FB], g * (16 * fb_total(k)) + 16 * fb_count(k))
                    b = fb[:, k % FB, 1].rearrange("p (a b) -> p a b", a=4)
                    pool.tensor_tensor(b, b, bc(SUMS[:, c, 1, 4 * h:4 * h + 4], P), ALU.subtract).then_inc(b_shifted, 1)
                    if h == 0:
                        pool.wait_ge(cb_ready, g * (2 * TT) + 2 * c + 2)
                    if k >= 2:
                        pool.wait_ge(t_sum, g * STEPS + k - 1)
                    if k >= MS:
                        pool.wait_ge(y_done, g * STEPS + k - MS + 1)
                    for way, dst in ((1, tl[:, k % 2]), (0, tu[:, k % MS])):
                        one = cb[:, c % 2, way].unsqueeze(1).to_broadcast([P, 4, P])
                        pool.tensor_tensor(dst.rearrange("p (a b) -> p a b", a=4), one,
                                           bc(DT[:, c, way, 4 * h:4 * h + 4], P), ALU.mult).then_inc(masked, 1)
                    if k >= 3 and h == 1:
                        start_y(g, (k - 3) // 2)
                start_y(g, TT - 1)

            pool.memset(xpad[:], 0.0).then_inc(pads, 1)
            groups(pool, group)

        @block.tensor
        def _(pe):
            ident = m.con[:, CON_ID:CON_ID + P]

            def project(g, j, n):
                pr.half(pe, u_hi, u_lo, g * GT + (UG + j), j % 2, n)

            def turn(g, i):
                pe.wait_ge(conv_done, g * CT + i + 1)
                for n in range(2):
                    if i >= 2:
                        pe.wait_ge(tm_ready, g * NT + 2 * i + n - 3)
                    for q in range(4):
                        c = 4 * n + q
                        mm = pe.transpose(m.ps[:, 4 + (2 * i + n) % 4, q * P:(q + 1) * P],
                                          flat_conv(i)[:, c * P:(c + 1) * P], ident)
                    mm.then_inc(turned, 1)

            def state(g, n, bank):
                pe.wait_ge(xw_ready, g * NS + n + 1)
                pe.matmul(m.ps[:, bank], b_tm[:, gives(n)], xw[:, n % 2], start=True, stop=True).then_inc(st_done, 1)

            def group(g, last):
                project(g, 0, 0)
                project(g, 0, 1)
                turn(g, 0)
                project(g, 1, 0)
                turn(g, 1)
                project(g, 1, 1)
                turn(g, 2)
                project(g, 2, 0)
                turn(g, 3)
                project(g, 2, 1)
                project(g, 3, 0)
                turn(g, 4)
                project(g, 3, 1)
                pe.wait_ge(tm_ready, g * NT + NT)
                for n in range(NS // 2):
                    if n >= 2:
                        pe.wait_ge(st_ready, g * NS + n - 1)
                    state(g, n, 6 + n % 2)
                    if n in (1, 3):
                        project(g, 4, n // 2)
                pe.wait_ge(conv_done, g * CT + CT)
                pe.wait_ge(st_ready, g * NS + NS // 2)

                def correlate(c):
                    chunk = slice(c * P, (c + 1) * P)
                    pe.matmul(m.ps[:, 7, 0:P], bm_t[:, chunk], cm_t[:, chunk], start=True, stop=True).then_inc(cb_done, 1)

                correlate(0)
                for k in range(LAST):
                    if 2 <= k < STEPS + 2:
                        j = k - 2
                        c, h = divmod(j, 2)
                        chunk = slice(c * P, (c + 1) * P)
                        pe.wait_ge(m_ready, g * STEPS + j + 1)
                        if h == 0:
                            if c >= 1:
                                pe.wait_ge(y_read, g * TT + c)
                                pe.wait_ge(off_read, g * NS + off_before[c])
                            for way, n in offs[c]:
                                if way == 0:
                                    pe.wait_ge(st_ready, g * NS + n + 1)
                                pe.matmul(m.ps[:, 5 + way], cm_t[:, chunk], states[:, slot(n)], start=True,
                                          stop=True).then_inc(off_done, 1)
                        for i in range(4):
                            hh = 4 * h + i
                            mm = pe.matmul(m.ps[:, 4, hh * 64:(hh + 1) * 64], tu[:, j % MS, i * P:(i + 1) * P],
                                           xs[:, c, hh * 64:(hh + 1) * 64], start=True, stop=True)
                        mm.then_inc(y_done, 1)
                    c, h = divmod(k, 2)
                    if h == 0 and c + 1 < TT:
                        pe.wait_ge(cb_ready, g * (2 * TT) + 2 * c + 2)
                        if k >= 6:
                            pe.wait_ge(yz_ready, g * TT + (k - 4) // 2)
                        elif c >= 1:
                            pe.wait_ge(st_ready, g * NS + forward[c - 1] + 1)
                        correlate(c + 1)
                    if k < STEPS and h == 1:
                        pe.wait_ge(cb_ready, g * (2 * TT) + 2 * min(c + 2, TT))
                        if c in forward:
                            state(g, forward[c], 7)
                    if k in halves:
                        project(g, *halves[k])
                    if k >= 5 and h == 1 and (k - 5) // 2 < TT:
                        t = (k - 5) // 2
                        pe.wait_ge(off_added, g * NS + off_before[t] + len(offs[t]))
                        if c in forward:
                            pe.wait_ge(st_ready, g * NS + forward[c] + 1)
                        if k >= STEPS - 1:
                            pe.wait_ge(yz_ready, g * TT + t)
                        for i in range(4):
                            mm = pe.transpose(m.ps[:, 7, i * P:(i + 1) * P], y[:, t % 2, i * P:(i + 1) * P], ident)
                        mm.then_inc(y_turned, 1)

            groups(pe, group)


def attention_stage(m, pr, u_hi, u_lo):
    nc, d = m.nc, m.dram
    spans = [(max(b - 1, 0), min(b + 1, BLOCKS - 1) - max(b - 1, 0) + 1, P if b == 0 else 0) for b in range(BLOCKS)]
    slopes = [2.0 ** (-8.0 * (h + 1) / HEADS) for h in range(HEADS)]
    IH = HEADS // 2
    ITEMS = 2 * BLOCKS
    item = lambda it: (*spans[it // 2], it // 2, (it % 2) * IH)
    turns = [IH * spans[it // 2][1] // 4 for it in range(ITEMS)]
    turns_before = [sum(turns[:it]) for it in range(ITEMS)]
    NTURN = sum(turns)
    rep = HEADS // KVH
    with ExitStack() as ctx:
        sem = lambda n: m.semaphore(f"att_{n}")
        sb = lambda n, s, t=F32: ctx.enter_context(nc.sbuf_tensor(n, s, t))
        qs = sb("qs", [P, HEADS // 2, SEQ])
        kd = sb("kd", [P, KVH, SEQ])
        vt = sb("vt", [P, 2, SEQ])
        v = sb("v", [P, BLOCKS, KVH * HD])
        s_sb = sb("s_sb", [P, 2, IH, 3 * P])
        pt = sb("pt", [P, IH * 3, P])
        o = sb("o", [P, 2, BANK])
        ot = sb("ot_sb", [P, 2, 4, P])
        st = sb("att_st", [P, 2, 6, IH])
        qk_landed, v_landed, s_done, s_read = sem("qk_landed"), sem("v_landed"), sem("s_done"), sem("s_read")
        stat, m_ready, p_ready, sink_e, den = sem("stat"), sem("m_ready"), sem("p_ready"), sem("sink_e"), sem("den")
        v_turned, v_ready, p_turned, pt_ready = sem("v_turned"), sem("v_ready"), sem("p_turned"), sem("pt_ready")
        o_done, o_ready, o_turned, ot_ready = sem("o_done"), sem("o_ready"), sem("o_turned"), sem("ot_ready")
        ot_stored = [sem(f"ot_stored{r}") for r in range(2)]
        block = ctx.enter_context(nc.Block())
        units = Units(m, GATE0)
        MAX, NMAX, SINK, ESINK, SUM, RSUM = range(6)

        @block.sync
        def _(sp):
            def load_weights(u):
                sp.wait_ge(m.w_lo_ready, GATE0 + u - 1)
                load_unit(sp, m, u % 2, d["w_all"][(GATE0 + u) * P:(GATE0 + u + 1) * P, :])

            def load_qk(s):
                rows = lambda tile, n: d["proj"][tile * P:(tile + n) * P, s * SEQ:(s + 1) * SEQ]
                sp.dma_start(qs[:], rows(Q0, 8).rearrange("(a p) t -> p a t", p=P)).then_inc(qk_landed, 16)
                for half in range(2):
                    sp.dma_start(kd[half * 64:(half + 1) * 64], rows(K0, 2).rearrange("(a p) t -> p a t", p=HD)).then_inc(qk_landed, 16)

            load_qk(0)
            for s in range(NSEQ):
                for r in range(2):
                    if s:
                        sp.wait_ge(ot_stored[r], s * (ITEMS * 8))
                sp.dma_start(vt[:], d["proj"][V0 * P:(V0 + 2) * P, s * SEQ:(s + 1) * SEQ]
                             .rearrange("(a p) t -> p a t", p=P)).then_inc(v_landed, 16)
                load_weights(s * ITEMS + 2)
                load_weights(s * ITEMS + 3)
                for it in range(ITEMS):
                    if it + 2 < ITEMS:
                        load_weights(s * ITEMS + it + 4)
                    if it == ITEMS - 1 and s + 1 < NSEQ:
                        sp.wait_ge(s_done, (s + 1) * (ITEMS * IH))
                        load_qk(s + 1)
                    b, half = divmod(it, 2)
                    sp.wait_ge(ot_ready, s * ITEMS + it + 1)
                    sp.dma_start(d["ot"].rearrange("(a p) t -> p a t", p=P)
                                 [:, 4 * half:4 * half + 4, s * SEQ + b * P:s * SEQ + (b + 1) * P],
                                 ot[:, it % 2]).then_inc(ot_stored[it % 2], 16)
            for r in range(2):
                sp.wait_ge(ot_stored[r], NSEQ * (ITEMS * 8))

        @block.tensor
        def _(pe):
            ident = m.con[:, CON_ID:CON_ID + P]
            with pe.Fori(0, NSEQ) as s:
                def project(j, n):
                    pr.half(pe, u_hi, u_lo, s * ITEMS + (GATE0 + j), j % 2, n)

                def scores(it):
                    k0, nk, _, b, h0 = item(it)
                    for i in range(IH):
                        n, h = it * IH + i, h0 + i
                        if n >= 2:
                            pe.wait_ge(s_read, s * (ITEMS * IH) + n - 1)
                        half = slice((h % 2) * 64, (h % 2) * 64 + 64)
                        pe.matmul(m.ps[:, 4 + n % 2, 0:nk * P], qs[half, h // 2, b * P:(b + 1) * P],
                                  kd[half, h // rep, k0 * P:(k0 + nk) * P], start=True, stop=True).then_inc(s_done, 1)

                pe.wait_ge(qk_landed, s * 48 + 48)
                scores(0)
                project(0, 0)
                project(0, 1)
                pe.wait_ge(v_landed, s * 16 + 16)
                for n in range(2):
                    for i in range(4):
                        kb, ft = divmod(4 * n + i, 2)
                        mm = pe.transpose(m.ps[:, 6 + n, i * P:(i + 1) * P], vt[:, ft, kb * P:(kb + 1) * P], ident)
                    mm.then_inc(v_turned, 1)
                for it in range(ITEMS):
                    k0, nk, _, b, h0 = item(it)
                    if it + 1 < ITEMS:
                        scores(it + 1)
                    if it == 0:
                        pe.wait_ge(v_ready, s * 2 + 2)
                    else:
                        pe.wait_ge(ot_ready, s * ITEMS + it)
                    for t in range(turns[it]):
                        last_head = (4 * t + 3) // nk
                        pe.wait_ge(p_ready, s * (ITEMS * IH) + (it * IH + last_head + 1))
                        n = turns_before[it] + t
                        if n >= 2:
                            pe.wait_ge(pt_ready, s * NTURN + (n - 1))
                        for i in range(4):
                            h, kb = divmod(4 * t + i, nk)
                            mm = pe.transpose(m.ps[:, 6 + n % 2, i * P:(i + 1) * P],
                                              s_sb[:, it % 2, h, kb * P:(kb + 1) * P], ident)
                        mm.then_inc(p_turned, 1)
                    if it + 1 < ITEMS:
                        project(it + 1, 0)
                    pe.wait_ge(pt_ready, s * NTURN + (turns_before[it] + turns[it]))
                    for h in range(IH):
                        g = (h0 + h) // rep
                        for kb in range(nk):
                            mm = pe.matmul(m.ps[:, 7, h * 64:(h + 1) * 64], pt[:, h * nk + kb],
                                           v[:, k0 + kb, g * HD:(g + 1) * HD], start=kb == 0, stop=kb == nk - 1)
                    mm.then_inc(o_done, 1)
                    if it + 1 < ITEMS:
                        project(it + 1, 1)
                    pe.wait_ge(o_ready, s * ITEMS + it + 1)
                    for i in range(4):
                        mm = pe.transpose(m.ps[:, 7, i * P:(i + 1) * P], o[:, it % 2, i * P:(i + 1) * P], ident)
                    mm.then_inc(o_turned, 1)

        @block.vector
        def _(dve):
            with dve.Fori(0, NSEQ) as s:
                def read_scores(it):
                    _, nk, c0, _, h0 = item(it)
                    if it >= 2:
                        dve.wait_ge(p_turned, s * NTURN + turns_before[it - 1])
                    for i in range(IH):
                        n = it * IH + i
                        dve.wait_ge(s_done, s * (ITEMS * IH) + n + 1)
                        dve.scalar_tensor_tensor(s_sb[:, it % 2, i, 0:nk * P],
                                                 m.con[:, CON_DIST + c0:CON_DIST + c0 + nk * P], -slopes[h0 + i],
                                                 m.ps[:, 4 + n % 2, 0:nk * P], ALU.mult, ALU.add).then_inc(s_read, 1)
                    t = st[:, it % 2]
                    sink = m.rows[:, R_SINK + h0:R_SINK + h0 + IH]
                    dve.wait_ge(s_read, s * (ITEMS * IH) + (it + 1) * IH)
                    dve.tensor_reduce(t[:, MAX], s_sb[:, it % 2, :, 0:nk * P], AX.X, ALU.max).then_inc(stat, 1)
                    dve.wait_ge(stat, s * (2 * ITEMS) + (2 * it + 1))
                    dve.tensor_tensor(t[:, MAX], t[:, MAX], sink, ALU.max).then_inc(stat, 1)
                    dve.wait_ge(stat, s * (2 * ITEMS) + (2 * it + 2))
                    dve.tensor_scalar(t[:, NMAX], t[:, MAX], -1.0, None, ALU.mult).then_inc(m_ready, 1)
                    dve.tensor_tensor(t[:, SINK], sink, t[:, MAX], ALU.subtract).then_inc(m_ready, 1)

                units.lo(dve, s * ITEMS, 0)
                read_scores(0)
                units.lo(dve, s * ITEMS + 1, 1)
                for n in range(2):
                    dve.wait_ge(v_turned, s * 2 + n + 1)
                    dve.tensor_copy(v[:, 2 * n:2 * n + 2].rearrange("p a b -> p (a b)"), m.ps[:, 6 + n]).then_inc(v_ready, 1)
                for it in range(ITEMS):
                    if it + 1 < ITEMS:
                        read_scores(it + 1)
                    if it + 2 < ITEMS:
                        units.lo(dve, s * ITEMS + (it + 2), it % 2)
                    t = st[:, it % 2]
                    dve.wait_ge(sink_e, s * ITEMS + it + 1)
                    dve.wait_ge(p_ready, s * (ITEMS * IH) + (it + 1) * IH)
                    dve.tensor_tensor(t[:, SUM], t[:, SUM], t[:, ESINK], ALU.add).then_inc(den, 1)
                    dve.wait_ge(den, s * (2 * ITEMS) + (2 * it + 1))
                    dve.reciprocal(t[:, RSUM], t[:, SUM]).then_inc(den, 1)
                    dve.wait_ge(den, s * (2 * ITEMS) + (2 * it + 2))
                    dve.wait_ge(o_done, s * ITEMS + it + 1)
                    if it >= 2:
                        dve.wait_ge(o_turned, s * ITEMS + it - 1)
                    dve.tensor_tensor(o[:, it % 2].rearrange("p (h w) -> p h w", h=IH),
                                      m.ps[:, 7].rearrange("p (h w) -> p h w", h=IH),
                                      bc(t[:, RSUM], HD), ALU.mult).then_inc(o_ready, 1)

        @block.scalar
        def _(act):
            with act.Fori(0, NSEQ) as s:
                def drain(j):
                    pr.evacuate(act, s * ITEMS + (GATE0 + j), j % 2, ACT.Sigmoid)

                def exponents(it):
                    nk = item(it)[1]
                    t = st[:, it % 2]
                    act.wait_ge(m_ready, s * (2 * ITEMS) + (2 * it + 2))
                    act.activation(t[:, ESINK], t[:, SINK], ACT.Exp).then_inc(sink_e, 1)
                    for i in range(IH):
                        p = s_sb[:, it % 2, i, 0:nk * P]
                        act.activation(p, p, ACT.Exp, bias=t[:, NMAX, i:i + 1],
                                       accum_out=t[:, SUM, i:i + 1]).then_inc(p_ready, 1)

                units.hi(act, s * ITEMS, 0)
                units.hi(act, s * ITEMS + 1, 1)
                exponents(0)
                for it in range(ITEMS):
                    if it:
                        act.wait_ge(o_done, s * ITEMS + it)
                    for i in range(turns[it]):
                        n = turns_before[it] + i
                        act.wait_ge(p_turned, s * NTURN + n + 1)
                        act.activation(pt[:, 4 * i:4 * i + 4].rearrange("p a b -> p (a b)"),
                                       m.ps[:, 6 + n % 2], ACT.Copy).then_inc(pt_ready, 1)
                    if it + 2 < ITEMS:
                        units.hi(act, s * ITEMS + (it + 2), it % 2)
                    drain(it)
                    if it + 1 < ITEMS:
                        exponents(it + 1)
                    act.wait_ge(o_turned, s * ITEMS + it + 1)
                    if it >= 2:
                        act.wait_ge(ot_stored[it % 2], s * (ITEMS * 8) + (it // 2) * 16)
                    act.activation(ot[:, it % 2], m.ps[:, 7].rearrange("p (a b) -> p a b", a=4),
                                   ACT.Copy).then_inc(ot_ready, 1)
            for r in range(2):
                act.wait_ge(pr.stored[r], NPROJ * 8)


def ssm_out_stage(m):
    nc, d = m.nc, m.dram
    NK = 2 * KT
    with ExitStack() as ctx:
        sem = lambda n: m.semaphore(f"wb_{n}")
        sb = lambda n, s, t=F32: ctx.enter_context(nc.sbuf_tensor(n, s, t))
        hi, lo = sb("y_hi", [P, NK, TOK], F32R), sb("y_lo", [P, NK, TOK], F32R)
        stage = sb("y_stage", [P, 2, TOK])
        rms = sb("y_rms", [P, TOK])
        NL = 4
        y_in = lambda k: m.resid[:, 4 + k % NL]
        sq = lambda k: m.resid[:, 2 + k % 2]
        landed = [sem(f"landed{r}") for r in range(NL)]
        gate_landed = [sem(f"gate_landed{r}") for r in range(2)]
        sq_summed = sem("sq_summed")
        hi_done, lo_done, sq_done, sq_used, mean, root, rms_ready = (sem(n) for n in (
            "hi_done", "lo_done", "sq_done", "sq_used", "mean", "root", "rms_ready"))
        scaled, gated = sem("scaled"), sem("gated")
        block = ctx.enter_context(nc.Block())
        units = Units(m, U_WB)
        both = lambda r: m.ps[:, 2 * r:2 * r + 2].rearrange("p a b -> p (a b)")

        @block.sync
        def _(sp):
            for k in range(NK):
                if k >= NL:
                    sp.wait_ge(lo_done, k - NL + 1)
                    sp.wait_ge(sq_done, k - NL + 1)
                sp.dma_start(y_in(k), d["yt"][k * P:(k + 1) * P, :]).then_inc(landed[k % NL], 16)
            for r in range(2):
                sp.dma_start(stage[:, r], d["proj"][(GATE0 + 8 + r) * P:(GATE0 + 9 + r) * P, :]).then_inc(gate_landed[r], 16)
            w = d["w_all"]

            def next_units(i, r):
                for s in range(2):
                    row = sp.snap(i * (4 * P) + (U_WB + 2 + 2 * r + s) * P)
                    sp.wait_ge(m.w_lo_ready, i * 4 + (U_WB + 1 + 2 * r + s))
                    load_unit(sp, m, s, w[bass.ds(row, P), :])
            with sp.Fori(0, KT // 2 - 1) as i:
                for r in range(2):
                    next_units(i, r)
                    row = sp.snap(i * (2 * P) + (GATE0 + 8 + 2 + r) * P)
                    sp.wait_ge(gated, i * 2 + r + 1)
                    sp.dma_start(stage[:, r], d["proj"][bass.ds(row, P), :]).then_inc(gate_landed[r], 16)
            with sp.Fori(KT // 2 - 1, KT // 2) as i:
                for r in range(2):
                    next_units(i, r)

        @block.scalar
        def _(act):
            units.hi(act, 0, 0, first=True)
            units.hi(act, 1, 1, first=True)
            for k in range(NK):
                act.wait_ge(landed[k % NL], 16 * (k // NL + 1))
                act.activation(hi[:, k], y_in(k), ACT.Copy, scale=m.gains[:, G_SSM + k:G_SSM + k + 1]).then_inc(hi_done, 1)
                if k >= 2:
                    act.wait_ge(sq_used, max(k - 2, 1))
                act.activation(sq(k), y_in(k), ACT.Square).then_inc(sq_done, 1)
            units.hi(act, 2, 0)
            units.hi(act, 3, 1)
            act.wait_ge(mean, 1)
            act.activation(rms[:], rms[:], ACT.Sqrt).then_inc(root, 1)
            with act.Fori(2, KT) as i:
                for r in range(2):
                    units.hi(act, i * 2 + r, r)

        @block.vector
        def _(dve):
            units.lo(dve, 0, 0)
            units.lo(dve, 1, 1)
            for k in range(NK):
                dve.wait_ge(hi_done, k + 1)
                dve.scalar_tensor_tensor(lo[:, k], y_in(k), m.gains[:, G_SSM + k:G_SSM + k + 1],
                                         hi[:, k].bitcast(F32), ALU.mult, ALU.subtract).then_inc(lo_done, 1)
            units.lo(dve, 2, 0)
            units.lo(dve, 3, 1)
            dve.wait_ge(sq_summed, 1)
            dve.tensor_scalar(rms[:], m.ps[:, 4:6].rearrange("p a b -> p (a b)"), 1.0 / (2 * D), EPS,
                              ALU.mult, ALU.add).then_inc(mean, 1)
            dve.wait_ge(root, 1)
            dve.reciprocal(rms[:], rms[:]).then_inc(rms_ready, 1)
            dve.wait_ge(rms_ready, 1)

            def finish(at, r):
                dst = m.resid[:, at] if isinstance(at, int) else m.resid[:, bass.ds(dve.snap(at), 1)].squeeze(1)
                dve.wait_ge(m.w_used, at * 2 + (U_WB + 2))
                dve.tensor_tensor(dst, both(r), rms[:], ALU.mult).then_inc(scaled, 1)
                dve.wait_ge(gate_landed[r], (at - r) * 8 + 16)
                dve.wait_ge(scaled, at + 1)
                dve.tensor_tensor(dst, dst, stage[:, r], ALU.mult).then_inc(gated, 1)

            finish(0, 0)
            units.lo(dve, 4, 0)
            units.lo(dve, 5, 1)
            finish(1, 1)
            with dve.Fori(1, KT // 2 - 1) as i:
                for r in range(2):
                    units.lo(dve, i * 4 + 2 * r + 2, 0)
                    units.lo(dve, i * 4 + 2 * r + 3, 1)
                    finish(i * 2 + r, r)
            units.lo(dve, 2 * KT - 2, 0)
            units.lo(dve, 2 * KT - 1, 1)
            finish(KT - 2, 0)
            finish(KT - 1, 1)

        @block.gpsimd
        def _(pool):
            for k in range(1, NK):
                pool.wait_ge(sq_done, k + 1)
                if k >= 2:
                    pool.wait_ge(sq_used, k - 1)
                pool.tensor_tensor(rms[:], sq(0) if k == 1 else rms[:], sq(k), ALU.add).then_inc(sq_used, 1)

        @block.tensor
        def _(pe):

            def tile(at, r, peel):
                for s in range(2):
                    units.wait(pe, at * 2 + s)
                    if s == 0 and not peel:
                        pe.wait_ge(scaled, at - 1)
                    for n in range(2):
                        c = slice(n * BANK, (n + 1) * BANK)
                        for k in range(KT):
                            if peel and r == 0 and n == 0:
                                pe.wait_ge(lo_done, s * KT + k + 1)
                            mm = products(pe, m.ps[:, 2 * r + n],
                                          [(wslice(m, s, k * P, (k + 1) * P), (hi[:, s * KT + k, c], lo[:, s * KT + k, c]))],
                                          first_of_group=s == 0 and k == 0, last_of_group=s == 1 and k == KT - 1)
                    mm.then_inc(m.w_used, 1)
                    if peel and r == 1 and s == 0:
                        pe.wait_ge(sq_used, NK - 1)
                        for n in range(2):
                            mm = pe.matmul(m.ps[:, 4 + n], m.con[:, CON_ONES:CON_ONES + P],
                                           rms[:, n * BANK:(n + 1) * BANK], start=True, stop=True)
                        mm.then_inc(sq_summed, 1)
            for r in range(2):
                tile(r, r, True)
            with pe.Fori(1, KT // 2) as i:
                for r in range(2):
                    tile(i * 2 + r, r, False)


def attention_out_stage(m, m_hi, m_lo):
    nc, d = m.nc, m.dram
    with ExitStack() as ctx:
        sem = lambda n: m.semaphore(f"wa_{n}")
        sb = lambda n, s, t=F32: ctx.enter_context(nc.sbuf_tensor(n, s, t))
        hi, lo = sb("o_hi", [P, KT, TOK], F32R), sb("o_lo", [P, KT, TOK], F32R)
        NL = 4
        stage = sb("o_stage", [P, NL, TOK])
        landed = [sem(f"landed{r}") for r in range(NL)]
        gate_landed = [sem(f"gate_landed{r}") for r in range(2)]
        hi_done, lo_done, gated, summed, m_hi_done, merged = (sem(n) for n in (
            "hi_done", "lo_done", "gated", "summed", "m_hi_done", "merged"))
        x_landed = sem("x_landed")
        block = ctx.enter_context(nc.Block())
        units = Units(m, U_WA)
        both = lambda r: m.ps[:, 2 * r:2 * r + 2].rearrange("p a b -> p (a b)")

        @block.sync
        def _(sp):
            for k in range(KT):
                if k >= NL:
                    sp.wait_ge(lo_done, k - NL + 1)
                sp.dma_start(stage[:, k % NL], d["ot"][k * P:(k + 1) * P, :]).then_inc(landed[k % NL], 16)
            sp.wait_ge(lo_done, KT)
            for r in range(2):
                sp.dma_start(stage[:, r], d["proj"][(GATE0 + r) * P:(GATE0 + r + 1) * P, :]).then_inc(gate_landed[r], 16)
            w = d["w_all"]
            with sp.Fori(0, KT // 2 - 1) as i:
                for r in range(2):
                    row = sp.snap(i * (2 * P) + (U_WA + 2 + r) * P)
                    g_row = sp.snap(i * (2 * P) + (GATE0 + 2 + r) * P)
                    sp.wait_ge(m.w_lo_ready, i * 2 + (U_WA + 1 + r))
                    load_unit(sp, m, r, w[bass.ds(row, P), :])
                    sp.wait_ge(merged, i * 2 + r + 1)
                    sp.dma_start(stage[:, r], d["proj"][bass.ds(g_row, P), :]).then_inc(gate_landed[r], 16)
            for r in range(2):
                sp.wait_ge(m.w_lo_ready, U_WA + KT - 1 + r)
                load_unit(sp, m, r, w[(U_WA + KT + r) * P:(U_WA + KT + r + 1) * P, :])
            for t in range(TT):
                sp.wait_ge(merged, t + 1)
                sp.dma_start(m.resid[:, t], d["x"][t * P:(t + 1) * P, :]).then_inc(x_landed, 16)
            sp.wait_ge(x_landed, TT * 16)

        @block.scalar
        def _(act):
            for r in range(2):
                units.hi(act, r, r, first=True)
            for k in range(KT):
                act.wait_ge(landed[k % NL], 16 * (k // NL + 1))
                act.activation(hi[:, k], stage[:, k % NL], ACT.Copy).then_inc(hi_done, 1)
            with act.Fori(1, KT // 2) as i:
                for r in range(2):
                    units.hi(act, i * 2 + r, r)

        @block.vector
        def _(dve):
            units.lo(dve, 0, 0)
            for k in range(KT):
                dve.wait_ge(hi_done, k + 1)
                dve.tensor_tensor(lo[:, k], stage[:, k % NL], hi[:, k].bitcast(F32), ALU.subtract).then_inc(lo_done, 1)

            def finish(at, r):
                one = (lambda t: t[:, at]) if isinstance(at, int) else (lambda t, j=dve.snap(at): t[:, bass.ds(j, 1)].squeeze(1))
                dve.wait_ge(m.w_used, at + (U_WA + 1))
                dve.wait_ge(gate_landed[r], (at - r) * 8 + 16)
                dve.tensor_tensor(stage[:, r], both(r), stage[:, r], ALU.mult).then_inc(gated, 1)
                dve.wait_ge(gated, at + 1)
                dve.tensor_tensor(one(m.resid), one(m.resid), stage[:, r], ALU.add).then_inc(summed, 1)
                dve.wait_ge(summed, at + 1)
                dve.tensor_scalar(one(m_hi), one(m.resid), 1.0, None, ALU.mult).then_inc(m_hi_done, 1)
                dve.wait_ge(m_hi_done, at + 1)
                dve.tensor_tensor(one(m_lo), one(m.resid), one(m_hi).bitcast(F32), ALU.subtract).then_inc(merged, 1)

            with dve.Fori(0, KT // 2 - 1) as i:
                units.lo(dve, i * 2 + 1, 1)
                finish(i * 2, 0)
                units.lo(dve, i * 2 + 2, 0)
                finish(i * 2 + 1, 1)
            units.lo(dve, KT - 1, 1)
            finish(KT - 2, 0)
            finish(KT - 1, 1)

        @block.tensor
        def _(pe):
            def tile(at, r, peel):
                units.wait(pe, at)
                if not peel:
                    pe.wait_ge(gated, at - 1)
                for n in range(2):
                    c = slice(n * BANK, (n + 1) * BANK)
                    for k in range(KT):
                        if peel and r == 0 and n == 0:
                            pe.wait_ge(lo_done, k + 1)
                        mm = products(pe, m.ps[:, 2 * r + n], [(wslice(m, r, k * P, (k + 1) * P), (hi[:, k, c], lo[:, k, c]))],
                                      first_of_group=k == 0, last_of_group=k == KT - 1)
                mm.then_inc(m.w_used, 1)
            for r in range(2):
                tile(r, r, True)
            with pe.Fori(1, KT // 2) as i:
                for r in range(2):
                    tile(i * 2 + r, r, False)


def residual_stage(m, name, first, hi, lo):
    nc, d = m.nc, m.dram
    n_units = KT
    with ExitStack() as ctx:
        sem = lambda n: m.semaphore(f"{name}_{n}")
        part_done, added = sem("part_done"), sem("added")
        block = ctx.enter_context(nc.Block())
        units = Units(m, first)

        @block.sync
        def _(sp):
            stream_weights(sp, m, first, n_units)

        @block.scalar
        def _(act):
            for r in range(2):
                units.hi(act, r, r, first=True)
            with act.Fori(1, n_units // 2) as i:
                for r in range(2):
                    units.hi(act, i * 2 + r, r)

        @block.vector
        def _(dve):
            units.lo(dve, 0, 0)

            def add(u):
                col = (u % 2) * BANK
                for g in range(4):
                    wait_part(dve, units, part_done, u, g)
                    dst = m.resid[:, 2 * g:2 * g + 2, col:col + BANK]
                    dve.tensor_tensor(dst, dst, m.ps[:, 2 * (g % 2):2 * (g % 2) + 2], ALU.add).then_inc(added, 1)
            for u in range(n_units):
                if u + 1 < n_units:
                    units.lo(dve, u + 1, (u + 1) % 2)
                add(u)

        @block.tensor
        def _(pe):
            for u in range(n_units):
                units.wait(pe, u)
                parts(pe, m, u % 2, part_done, hi, lo, 2 * (u // 2),
                      lambda g: pe.wait_ge(added, 4 * u + g - 1) if 4 * u + g >= 2 else None)


def wait_part(eng, units, part_done, u, g):
    if g < 3:
        eng.wait_ge(part_done, u * 3 + (g + 1))
    else:
        units.products_done(eng, u)


def parts(pe, m, r, part_done, hi, lo, kt, wait_bank):
    for g in range(4):
        wait_bank(g)
        for t in (2 * g, 2 * g + 1):
            s = slice(t * P, (t + 1) * P)
            mm = products(pe, m.ps[:, 2 * (g % 2) + t % 2],
                          [((hi[:, kt + i, s], lo[:, kt + i, s]), wslice(m, r, i * BANK, (i + 1) * BANK))
                           for i in range(2)])
        mm.then_inc(part_done if g < 3 else m.w_used, 1)


def memory_stage(m, mem_hi, mem_lo, k_t, v_c):
    nc, d = m.nc, m.dram
    with ExitStack() as ctx:
        sem = lambda n: m.semaphore(f"kv_{n}")
        k_read, v_read = sem("k_read"), sem("v_read")
        block = ctx.enter_context(nc.Block())
        units = Units(m, U_KV)

        @block.sync
        def _(sp):
            stream_weights(sp, m, U_KV, 16)

        @block.scalar
        def _(act):
            for r in range(2):
                units.hi(act, r, r, first=True)
            with act.Fori(1, KT) as i:
                for r in range(2):
                    units.hi(act, i * 2 + r, r)

        @block.vector
        def _(dve):
            units.lo(dve, 0, 0)
            with dve.Fori(0, KT // 2) as i:
                for r in range(2):
                    j = dve.snap(i * 2 + r)
                    units.lo(dve, i * 2 + (r + 1), 1 - r)
                    units.products_done(dve, i * 2 + r)
                    dve.tensor_scalar(k_t[:, bass.ds(j, 1)].squeeze(1), m.ps[:, r], 1.0, None, ALU.mult).then_inc(k_read, 1)
            for u in range(KT, 2 * KT):
                if u + 1 < 2 * KT:
                    units.lo(dve, u + 1, (u + 1) % 2)
                if u % 4 == 3:
                    n = (u - KT) // 4
                    units.products_done(dve, u)
                    for t in range(MT):
                        dve.tensor_copy(v_c[:, t, n * BANK:(n + 1) * BANK], m.ps[:, 4 + t]).then_inc(v_read, 1)

        @block.tensor
        def _(pe):
            def k_tile(at, r, peel):
                units.wait(pe, at)
                if not peel:
                    pe.wait_ge(k_read, at - 1)
                mm = products(pe, m.ps[:, r], [(wslice(m, r, k * P, (k + 1) * P), (mem_hi[:, k], mem_lo[:, k]))
                                               for k in range(KT)])
                mm.then_inc(m.w_used, 1)
            for r in range(2):
                k_tile(r, r, True)
            with pe.Fori(1, KT // 2) as i:
                for r in range(2):
                    k_tile(i * 2 + r, r, False)
            for u in range(KT, 2 * KT):
                n, kp = divmod(u - KT, 4)
                units.wait(pe, u)
                if u == KT + 4:
                    pe.wait_ge(v_read, MT)
                for t in range(MT):
                    s = slice(t * P, (t + 1) * P)
                    mm = products(pe, m.ps[:, 4 + t],
                                  [((mem_hi[:, 2 * kp + i, s], mem_lo[:, 2 * kp + i, s]),
                                    wslice(m, u % 2, i * BANK, (i + 1) * BANK)) for i in range(2)],
                                  first_of_group=kp == 0, last_of_group=kp == 3)
                mm.then_inc(m.w_used, 1)


def query_stage(m, u_hi, u_lo, q_t):
    nc, d = m.nc, m.dram
    with ExitStack() as ctx:
        drained = m.semaphore("q_drained")
        block = ctx.enter_context(nc.Block())
        units = Units(m, U_Q)

        @block.sync
        def _(sp):
            stream_weights(sp, m, U_Q, KT)

        @block.scalar
        def _(act):
            for r in range(2):
                units.hi(act, r, r, first=True)
            with act.Fori(1, KT // 2) as i:
                for r in range(2):
                    units.hi(act, i * 2 + r, r)

        @block.vector
        def _(dve):
            units.lo(dve, 0, 0)

            def finish(at, r):
                dst = q_t[:, at] if isinstance(at, int) else q_t[:, bass.ds(dve.snap(at), 1)].squeeze(1)
                units.products_done(dve, at)
                dve.tensor_scalar(dst, m.ps[:, 2 * r:2 * r + 2].rearrange("p a b -> p (a b)"), XHD ** -0.5, None,
                                  ALU.mult).then_inc(drained, 1)
            with dve.Fori(0, KT // 2 - 1) as i:
                units.lo(dve, i * 2 + 1, 1)
                finish(i * 2, 0)
                units.lo(dve, i * 2 + 2, 0)
                finish(i * 2 + 1, 1)
            units.lo(dve, KT - 1, 1)
            finish(KT - 2, 0)
            finish(KT - 1, 1)

        @block.tensor
        def _(pe):
            def tile(at, r, peel):
                units.wait(pe, at)
                if not peel:
                    pe.wait_ge(drained, at - 1)
                for n in range(2):
                    c = slice(n * BANK, (n + 1) * BANK)
                    mm = products(pe, m.ps[:, 2 * r + n],
                                  [(wslice(m, r, k * P, (k + 1) * P), (u_hi[:, k, c], u_lo[:, k, c])) for k in range(KT)])
                mm.then_inc(m.w_used, 1)
            for r in range(2):
                tile(r, r, True)
            with pe.Fori(1, KT // 2) as i:
                for r in range(2):
                    tile(i * 2 + r, r, False)


def cross_stage(m, q_t, k_t, v_c, o_hi, o_lo):
    nc = m.nc
    with ExitStack() as ctx:
        sem = lambda n: m.semaphore(f"cr_{n}")
        sb = lambda n, s, t=F32: ctx.enter_context(nc.sbuf_tensor(n, s, t))
        p = sb("cr_p", [P, 2, XH, MEM])
        pt = sb("cr_pt", [P, 2 * XH, P])
        st = sb("cr_st", [P, 2, 3, XH])
        s_done, neg_max, exp_done, inv, normed, p_turned, pt_ready, o_done, hi_done, lo_done = (sem(n) for n in (
            "s_done", "neg_max", "exp_done", "inv", "normed", "p_turned", "pt_ready", "o_done", "hi_done", "lo_done"))
        block = ctx.enter_context(nc.Block())
        scores = m.ps[:, 4:6].rearrange("p a (h k) -> p (a h) k", h=2)

        @block.tensor
        def _(pe):
            ident = m.con[:, CON_ID:CON_ID + P]

            def score(t):
                s = t // BLOCKS
                if t:
                    pe.wait_ge(exp_done, XH * t)
                for h in range(XH):
                    for i in range(2):
                        mm = pe.matmul(scores[:, h], q_t[:, 2 * h + i, t * P:(t + 1) * P],
                                       k_t[:, 2 * h + i, s * MEM:(s + 1) * MEM], start=i == 0, stop=i == 1)
                mm.then_inc(s_done, 1)
            score(0)
            for t in range(TT):
                s = t // BLOCKS
                if t + 1 < TT:
                    score(t + 1)
                for n in range(2):
                    pe.wait_ge(normed, XH * t + 2 * n + 2)
                    if t:
                        pe.wait_ge(pt_ready, 2 * (t - 1) + n + 1)
                    for i in range(4):
                        h, kb = divmod(4 * n + i, 2)
                        mm = pe.transpose(m.ps[:, 6 + n, i * P:(i + 1) * P], p[:, t % 2, h, kb * P:(kb + 1) * P], ident)
                    mm.then_inc(p_turned, 1)
                if t:
                    pe.wait_ge(lo_done, 2 * t)
                for n in range(2):
                    pe.wait_ge(pt_ready, 2 * t + n + 1)
                    for i in range(4):
                        f = 4 * n + i
                        h = f // 2
                        for kb in range(2):
                            mm = pe.matmul(m.ps[:, n, i * P:(i + 1) * P], v_c[:, 2 * s + kb, f * P:(f + 1) * P],
                                           pt[:, 2 * h + kb], start=kb == 0, stop=kb == 1)
                    mm.then_inc(o_done, 1)

        @block.vector
        def _(dve):
            def maxima(t):
                dve.wait_ge(s_done, t + 1)
                dve.tensor_reduce(st[:, t % 2, 0], scores, AX.X, ALU.max, negate=True).then_inc(neg_max, 1)

            maxima(0)
            for t in range(TT):
                if t + 1 < TT:
                    maxima(t + 1)
                dve.wait_ge(exp_done, XH * (t + 1))
                dve.reciprocal(st[:, t % 2, 2], st[:, t % 2, 1]).then_inc(inv, 1)
                dve.wait_ge(inv, t + 1)
                for h in range(XH):
                    dve.tensor_scalar(p[:, t % 2, h], p[:, t % 2, h], st[:, t % 2, 2, h:h + 1], None,
                                      ALU.mult).then_inc(normed, 1)
                for n in range(2):
                    dve.wait_ge(hi_done, 2 * t + n + 1)
                    dst = (slice(None), slice(4 * n, 4 * n + 4), slice(t * P, (t + 1) * P))
                    dve.tensor_tensor(o_lo[dst], m.ps[:, n].rearrange("p (a b) -> p a b", a=4),
                                      o_hi[dst].bitcast(F32), ALU.subtract).then_inc(lo_done, 1)

        @block.scalar
        def _(act):
            def exponents(t):
                act.wait_ge(neg_max, t + 1)
                if t >= 2:
                    act.wait_ge(p_turned, 2 * (t - 1))
                for h in range(XH):
                    act.activation(p[:, t % 2, h], scores[:, h], ACT.Exp, bias=st[:, t % 2, 0, h:h + 1],
                                   accum_out=st[:, t % 2, 1, h:h + 1]).then_inc(exp_done, 1)
            exponents(0)
            for t in range(TT):
                if t + 1 < TT:
                    exponents(t + 1)
                for n in range(2):
                    act.wait_ge(p_turned, 2 * t + n + 1)
                    if t:
                        act.wait_ge(o_done, 2 * t)
                    act.activation(pt[:, 4 * n:4 * n + 4].rearrange("p a b -> p (a b)"), m.ps[:, 6 + n],
                                   ACT.Copy).then_inc(pt_ready, 1)
                for n in range(2):
                    act.wait_ge(o_done, 2 * t + n + 1)
                    act.activation(o_hi[:, 4 * n:4 * n + 4, t * P:(t + 1) * P],
                                   m.ps[:, n].rearrange("p (a b) -> p a b", a=4), ACT.Copy).then_inc(hi_done, 1)


def ffn_stage(m, u_hi, u_lo):
    nc, d = m.nc, m.dram
    NC = HT // 2
    with ExitStack() as ctx:
        sem = lambda n: m.semaphore(f"ffn_{n}")
        sb = lambda n, s, t=F32: ctx.enter_context(nc.sbuf_tensor(n, s, t))
        g = sb("ffn_g", [P, 2, TOK])
        h_hi, h_lo = sb("h_hi", [P, 2, TOK], F32R), sb("h_lo", [P, 2, TOK], F32R)
        silu, prod, h_hi_done, h_ready, part_done, added = (sem(n) for n in (
            "silu", "prod", "h_hi_done", "h_ready", "part_done", "added"))
        block = ctx.enter_context(nc.Block())
        units = Units(m, U_FFN)
        both = lambda r: m.ps[:, 2 * r:2 * r + 2].rearrange("p a b -> p (a b)")
        at = lambda c, k: (c - 1) * 6 + (4 + k)

        @block.sync
        def _(sp):
            stream_weights(sp, m, U_FFN, 3 * HT)

        @block.scalar
        def _(act):
            def gate(u, c, r, first=False):
                if not first:
                    act.wait_ge(h_ready, c * 2 + (r - 1))
                units.products_done(act, u)
                act.activation(g[:, r], both(r), ACT.Silu).then_inc(silu, 1)

            def hidden(c, r):
                act.wait_ge(prod, c * 2 + (r + 1))
                act.activation(h_hi[:, r], g[:, r], ACT.Copy).then_inc(h_hi_done, 1)

            units.hi(act, 0, 0, first=True)
            units.hi(act, 1, 1, first=True)
            gate(0, 0, 0, True)
            units.hi(act, 2, 0)
            gate(1, 0, 1, True)
            units.hi(act, 3, 1)
            units.hi(act, 4, 0)
            hidden(0, 0)
            units.hi(act, 5, 1)
            hidden(0, 1)
            with act.Fori(1, NC) as c:
                gate(at(c, 0), c, 0)
                units.hi(act, at(c, 2), 0)
                gate(at(c, 1), c, 1)
                units.hi(act, at(c, 3), 1)
                units.hi(act, at(c, 4), 0)
                units.hi(act, at(c, 5), 1)
                units.hi(act, at(c, 6), 0)
                hidden(c, 0)
                units.hi(act, at(c, 7), 1)
                hidden(c, 1)

        @block.vector
        def _(dve):
            def up(u, c, r):
                dve.wait_ge(silu, c * 2 + (r + 1))
                units.products_done(dve, u)
                dve.tensor_tensor(g[:, r], both(r), g[:, r], ALU.mult).then_inc(prod, 1)

            def low(c, r):
                dve.wait_ge(h_hi_done, c * 2 + (r + 1))
                dve.tensor_tensor(h_lo[:, r], g[:, r], h_hi[:, r].bitcast(F32), ALU.subtract).then_inc(h_ready, 1)

            def down(u, d_at, n):
                for k in range(4):
                    if k < 3:
                        dve.wait_ge(part_done, d_at * 3 + (k + 1))
                    else:
                        units.products_done(dve, u)
                    dst = m.resid[:, 2 * k:2 * k + 2, n * BANK:(n + 1) * BANK]
                    dve.tensor_tensor(dst, dst, m.ps[:, 2 * (k % 2):2 * (k % 2) + 2], ALU.add).then_inc(added, 1)

            for u in range(4):
                units.lo(dve, u, u % 2)
            units.lo(dve, 4, 0)
            up(2, 0, 0)
            units.lo(dve, 5, 1)
            up(3, 0, 1)
            low(0, 0)
            low(0, 1)
            with dve.Fori(1, NC) as c:
                units.lo(dve, at(c, 2), 0)
                units.lo(dve, at(c, 3), 1)
                down(at(c, 2), c * 2 - 2, 0)
                units.lo(dve, at(c, 4), 0)
                down(at(c, 3), c * 2 - 1, 1)
                units.lo(dve, at(c, 5), 1)
                units.lo(dve, at(c, 6), 0)
                up(at(c, 4), c, 0)
                units.lo(dve, at(c, 7), 1)
                low(c, 0)
                up(at(c, 5), c, 1)
                low(c, 1)
            down(at(NC, 0), 2 * NC - 2, 0)
            down(at(NC, 1), 2 * NC - 1, 1)

        @block.tensor
        def _(pe):
            def tile(u, r):
                units.wait(pe, u)
                for n in range(2):
                    s = slice(n * BANK, (n + 1) * BANK)
                    mm = products(pe, m.ps[:, 2 * r + n],
                                  [(wslice(m, r, k * P, (k + 1) * P), (u_hi[:, k, s], u_lo[:, k, s])) for k in range(KT)])
                mm.then_inc(m.w_used, 1)

            def down(u, d_at, n, c):
                units.wait(pe, u)

                def bank_free(k):
                    if n == 0 and k < 2:
                        if k == 0:
                            pe.wait_ge(silu, c * 2 + 2)
                    else:
                        pe.wait_ge(added, d_at * 4 + (k - 1))
                parts(pe, m, n, part_done, h_hi, h_lo, 0, bank_free)

            tile(0, 0)
            tile(1, 1)
            pe.wait_ge(silu, 1)
            tile(2, 0)
            pe.wait_ge(silu, 2)
            tile(3, 1)
            with pe.Fori(1, NC) as c:
                pe.wait_ge(prod, c * 2 - 1)
                tile(at(c, 0), 0)
                pe.wait_ge(prod, c * 2)
                tile(at(c, 1), 1)
                pe.wait_ge(h_ready, c * 2)
                down(at(c, 2), c * 2 - 2, 0, c)
                down(at(c, 3), c * 2 - 1, 1, c)
                pe.wait_ge(added, c * 8 - 1)
                tile(at(c, 4), 0)
                pe.wait_ge(added, c * 8)
                tile(at(c, 5), 1)
            pe.wait_ge(h_ready, 2 * NC)
            pe.wait_ge(prod, 2 * NC)
            down(at(NC, 0), 2 * NC - 2, 0, NC - 1)
            down(at(NC, 1), 2 * NC - 1, 1, NC - 1)


def final_stage(m):
    nc, d = m.nc, m.dram
    with ExitStack() as ctx:
        sem = lambda n: m.semaphore(f"fin_{n}")
        sq = ctx.enter_context(nc.sbuf_tensor("fin_sq", [P, 2, D], F32))
        ss = ctx.enter_context(nc.sbuf_tensor("fin_ss", [P, 3, TT], F32))
        gain = ctx.enter_context(nc.sbuf_tensor("fin_gain", [P, D], F32))
        squared, mean, root, rstd, ready, stored, gain_landed = (sem(n) for n in (
            "squared", "mean", "root", "rstd", "ready", "stored", "gain_landed"))
        block = ctx.enter_context(nc.Block())

        @block.scalar
        def _(act):
            for t in range(TT):
                if t >= 2:
                    act.wait_ge(squared, t - 1)
                act.activation(sq[:, t % 2], m.resid[:, t], ACT.Square, accum_out=ss[:, 0, t:t + 1]).then_inc(squared, 1)
            act.wait_ge(mean, 1)
            act.activation(ss[:, 2], ss[:, 1], ACT.Sqrt).then_inc(root, 1)

        @block.vector
        def _(dve):
            dve.wait_ge(squared, TT)
            dve.tensor_scalar(ss[:, 1], ss[:, 0], 1.0 / D, EPS, ALU.mult, ALU.add).then_inc(mean, 1)
            dve.wait_ge(root, 1)
            dve.reciprocal(ss[:, 0], ss[:, 2]).then_inc(rstd, 1)
            dve.wait_ge(rstd, 1)
            dve.wait_ge(gain_landed, 16)
            for t in range(TT):
                dve.scalar_tensor_tensor(m.resid[:, t], m.resid[:, t], ss[:, 0, t:t + 1],
                                         gain[:], ALU.mult, ALU.mult).then_inc(ready, 1)

        @block.sync
        def _(sp):
            sp.dma_start(gain[:], d["g_final"].partition_broadcast(P)).then_inc(gain_landed, 16)
            for t in range(TT):
                sp.wait_ge(ready, t + 1)
                sp.dma_start(d["y"][t * P:(t + 1) * P, :], m.resid[:, t]).then_inc(stored, 16)
            sp.wait_ge(stored, 16 * TT)


def build(nc, dram):
    with ExitStack() as top:
        m = open_core(nc, top, dram)
        sb = lambda ctx, n, s, t=F32: ctx.enter_context(nc.sbuf_tensor(n, s, t))
        prep_stage(m)
        with ExitStack() as mix:
            u_hi, u_lo = sb(mix, "u_hi", [P, KT, TOK], F32R), sb(mix, "u_lo", [P, KT, TOK], F32R)
            norm_stage(m, "mix", dram["x"], G_MIX, u_hi, u_lo, TT, True)
            pr = Projection(m, mix)
            first_stage(m, pr, u_hi, u_lo)
            ssd_stage(m, pr, u_hi, u_lo)
            attention_stage(m, pr, u_hi, u_lo)
        m.resid = sb(top, "resid", [P, TT, D])
        ssm_out_stage(m)
        with ExitStack() as ctx:
            m_hi, m_lo = sb(ctx, "m_hi", [P, KT, TOK], F32R), sb(ctx, "m_lo", [P, KT, TOK], F32R)
            attention_out_stage(m, m_hi, m_lo)
            residual_stage(m, "out", U_OUT, m_hi, m_lo)
        m.recycle()
        with ExitStack() as ctx:
            k_t, v_c = sb(ctx, "k_t", [P, KT, NSEQ * MEM]), sb(ctx, "v_c", [P, MT, D])
            with ExitStack() as c2:
                mem_hi, mem_lo = (sb(c2, n, [P, KT, NSEQ * MEM], F32R) for n in ("mem_hi", "mem_lo"))
                norm_stage(m, "mem", dram["mem"], G_MEM, mem_hi, mem_lo, MT, True)
                memory_stage(m, mem_hi, mem_lo, k_t, v_c)
            c_hi, c_lo = sb(ctx, "c_hi", [P, KT, TOK], F32R), sb(ctx, "c_lo", [P, KT, TOK], F32R)
            norm_stage(m, "crs", m.resid, G_CROSS, c_hi, c_lo, TT, False)
            q_t = sb(ctx, "q_t", [P, KT, TOK])
            query_stage(m, c_hi, c_lo, q_t)
            cross_stage(m, q_t, k_t, v_c, c_hi, c_lo)
            residual_stage(m, "wo", U_O, c_hi, c_lo)
        with ExitStack() as ctx:
            f_hi, f_lo = sb(ctx, "f_hi", [P, KT, TOK], F32R), sb(ctx, "f_lo", [P, KT, TOK], F32R)
            norm_stage(m, "ffn", m.resid, G_FFN, f_hi, f_lo, TT, False)
            ffn_stage(m, f_hi, f_lo)
        final_stage(m)



def tiles_a(w):
    k, n = w.shape
    return w.reshape(KT, P, n // P, P).transpose(2, 1, 0, 3).reshape(-1, 1024)


def tiles_b(w):
    k, n = w.shape
    return w.reshape(k // (2 * P), 2, P, n // BANK, BANK).transpose(0, 3, 2, 1, 4).reshape(-1, 1024)


def lay_out(i):
    a = {k: np.asarray(v) for k, v in i.items()}
    w = a["w_in"][0]
    c = 1536
    z, xbc, dtw, gates = w[:, c:c + 2048], w[:, c + 2048:c + 5120], w[:, c + 5120:c + 5184], w[:, c + 5184:]
    chans = np.concatenate([np.r_[g * GW:(g + 1) * GW, 2048 + g * P:2048 + (g + 1) * P, 2560 + g * P:2560 + (g + 1) * P]
                            for g in range(GROUPS)])
    kv = a["w_kv_cross"][0]
    v_units = kv[:, 1024:].reshape(4, 2, P, 2, BANK).transpose(3, 0, 2, 1, 4).reshape(-1, 1024)
    gu = a["w_gate_up"][0]
    gate, up = (tiles_a(gu[:, s:s + HID]).reshape(HT // 2, 2 * P, 1024) for s in (0, HID))
    down = tiles_b(a["w_down"][0]).reshape(HT // 2, 2 * P, 1024)
    ffn = [gate[0], up[0]]
    for k in range(1, HT // 2):
        ffn += [gate[k], down[k - 1], up[k]]
    ffn.append(down[-1])
    wb = a["w_br_ssm"][0].reshape(2, KT, P, KT, P).transpose(3, 0, 2, 1, 4).reshape(-1, 1024)
    groups = [tiles_a(np.concatenate([z[:, g * GW:(g + 1) * GW], xbc[:, chans[g * CT * P:(g + 1) * CT * P]]], axis=1))
              for g in range(GROUPS)]
    w_all = np.concatenate([tiles_a(w[:, 1280:1536]), *groups, tiles_a(w[:, :1280]), tiles_a(gates), wb,
                            tiles_a(a["w_br_attn"][0]), tiles_b(a["w_out"][0]), tiles_a(kv[:, :1024]), v_units,
                            tiles_a(a["w_q_cross"][0]), tiles_b(a["w_o_cross"][0]), *ffn])
    taps = np.concatenate([a["conv_w"][0], a["conv_b"][0][None]])[:, chans]
    taps = taps.reshape(TAPS + 1, GROUPS, CT, P).transpose(1, 3, 2, 0).reshape(GROUPS * P, CT * (TAPS + 1))
    col = lambda n: a[n].reshape(-1, P).T
    return {
        "x": np.concatenate([a["x_prompt"][0], a["x_sample"][0]]),
        "mem": np.concatenate([a["mem_prompt"][0], a["mem_sample"][0]]),
        "w_all": w_all,
        "w_dt": dtw.reshape(KT, P, 64).transpose(1, 0, 2).reshape(P, KT * 64),
        "taps": taps,
        "gains": np.concatenate([col(n) for n in ("norm_mix", "norm_cross", "norm_mem", "norm_ffn", "ssm_norm")], axis=1),
        "rows": np.concatenate([a["a_log"].ravel(), a["dt_bias"].ravel(), a["d_skip"].ravel(), a["attn_sink"].ravel()]),
        "g_final": a["norm_final"].ravel(),
        "con": constants(),
    }


def kernel(**inputs):
    import concourse.bacc as bacc
    from concourse.bass_utils import run_bass_kernel_spmd

    arrays = {k: np.ascontiguousarray(v) for k, v in lay_out(inputs).items()}
    nc = bacc.Bacc("TRN2", target_bir_lowering=False, num_devices=1)
    dram = {k: nc.dram_tensor(f"{k}_dram", v.shape, F32, kind="ExternalInput").ap() for k, v in arrays.items()}
    for name, tiles in (("proj", NPROJ), ("yt", 2 * KT), ("ot", KT)):
        dram[name] = nc.dram_tensor(f"{name}_dram", [tiles * P, TOK], F32, kind="Internal").ap()
    dram["steps"] = nc.dram_tensor("steps_dram", [GROUPS * P, STEPW], F32, kind="Internal").ap()
    dram["sums"] = nc.dram_tensor("sums_dram", [GROUPS * TT * 2, 2 * BANK], F32, kind="Internal").ap()
    dram["y"] = nc.dram_tensor("y_dram", [TOK, D], F32, kind="ExternalOutput").ap()
    build(nc, dram)
    y = run_bass_kernel_spmd(nc, [{f"{k}_dram": v for k, v in arrays.items()}], core_ids=[0]).results[0]["y_dram"]
    return y[:SEQ][None], y[SEQ:][None]
```

```python
from contextlib import ExitStack

import numpy as np
import concourse.bass as bass
from concourse import mybir

F32 = mybir.dt.float32
F32R = mybir.dt.float32r
ACT = mybir.ActivationFunctionType
ALU = mybir.AluOpType
AX = mybir.AxisListType

P = 128
NSEQ = 2
SEQ = 512
TOK = NSEQ * SEQ
TT = TOK // P
D = 1024
KT = D // P
EPS = 1e-6
HEADS, KVH, HD = 16, 4, 64
BLOCKS = SEQ // P
GROUPS, GH, NSTATE = 4, 8, 128
SSMH = GROUPS * GH
GW = GH * 64
XT = GW // P
CT = XT + 2
TAPS = 5
HALO = TAPS // 2
MEM = 256
MT = NSEQ * MEM // P
XHD = 256
XH = D // XHD
HID = 2816
HT = HID // P
FAR = 1e35
BANK = 512

GT = XT + CT
V0, GRP0 = 0, 2
Q0 = GRP0 + GROUPS * GT
K0 = Q0 + 8
GATE0 = K0 + 2
NPROJ = GATE0 + 16
STEPW = 5 * TT * 2 * GH + GH

U_PROJ = 0
U_WB = U_PROJ + NPROJ
U_WA = U_WB + 16
U_OUT = U_WA + 8
U_KV = U_OUT + 8
U_Q = U_KV + 16
U_O = U_Q + 8
U_FFN = U_O + 8
NUNITS = U_FFN + 3 * HT

CON_ID, CON_ONES, CON_UP, CON_LOW = 0, 128, 256, 384
CON_DIST = 512
NCON = CON_DIST + 3 * P
G_MIX, G_CROSS, G_MEM, G_FFN, G_SSM = 0, 8, 16, 24, 32
NG = 48
R_ALOG, R_DTB, R_SKIP, R_SINK = 0, 64, 128, 160
NR = R_SINK + HEADS


def constants():
    i = np.arange(P)
    c = np.zeros((P, NCON), np.float32)
    c[:, CON_ID:CON_ID + P] = np.eye(P)
    c[:, CON_ONES:CON_ONES + P] = 1.0
    c[:, CON_UP:CON_UP + P] = i[:, None] <= i[None, :]
    c[:, CON_LOW:CON_LOW + P] = i[:, None] >= i[None, :]
    k = np.arange(3 * P) - P
    dist = np.abs(i[:, None] - k[None, :]).astype(np.float32)
    c[:, CON_DIST:] = np.where(dist <= 128, dist, FAR)
    return c


class Core:

    def semaphore(self, name):
        self.stage_sems.append(self.nc.alloc_semaphore(name=name))
        return self.stage_sems[-1]

    def recycle(self):
        self.nc.clear_and_free_semaphores(self.stage_sems)
        self.stage_sems = []
        self.nc.all_engine_barrier()


def open_core(nc, ctx, dram):
    m = Core()
    m.nc, m.dram, m.stage_sems = nc, dram, []

    def sb(name, shape, dt=F32):
        return ctx.enter_context(nc.sbuf_tensor(name, shape, dt))

    m.con = sb("con", [P, NCON])
    m.gains = sb("gains", [P, NG])
    m.rows = sb("rows", [P, NR])
    m.w_raw = sb("w_raw", [P, 2, 1024])
    m.w_hi = sb("w_hi", [P, 2, 1024], F32R)
    m.w_lo = sb("w_lo", [P, 2, 1024], F32R)
    m.ps = ctx.enter_context(nc.psum_tensor("ps", [P, 8, BANK], F32))
    m.w_landed = [nc.alloc_semaphore(name=f"w_landed{r}") for r in range(2)]
    m.w_hi_ready = nc.alloc_semaphore(name="w_hi_ready")
    m.w_lo_ready = nc.alloc_semaphore(name="w_lo_ready")
    m.w_used = nc.alloc_semaphore(name="w_used")
    return m



def load_unit(sp, m, r, rows):
    sp.dma_start(m.w_raw[:, r], rows).then_inc(m.w_landed[r], 16)


def stream_weights(sp, m, first, n):
    end = min(first + n + 2, NUNITS)
    pairs = (end - first - 2) // 2
    if pairs <= 0:
        return
    w = m.dram["w_all"]
    with sp.Fori(0, pairs) as i:
        for r in range(2):
            row = sp.snap(i * (2 * P) + (first + 2 + r) * P)
            sp.wait_ge(m.w_lo_ready, i * 2 + (first + 1 + r))
            load_unit(sp, m, r, w[bass.ds(row, P), :])


def split_hi(act, m, r, landed, used):
    act.wait_ge(m.w_landed[r], landed)
    if used is not None:
        act.wait_ge(m.w_used, used)
    act.activation(m.w_hi[:, r], m.w_raw[:, r], ACT.Copy).then_inc(m.w_hi_ready, 1)


def split_lo(dve, m, r, hi_ready):
    dve.wait_ge(m.w_hi_ready, hi_ready)
    dve.tensor_tensor(m.w_lo[:, r], m.w_raw[:, r], m.w_hi[:, r].bitcast(F32),
                      ALU.subtract).then_inc(m.w_lo_ready, 1)


class Units:

    def __init__(self, m, first):
        self.m, self.first = m, first

    def hi(self, act, at, r, first=False):
        u = self.first + at
        split_hi(act, self.m, r, ring_landed(self.first, at, r), None if first else u - 1)

    def lo(self, dve, at, r):
        split_lo(dve, self.m, r, self.first + at + 1)

    def products_done(self, eng, at):
        eng.wait_ge(self.m.w_used, self.first + at + 1)

    def wait(self, pe, at):
        pe.wait_ge(self.m.w_lo_ready, self.first + at + 1)


def ring_landed(first, at, r):
    return (at - r) * 8 + (first // 2 + 1) * 16


def products(pe, out, pairs, last_of_group=True, first_of_group=True):
    n = len(pairs)
    for k, ((l_hi, l_lo), (r_hi, r_lo)) in enumerate(pairs):
        for q, (a, b) in enumerate(((l_hi, r_hi), (l_hi, r_lo), (l_lo, r_hi))):
            mm = pe.matmul(out, a, b, start=first_of_group and k == 0 and q == 0,
                           stop=last_of_group and k == n - 1 and q == 2)
    return mm


def wslice(m, r, a, b):
    return m.w_hi[:, r, a:b], m.w_lo[:, r, a:b]



def norm_stage(m, name, source, gain, hi, lo, tiles, source_is_dram, first_stage=False, xn=None):
    nc = m.nc
    wide = tiles // 4
    with ExitStack() as ctx:
        sem = lambda n: m.semaphore(f"{name}_{n}")
        x = ctx.enter_context(nc.sbuf_tensor(f"{name}_x", [P, tiles, D], F32)) if source_is_dram else source
        if xn is None:
            xn = ctx.enter_context(nc.sbuf_tensor(f"{name}_xn", [P, tiles, D], F32))
        ss = ctx.enter_context(nc.sbuf_tensor(f"{name}_ss", [P, 3, tiles], F32))
        landed = [sem(f"landed{t}") for t in range(tiles)] if source_is_dram else []
        squared, mean, root, rstd, scaled = sem("squared"), sem("mean"), sem("root"), sem("rstd"), sem("scaled")
        turned, hi_done, lo_done = sem("turned"), sem("hi_done"), sem("lo_done")
        block = ctx.enter_context(nc.Block())
        groups = [(n, j) for n in range(wide) for j in range(KT)]
        units = Units(m, 0)
        if first_stage:
            con_landed, gains_landed, rest_landed = sem("con_landed"), sem("gains_landed"), sem("rest_landed")

        def in_order(statistics, split):
            for n in range(wide):
                statistics(n)
                if source_is_dram:
                    split(n)
            if not source_is_dram:
                for n in range(wide):
                    split(n)

        if source_is_dram:
            @block.sync
            def _(sp):
                for t in range(tiles):
                    sp.dma_start(x[:, t], source[t * P:(t + 1) * P, :]).then_inc(landed[t], 16)
                    if first_stage and t == 1:
                        sp.dma_start(m.con[:], m.dram["con"]).then_inc(con_landed, 16)
                        sp.dma_start(m.gains[:], m.dram["gains"]).then_inc(gains_landed, 16)
                    if first_stage and t % 4 == 3:
                        load_unit(sp, m, t // 4, m.dram["w_all"][t // 4 * P:(t // 4 + 1) * P, :])

                if first_stage:
                    sp.dma_start(m.rows[:], m.dram["rows"].partition_broadcast(P)).then_inc(rest_landed, 16)
                    sp.dma_start(m.w_dt[:], m.dram["w_dt"]).then_inc(rest_landed, 16)
                    sp.wait_ge(rest_landed, 32)

        @block.scalar
        def _(act):
            def statistics(n):
                for t in range(4 * n, 4 * n + 4):
                    if source_is_dram:
                        act.wait_ge(landed[t], 16)
                    act.activation(xn[:, t], x[:, t], ACT.Square, accum_out=ss[:, 0, t:t + 1]).then_inc(squared, 1)
                act.wait_ge(mean, n + 1)
                act.activation(ss[:, 2, 4 * n:4 * n + 4], ss[:, 1, 4 * n:4 * n + 4], ACT.Sqrt).then_inc(root, 1)

            def split(n):
                if first_stage and n == 0:
                    act.wait_ge(gains_landed, 16)
                for j in range(KT):
                    i = n * KT + j
                    act.wait_ge(turned, i + 1)
                    act.activation(hi[:, j, n * BANK:(n + 1) * BANK], m.ps[:, 4 + i % 4], ACT.Copy,
                                   scale=m.gains[:, gain + j:gain + j + 1]).then_inc(hi_done, 1)

            in_order(statistics, split)
            if first_stage:
                units.hi(act, 0, 0, first=True)

        @block.vector
        def _(dve):
            def statistics(n):
                four = slice(4 * n, 4 * n + 4)
                dve.wait_ge(squared, 4 * n + 4)
                dve.tensor_scalar(ss[:, 1, four], ss[:, 0, four], 1.0 / D, EPS, ALU.mult, ALU.add).then_inc(mean, 1)
                dve.wait_ge(root, n + 1)
                dve.reciprocal(ss[:, 0, four], ss[:, 2, four]).then_inc(rstd, 1)
                dve.wait_ge(rstd, n + 1)
                for t in range(4 * n, 4 * n + 4):
                    dve.tensor_scalar(xn[:, t], x[:, t], ss[:, 0, t:t + 1], None, ALU.mult).then_inc(scaled, 1)

            def split(n):
                for j in range(KT):
                    i = n * KT + j
                    dve.wait_ge(hi_done, i + 1)
                    dve.scalar_tensor_tensor(lo[:, j, n * BANK:(n + 1) * BANK], m.ps[:, 4 + i % 4],
                                             m.gains[:, gain + j:gain + j + 1],
                                             hi[:, j, n * BANK:(n + 1) * BANK].bitcast(F32),
                                             ALU.mult, ALU.subtract).then_inc(lo_done, 1)

            in_order(statistics, split)
            if first_stage:
                units.lo(dve, 0, 0)

        @block.tensor
        def _(pe):
            ident = m.con[:, CON_ID:CON_ID + P]
            if first_stage:
                pe.wait_ge(con_landed, 16)
            for i, (n, j) in enumerate(groups):
                if j == 0:
                    pe.wait_ge(scaled, 4 * (n + 1))
                if i >= 4:
                    pe.wait_ge(lo_done, i - 3)
                for t in range(4):
                    mm = pe.transpose(m.ps[:, 4 + i % 4, t * P:(t + 1) * P],
                                      xn[:, 4 * n + t, j * P:(j + 1) * P], ident)
                mm.then_inc(turned, 1)


class Projection:

    def __init__(self, m, ctx):
        self.m = m
        self.out = ctx.enter_context(m.nc.sbuf_tensor("proj_out", [P, 2, TOK], F32))
        self.drained = m.nc.alloc_semaphore(name="proj_drained")
        self.stored = [m.nc.alloc_semaphore(name=f"proj_stored{r}") for r in range(2)]

    def evacuate(self, act, at, r, func, scale=1.0, peel=False):
        row = at * P if isinstance(at, int) else act.snap(at * P)
        if not peel:
            act.wait_ge(self.stored[r], (at - r) * 8)
        act.wait_ge(self.m.w_used, at + 1)
        act.activation(self.out[:, r], self.m.ps[:, 2 * r:2 * r + 2].rearrange("p a b -> p (a b)"), func,
                       scale=scale).then_inc(self.drained, 1)
        act.wait_ge(self.drained, at + 1)
        act.dma_start(self.m.dram["proj"][bass.ds(row, P), :], self.out[:, r]).then_inc(self.stored[r], 16)

    def half(self, pe, u_hi, u_lo, at, r, n, peel=False):
        m = self.m
        if n == 0:
            pe.wait_ge(m.w_lo_ready, at + 1)
            if not peel:
                pe.wait_ge(self.drained, at - 1)
        s = slice(n * BANK, (n + 1) * BANK)
        mm = products(pe, m.ps[:, 2 * r + n],
                      [(wslice(m, r, k * P, (k + 1) * P), (u_hi[:, k, s], u_lo[:, k, s])) for k in range(KT)])
        if n == 1:
            mm.then_inc(m.w_used, 1)


def first_stage(m, pr, u_hi, u_lo):
    nc, d = m.nc, m.dram
    with ExitStack() as ctx:
        sem = lambda n: m.semaphore(f"step_{n}")
        w_dt = m.w_dt
        w_dt_hi = ctx.enter_context(nc.sbuf_tensor("w_dt_hi", [P, KT * 64], F32R))
        w_dt_lo = ctx.enter_context(nc.sbuf_tensor("w_dt_lo", [P, KT * 64], F32R))
        dt_hi, dt_lo, dt_done = sem("dt_hi"), sem("dt_lo"), sem("dt_done")
        units = Units(m, U_PROJ)
        N = GRP0 + GT
        tmp = [ctx.enter_context(nc.sbuf_tensor(f"step_t{i}", [P, TT, 64], F32)) for i in range(4)]
        sums, dt, exp_a, w_in, dec = (ctx.enter_context(nc.sbuf_tensor(f"step_{n}", [P, TT, 64], F32))
                                      for n in ("sums", "dt", "exp_a", "w_in", "dec"))
        rows = ctx.enter_context(nc.sbuf_tensor("sum_rows", [64, TOK], F32))
        by_group = ctx.enter_context(nc.sbuf_tensor("by_group", [P, GROUPS, STEPW], F32))
        neg_a = ctx.enter_context(nc.sbuf_tensor("neg_a", [P, 64], F32))
        dve_step, act_step, pe_step = sem("dve"), sem("act"), sem("pe")
        rows_ready, grouped, stored = sem("rows_ready"), sem("grouped"), sem("stored")
        block = ctx.enter_context(nc.Block())
        flat = lambda ap: ap.rearrange("p a b -> p (a b)")
        bias = m.rows[:, R_DTB:R_DTB + 64].unsqueeze(1).to_broadcast([P, TT, 64])
        TERMS = 9

        n_dve = 0

        @block.vector
        def _(dve):
            nonlocal n_dve
            count = [0]

            def chain(ins):
                count[0] += 1
                ins.then_inc(dve_step, 1)
                dve.wait_ge(dve_step, count[0])

            dve.wait_ge(dt_hi, 1)
            dve.tensor_tensor(w_dt_lo[:], w_dt[:], w_dt_hi[:].bitcast(F32), ALU.subtract).then_inc(dt_lo, 1)
            units.lo(dve, 1, 1)
            units.lo(dve, 2, 0)
            x, mag, z, z2 = tmp
            dve.wait_ge(dt_done, 1)
            chain(dve.tensor_tensor(x[:], m.ps[:, 7].rearrange("p (a b) -> p a b", a=TT), bias, ALU.add))
            chain(dve.tensor_scalar(mag[:], x[:], -1.0, None, ALU.mult))
            chain(dve.tensor_tensor(mag[:], mag[:], x[:], ALU.min))
            dve.wait_ge(act_step, 1)
            chain(dve.tensor_scalar(z[:], mag[:], 2.0, None, ALU.add))
            chain(dve.reciprocal(z[:], z[:]))
            chain(dve.tensor_tensor(z[:], z[:], mag[:], ALU.mult))
            chain(dve.tensor_tensor(z2[:], z[:], z[:], ALU.mult))
            chain(dve.tensor_scalar(mag[:], z2[:], 2.0 / (2 * TERMS - 1), 2.0 / (2 * TERMS - 3), ALU.mult, ALU.add))
            for t in range(TERMS - 3, -1, -1):
                chain(dve.tensor_tensor(mag[:], mag[:], z2[:], ALU.mult))
                chain(dve.tensor_scalar(mag[:], mag[:], 2.0 / (2 * t + 1), None, ALU.add))
            chain(dve.tensor_tensor(mag[:], mag[:], z[:], ALU.mult))
            chain(dve.scalar_tensor_tensor(dt[:], x[:], 0.0, mag[:], ALU.max, ALU.add))
            dve.wait_ge(act_step, 2)
            chain(dve.tensor_scalar(neg_a[:], neg_a[:], -1.0, None, ALU.mult))
            dta = tmp[0]
            chain(dve.tensor_tensor(dta[:], dt[:], neg_a[:].unsqueeze(1).to_broadcast([P, TT, 64]), ALU.mult))
            n_dve = count[0]
            units.lo(dve, 3, 1)
            dve.wait_ge(pe_step, 1)
            for way in range(2):
                src = m.ps[:, 4 + way, 0:TT * 32].rearrange("p (a b) -> p a b", a=TT)
                chain(dve.tensor_copy(sums[:, :, way * 32:way * 32 + 32], src))
            dve.wait_ge(pe_step, 2)
            tot = m.ps[:, 6].rearrange("p (a b) -> p a b", a=TT)
            chain(dve.tensor_tensor(tmp[1][:], tot, sums[:], ALU.subtract))
            dve.wait_ge(act_step, 5)
            chain(dve.tensor_tensor(w_in[:], tmp[2][:], dt[:], ALU.mult))
            units.lo(dve, 4, 0)
            dve.wait_ge(pe_step, 3)
            dve.tensor_copy(rows[:], m.ps[0:64, 4:6].rearrange("p a b -> p (a b)")).then_inc(rows_ready, 1)
            for g in range(GROUPS):
                for i, src in enumerate((sums, dt, exp_a, w_in, dec)):
                    dve.tensor_copy(by_group[:, g, i * 2 * GH * TT:(i + 1) * 2 * GH * TT]
                                    .rearrange("p (c w h) -> p c w h", c=TT, w=2),
                                    src[:].rearrange("p c (w h) -> p c w h", w=2)[:, :, :, g * GH:(g + 1) * GH]
                                    ).then_inc(grouped, 1)
                dve.tensor_copy(by_group[:, g, STEPW - GH:], m.rows[:, R_SKIP + g * GH:R_SKIP + (g + 1) * GH]
                                ).then_inc(grouped, 1)
                units.lo(dve, 5 + g, (5 + g) % 2)
            for u in range(5 + GROUPS, N + 1):
                units.lo(dve, u, u % 2)

        @block.sync
        def _(sp):
            def load_weights(u):
                sp.wait_ge(m.w_lo_ready, u - 1)
                load_unit(sp, m, u % 2, d["w_all"][u * P:(u + 1) * P, :])

            for u in range(2, 7):
                load_weights(u)
            sp.wait_ge(rows_ready, 1)
            dst = d["sums"].rearrange("(g c f) (w i t) -> g f w i c t", g=GROUPS, c=TT, w=2, i=4)
            n = 0
            for g in range(GROUPS):
                for f in range(2):
                    for way in range(2):
                        p0 = way * 32 + g * GH + f * 4
                        sp.dma_start(dst[g, f, way], rows[p0:p0 + 4].rearrange("p (c t) -> p c t", c=TT)
                                     ).then_inc(stored, 16)
                        n += 1
            for g in range(GROUPS):
                load_weights(7 + g)
                sp.wait_ge(grouped, 6 * (g + 1))
                sp.dma_start(d["steps"][g * P:(g + 1) * P, :], by_group[:, g]).then_inc(stored, 16)
            for u in range(7 + GROUPS, N + 2):
                load_weights(u)
            sp.wait_ge(stored, 16 * (n + GROUPS))

        @block.scalar
        def _(act):
            def service(j):
                if j + 1 <= N:
                    units.hi(act, j + 1, (j + 1) % 2, first=j == 0)
                if j:
                    tile = j - 1
                    pr.evacuate(act, tile, tile % 2, ACT.Silu if GRP0 <= tile < GRP0 + XT else ACT.Copy, peel=tile < 2)

            act.activation(w_dt_hi[:], w_dt[:], ACT.Copy).then_inc(dt_hi, 1)
            service(0)
            service(1)
            act.wait_ge(dve_step, 3)
            act.activation(tmp[1][:], tmp[1][:], ACT.Exp).then_inc(act_step, 1)
            act.activation(neg_a[:], m.rows[:, R_ALOG:R_ALOG + 64], ACT.Exp).then_inc(act_step, 1)
            service(2)
            act.wait_ge(dve_step, n_dve + 2)
            act.activation(exp_a[:], sums[:], ACT.Exp).then_inc(act_step, 1)
            act.wait_ge(dve_step, n_dve + 3)
            act.activation(dec[:], m.ps[:, 6].rearrange("p (a b) -> p a b", a=TT), ACT.Exp).then_inc(act_step, 1)
            act.activation(tmp[2][:], tmp[1][:], ACT.Exp).then_inc(act_step, 1)
            for j in range(3, N + 1):
                service(j)

        @block.tensor
        def _(pe):
            def project(u):
                for n in range(2):
                    pr.half(pe, u_hi, u_lo, u, u % 2, n, peel=u < 2)

            project(0)
            pe.wait_ge(dt_lo, 1)
            for t in range(TT):
                s = slice(t * P, (t + 1) * P)
                mm = products(pe, m.ps[:, 7, t * 64:(t + 1) * 64],
                              [((u_hi[:, k, s], u_lo[:, k, s]),
                                (w_dt_hi[:, k * 64:(k + 1) * 64], w_dt_lo[:, k * 64:(k + 1) * 64])) for k in range(KT)])
            mm.then_inc(dt_done, 1)
            project(1)
            project(2)
            dta = tmp[0]
            pe.wait_ge(dve_step, n_dve)
            for way, tri in ((0, CON_UP), (1, CON_LOW)):
                mm = pe.matmul(m.ps[:, 4 + way, 0:TT * 32], m.con[:, tri:tri + P],
                               dta[:, :, way * 32:way * 32 + 32], start=True, stop=True)
            mm.then_inc(pe_step, 1)
            pe.matmul(m.ps[:, 6], m.con[:, CON_ONES:CON_ONES + P], flat(dta[:]), start=True,
                      stop=True).then_inc(pe_step, 1)
            project(3)
            pe.wait_ge(dve_step, n_dve + 3)
            for c in range(TT):
                mm = pe.transpose(m.ps[0:64, 4 + c // 4, (c % 4) * P:(c % 4 + 1) * P], sums[:, c],
                                  m.con[:, CON_ID:CON_ID + P])
            mm.then_inc(pe_step, 1)
            with pe.Fori(2, N // 2) as i:
                for r in range(2):
                    for n in range(2):
                        pr.half(pe, u_hi, u_lo, i * 2 + r, r, n)


def bc(ap, n):
    return ap.unsqueeze(len(ap.shape)).to_broadcast([*ap.shape, n])


def ssd_stage(m, pr, u_hi, u_lo):
    nc, d = m.nc, m.dram
    STEPS = 2 * TT
    LAST = STEPS + 5
    NS = 12
    NT = 2 * (XT + 1)
    UG = GRP0 + GT
    order = [(q, way, k) for way in (1, 0) for q in range(NSEQ) for k in range(BLOCKS - 1)]
    gives = lambda n: order[n][0] * BLOCKS + (order[n][2] if order[n][1] == 0 else BLOCKS - 1 - order[n][2])
    index = {(order[n][1], gives(n) + (1 if order[n][1] == 0 else -1)): n for n in range(NS)}
    forward = {gives(n): n for n in range(NS // 2, NS)}
    slot = lambda n: n if n < NS // 2 else NS // 2 + n % 2
    offs = [[(way, index[way, c]) for way in range(2) if (way, c) in index] for c in range(TT)]
    off_before = [sum(len(o) for o in offs[:c]) for c in range(TT)]
    halves = {0: (5, 0), 1: (5, 1), 3: (6, 0), 5: (6, 1), 7: (7, 0), 9: (7, 1), 11: (8, 0), 13: (8, 1), 15: (9, 0), 16: (9, 1)}
    services = {0: 5, 2: 6, 6: 7, 10: 8, 14: 9}
    last_drain = 15
    FB = 3
    MS = 4
    with ExitStack() as ctx:
        sem = lambda n: m.semaphore(f"ssd_{n}")
        sb = lambda n, s, t=F32: ctx.enter_context(nc.sbuf_tensor(n, s, t))
        xpad = sb("xpad", [P, 2, NSEQ, SEQ + 2 * HALO])
        taps = sb("taps", [P, CT * (TAPS + 1)])
        conv = sb("conv", [P, 4, NSEQ, SEQ])
        xs = sb("xs", [P, TT, GW])
        b_tm = sb("b_tm", [P, TT, NSTATE])
        states = sb("states", [P, NS // 2 + 2, GW])
        grp = sb("grp", [P, STEPW])
        xw = sb("xw", [P, 2, GW])
        fb = sb("fb", [P, FB, 2, BANK])
        tl = sb("tl", [P, 2, BANK])
        tu = sb("tu", [P, MS, BANK])
        cb = sb("cb", [P, 2, 2, P])
        y = sb("y", [P, 2, GW])
        off = sb("off", [P, 2, GW])
        zy = sb("zy", [P, 2, XT, P])
        conv_slot = [0, 1, 0, 1, 2, 3]
        flat_conv = lambda i: conv[:, conv_slot[i]].rearrange("p a b -> p (a b)")
        bm_t, cm_t = flat_conv(XT), flat_conv(XT + 1)
        grp5 = grp[:, 0:STEPW - GH].rearrange("p (a c w h) -> p a c w h", a=5, c=TT, w=2)
        SUMS, DT, EXPA, WIN, DEC = (grp5[:, i] for i in range(5))
        skip = grp[:, STEPW - GH:]
        heads = lambda ap: ap.rearrange("p (h w) -> p h w", h=GH)

        taps_landed, grp_landed = sem("taps_landed"), sem("grp_landed")
        x_landed, z_landed, y_stored = ([sem(f"{n}{r}") for r in range(2)] for n in ("x_landed", "z_landed", "y_stored"))
        fb_landed = [sem(f"fb_landed{r}") for r in range(FB)]
        fb_count = lambda k: len(range(k % FB, k + 1, FB))
        fb_total = lambda k: len(range(k % FB, STEPS, FB))
        pads, conv_step, conv_done = sem("pads"), sem("conv_step"), sem("conv_done")
        turned, tm_ready = sem("turned"), sem("tm_ready")
        xw_ready, st_done, decayed, st_ready = sem("xw_ready"), sem("st_done"), sem("decayed"), sem("st_ready")
        cb_done, cb_ready = sem("cb_done"), sem("cb_ready")
        b_shifted, min_done, e_ready = sem("b_shifted"), sem("min_done"), sem("e_ready")
        masked, t_sum, m_ready = sem("masked"), sem("t_sum"), sem("m_ready")
        y_done, skipped, y_read = sem("y_done"), sem("skipped"), sem("y_read")
        off_done, off_read, off_added = sem("off_done"), sem("off_read"), sem("off_added")
        y_turned, yz_ready = sem("y_turned"), sem("yz_ready")
        block = ctx.enter_context(nc.Block())
        units = Units(m, UG)

        def groups(eng, group):
            with eng.Fori(0, GROUPS - 1) as g:
                group(g, False)
            group(GROUPS - 1, True)

        @block.sync
        def _(sp):
            at = lambda v: v if isinstance(v, int) else sp.snap(v)

            def load_weights(g, u):
                row = at(g * (GT * P) + (UG + u) * P)
                sp.wait_ge(m.w_lo_ready, g * GT + (UG + u - 1))
                load_unit(sp, m, u % 2, d["w_all"][bass.ds(row, P), :])

            def load_x(g, i):
                row = at(g * (GT * P) + (GRP0 + XT + i) * P)
                if i < 2:
                    sp.wait_ge(pr.stored[i % 2], g * (GT * 8) + (GRP0 + XT + 2) * 8)
                else:
                    sp.wait_ge(conv_step, g * (CT * TAPS) + (i - 1) * TAPS)
                sp.dma_start(xpad[:, i % 2, :, HALO:HALO + SEQ],
                             d["proj"][bass.ds(row, P), :].rearrange("p (a b) -> p a b", a=NSEQ)).then_inc(x_landed[i % 2], 16)

            def load_taps(g):
                row = at(g * P)
                sp.dma_start(taps[:], d["taps"][bass.ds(row, P), :]).then_inc(taps_landed, 16)

            def load_fb(g, k):
                row = at(g * STEPS + k)
                if k >= FB:
                    sp.wait_ge(m_ready, g * STEPS + (k - FB + 1))
                sp.dma_start(fb[:, k % FB].rearrange("p a b -> p (a b)"),
                             d["sums"][bass.ds(row, 1), :].squeeze(0).partition_broadcast(P)).then_inc(fb_landed[k % FB], 16)

            def load_z(g, c):
                row = at(g * (GT * P) + GRP0 * P)
                if c >= 2 or not isinstance(g, int) or g:
                    sp.wait_ge(y_stored[c % 2], g * (TT * 8) + (c // 2) * 16)
                sp.dma_start(zy[:, c % 2], d["proj"][bass.ds(row, XT * P), c * P:(c + 1) * P]
                             .rearrange("(a p) t -> p a t", p=P)).then_inc(z_landed[c % 2], 16)

            def store_y(g, c):
                row = at(g * (XT * P))
                sp.wait_ge(yz_ready, g * TT + (c + 1))
                sp.dma_start(d["yt"][bass.ds(row, XT * P), c * P:(c + 1) * P].rearrange("(a p) t -> p a t", p=P),
                             zy[:, c % 2]).then_inc(y_stored[c % 2], 16)

            def group(g, last):
                g_row = at(g * P)
                load_weights(g, 3)
                sp.dma_start(grp[:], d["steps"][bass.ds(g_row, P), :]).then_inc(grp_landed, 16)
                load_x(g, 2)
                load_x(g, 3)
                load_weights(g, 4)
                load_x(g, 4)
                load_x(g, 5)
                load_weights(g, 5)
                for k in range(FB):
                    load_fb(g, k)
                load_weights(g, 6)
                load_weights(g, 7)
                for k in range(LAST):
                    if k >= 6 and k % 2 == 0:
                        store_y(g, (k - 6) // 2)
                    if k >= 7 and k % 2 == 1 and (k - 7) // 2 + 2 < TT:
                        load_z(g, (k - 7) // 2 + 2)
                    if k in services and not (last and services[k] == 9):
                        load_weights(g, services[k] + 3)
                    if k + FB < STEPS:
                        load_fb(g, k + FB)
                    if k == LAST - 6 and not last:
                        load_taps(g + 1)
                        load_x(g + 1, 0)
                        load_x(g + 1, 1)
                if not last:
                    load_z(g + 1, 0)
                    load_z(g + 1, 1)

            load_taps(0)
            sp.wait_ge(pads, 1)
            load_x(0, 0)
            load_x(0, 1)
            load_z(0, 0)
            load_z(0, 1)
            load_weights(0, 2)
            groups(sp, group)
            for r in range(2):
                sp.wait_ge(y_stored[r], GROUPS * TT * 8)

        @block.vector
        def _(dve):
            def service(g, j):
                units.lo(dve, g * GT + (j + 1), (j + 1) % 2)

            def convolve(g, i):
                dve.wait_ge(x_landed[i % 2], g * (8 * CT) + 16 * (i // 2 + 1))
                if 2 <= i < XT:
                    dve.wait_ge(turned, g * NT + 2 * (i - 1))
                for t in range(TAPS):
                    w = taps[:, i * (TAPS + 1) + t:i * (TAPS + 1) + t + 1]
                    src, dst = xpad[:, i % 2, :, t:t + SEQ], conv[:, conv_slot[i]]
                    if t == 0:
                        ins = dve.tensor_scalar(dst, src, w, None, ALU.mult)
                    else:
                        dve.wait_ge(conv_step, g * (CT * TAPS) + (i * TAPS + t))
                        ins = dve.scalar_tensor_tensor(dst, src, w, dst, ALU.mult, ALU.add)
                    ins.then_inc(conv_step, 1)

            def state(g, n, bank):
                dve.wait_ge(st_done, g * NS + n + 1)
                if n >= NS // 2 + 2:
                    taker = gives(n - 2) + 1
                    dve.wait_ge(off_done, g * NS + off_before[taker] + 1)
                if order[n][2] == 0:
                    dve.tensor_copy(states[:, slot(n)], m.ps[:, bank]).then_inc(st_ready, 1)
                else:
                    dve.wait_ge(st_ready, g * NS + n)
                    dve.tensor_tensor(heads(states[:, slot(n)]), heads(states[:, slot(n - 1)]),
                                      bc(DEC[:, gives(n), order[n][1]], 64), ALU.mult).then_inc(decayed, 1)
                    dve.wait_ge(decayed, g * 8 + (n - n // 3))
                    dve.tensor_tensor(states[:, slot(n)], states[:, slot(n)], m.ps[:, bank], ALU.add).then_inc(st_ready, 1)

            def mask(g, c):
                dve.wait_ge(cb_done, g * TT + c + 1)
                if c >= 2:
                    dve.wait_ge(masked, g * (2 * STEPS) + 4 * (c - 1))
                for way, tri in ((0, CON_UP), (1, CON_LOW)):
                    dve.tensor_tensor(cb[:, c % 2, way], m.ps[:, 7, 0:P], m.con[:, tri:tri + P],
                                      ALU.mult).then_inc(cb_ready, 1)

            def finish_chunk(g, c):
                s = c % 2
                dve.wait_ge(skipped, g * TT + c + 1)
                dve.wait_ge(y_done, g * STEPS + 2 * c + 2)
                dve.tensor_tensor(y[:, s], y[:, s], m.ps[:, 4], ALU.add).then_inc(y_read, 1)
                for n, (way, _) in enumerate(offs[c]):
                    at = off_before[c] + n
                    if n == 0:
                        dve.wait_ge(off_done, g * NS + at + len(offs[c]))
                    if at >= 2:
                        dve.wait_ge(off_added, g * NS + at - 1)
                    dve.tensor_tensor(heads(off[:, at % 2]), heads(m.ps[:, 5 + way]), bc(EXPA[:, c, way], 64),
                                      ALU.mult).then_inc(off_read, 1)
                for n in range(len(offs[c])):
                    at = off_before[c] + n
                    dve.wait_ge(off_read, g * NS + at + 1)
                    if n == 0:
                        dve.wait_ge(y_read, g * TT + c + 1)
                    else:
                        dve.wait_ge(off_added, g * NS + at)
                    dve.tensor_tensor(y[:, s], y[:, s], off[:, at % 2], ALU.add).then_inc(off_added, 1)

            def group(g, last):
                dve.wait_ge(taps_landed, g * 16 + 16)
                service(g, 0)
                convolve(g, 0)
                convolve(g, 1)
                service(g, 1)
                convolve(g, 2)
                convolve(g, 3)
                service(g, 2)
                convolve(g, 4)
                convolve(g, 5)
                service(g, 3)
                dve.wait_ge(grp_landed, g * 16 + 16)
                state(g, 0, 6)
                state(g, 1, 7)
                service(g, 4)
                for n in range(2, NS // 2):
                    state(g, n, 6 + n % 2)
                mask(g, 0)
                for k in range(LAST):
                    c, h = divmod(k, 2)
                    if k >= 4 and h == 0 and (k - 4) // 2 < TT:
                        finish_chunk(g, (k - 4) // 2)
                    if k < STEPS:
                        dve.wait_ge(b_shifted, g * STEPS + k + 1)
                        for i in range(4):
                            f = fb[:, k % FB, 0, i * P:(i + 1) * P]
                            ins = dve.scalar_tensor_tensor(f, f, SUMS[:, c, 0, 4 * h + i:4 * h + i + 1],
                                                           fb[:, k % FB, 1, i * P:(i + 1) * P], ALU.subtract, ALU.min)
                        ins.then_inc(min_done, 1)
                    if 1 <= k <= STEPS:
                        j = k - 1
                        dve.wait_ge(masked, g * (2 * STEPS) + 2 * j + 2)
                        dve.tensor_tensor(tu[:, j % MS], tu[:, j % MS], tl[:, j % 2], ALU.add).then_inc(t_sum, 1)
                        dve.wait_ge(e_ready, g * STEPS + j + 1)
                        dve.wait_ge(t_sum, g * STEPS + j + 1)
                        dve.tensor_tensor(tu[:, j % MS], tu[:, j % MS], fb[:, j % FB, 0], ALU.mult).then_inc(m_ready, 1)
                    if k >= 6 and h == 0 and (k - 6) // 2 < TT:
                        gated = (k - 6) // 2
                        dve.wait_ge(z_landed[gated % 2], g * (8 * TT) + 16 * (gated // 2 + 1))
                        dve.wait_ge(y_turned, g * TT + gated + 1)
                        dve.tensor_tensor(zy[:, gated % 2], zy[:, gated % 2], m.ps[:, 7].rearrange("p (a b) -> p a b", a=XT),
                                          ALU.mult).then_inc(yz_ready, 1)
                    if h == 0 and c + 1 < TT:
                        mask(g, c + 1)
                    if h == 1 and c in forward:
                        state(g, forward[c], 7)
                    if k in services:
                        service(g, services[k])

            dve.wait_ge(pads, 1)
            groups(dve, group)

        @block.scalar
        def _(act):
            def drain(g, j, last):
                z = not last and j < XT
                pr.evacuate(act, g * GT + (UG + j), j % 2, ACT.Silu if z else ACT.Copy,
                            scale=HD ** -0.5 if last and j < K0 - Q0 else 1.0)

            def service(g, j, last):
                units.hi(act, g * GT + (j + 1), (j + 1) % 2)
                if j:
                    drain(g, j - 1, last)

            def silu(g, i):
                act.wait_ge(conv_step, g * (CT * TAPS) + TAPS * (i + 1))
                act.activation(flat_conv(i), flat_conv(i), ACT.Silu,
                               bias=taps[:, i * (TAPS + 1) + TAPS:(i + 1) * (TAPS + 1)]).then_inc(conv_done, 1)

            def copy_turned(g, i):
                for n in range(2):
                    act.wait_ge(turned, g * NT + 2 * i + n + 1)
                    dst = b_tm[:, 4 * n:4 * n + 4] if i == XT else xs[:, 4 * n:4 * n + 4, i * P:(i + 1) * P]
                    act.activation(dst, m.ps[:, 4 + (2 * i + n) % 4].rearrange("p (a b) -> p a b", a=4),
                                   ACT.Copy).then_inc(tm_ready, 1)

            def group(g, last):
                for r in range(2):
                    act.wait_ge(pr.stored[r], g * (GT * 8) + UG * 8)
                service(g, 0, last)
                silu(g, 0)
                silu(g, 1)
                service(g, 1, last)
                copy_turned(g, 0)
                silu(g, 2)
                copy_turned(g, 1)
                silu(g, 3)
                service(g, 2, last)
                copy_turned(g, 2)
                silu(g, 4)
                copy_turned(g, 3)
                service(g, 3, last)
                silu(g, 5)
                copy_turned(g, 4)
                service(g, 4, last)
                for k in range(STEPS):
                    act.wait_ge(min_done, g * STEPS + k + 1)
                    act.activation(fb[:, k % FB, 0], fb[:, k % FB, 0], ACT.Exp).then_inc(e_ready, 1)
                    if k in services:
                        service(g, services[k], last)
                    if k == last_drain:
                        drain(g, 9, last)

            groups(act, group)
            for r in range(2):
                act.wait_ge(pr.stored[r], (UG + GROUPS * GT) * 8)

        @block.gpsimd
        def _(pool):
            def weigh(g, n):
                if n >= 2:
                    pool.wait_ge(st_done, g * NS + n - 1)
                c = gives(n)
                pool.tensor_tensor(heads(xw[:, n % 2]), heads(xs[:, c]), bc(WIN[:, c, order[n][1]], 64),
                                   ALU.mult).then_inc(xw_ready, 1)

            def start_y(g, c):
                if c >= 2:
                    pool.wait_ge(y_turned, g * TT + c - 1)
                pool.tensor_tensor(heads(y[:, c % 2]), heads(xs[:, c]), bc(skip, 64), ALU.mult).then_inc(skipped, 1)

            def group(g, last):
                pool.wait_ge(grp_landed, g * 16 + 16)
                pool.wait_ge(tm_ready, g * NT + 2 * XT)
                for n in range(NS // 2):
                    weigh(g, n)
                for k in range(STEPS):
                    c, h = divmod(k, 2)
                    if h == 0 and c in forward:
                        weigh(g, forward[c])
                    pool.wait_ge(fb_landed[k % FB], g * (16 * fb_total(k)) + 16 * fb_count(k))
                    b = fb[:, k % FB, 1].rearrange("p (a b) -> p a b", a=4)
                    pool.tensor_tensor(b, b, bc(SUMS[:, c, 1, 4 * h:4 * h + 4], P), ALU.subtract).then_inc(b_shifted, 1)
                    if h == 0:
                        pool.wait_ge(cb_ready, g * (2 * TT) + 2 * c + 2)
                    if k >= 2:
                        pool.wait_ge(t_sum, g * STEPS + k - 1)
                    if k >= MS:
                        pool.wait_ge(y_done, g * STEPS + k - MS + 1)
                    for way, dst in ((1, tl[:, k % 2]), (0, tu[:, k % MS])):
                        one = cb[:, c % 2, way].unsqueeze(1).to_broadcast([P, 4, P])
                        pool.tensor_tensor(dst.rearrange("p (a b) -> p a b", a=4), one,
                                           bc(DT[:, c, way, 4 * h:4 * h + 4], P), ALU.mult).then_inc(masked, 1)
                    if k >= 3 and h == 1:
                        start_y(g, (k - 3) // 2)
                start_y(g, TT - 1)

            pool.memset(xpad[:], 0.0).then_inc(pads, 1)
            groups(pool, group)

        @block.tensor
        def _(pe):
            ident = m.con[:, CON_ID:CON_ID + P]

            def project(g, j, n):
                pr.half(pe, u_hi, u_lo, g * GT + (UG + j), j % 2, n)

            def turn(g, i):
                pe.wait_ge(conv_done, g * CT + i + 1)
                for n in range(2):
                    if i >= 2:
                        pe.wait_ge(tm_ready, g * NT + 2 * i + n - 3)
                    for q in range(4):
                        c = 4 * n + q
                        mm = pe.transpose(m.ps[:, 4 + (2 * i + n) % 4, q * P:(q + 1) * P],
                                          flat_conv(i)[:, c * P:(c + 1) * P], ident)
                    mm.then_inc(turned, 1)

            def state(g, n, bank):
                pe.wait_ge(xw_ready, g * NS + n + 1)
                pe.matmul(m.ps[:, bank], b_tm[:, gives(n)], xw[:, n % 2], start=True, stop=True).then_inc(st_done, 1)

            def group(g, last):
                project(g, 0, 0)
                project(g, 0, 1)
                turn(g, 0)
                project(g, 1, 0)
                turn(g, 1)
                project(g, 1, 1)
                turn(g, 2)
                project(g, 2, 0)
                turn(g, 3)
                project(g, 2, 1)
                project(g, 3, 0)
                turn(g, 4)
                project(g, 3, 1)
                pe.wait_ge(tm_ready, g * NT + NT)
                for n in range(NS // 2):
                    if n >= 2:
                        pe.wait_ge(st_ready, g * NS + n - 1)
                    state(g, n, 6 + n % 2)
                    if n in (1, 5):
                        project(g, 4, n // 4)
                pe.wait_ge(conv_done, g * CT + CT)
                pe.wait_ge(st_ready, g * NS + NS // 2)

                def correlate(c):
                    chunk = slice(c * P, (c + 1) * P)
                    pe.matmul(m.ps[:, 7, 0:P], bm_t[:, chunk], cm_t[:, chunk], start=True, stop=True).then_inc(cb_done, 1)

                correlate(0)
                for k in range(LAST):
                    if 2 <= k < STEPS + 2:
                        j = k - 2
                        c, h = divmod(j, 2)
                        chunk = slice(c * P, (c + 1) * P)
                        pe.wait_ge(m_ready, g * STEPS + j + 1)
                        if h == 0:
                            if c >= 1:
                                pe.wait_ge(y_read, g * TT + c)
                                pe.wait_ge(off_read, g * NS + off_before[c])
                            for way, n in offs[c]:
                                if way == 0:
                                    pe.wait_ge(st_ready, g * NS + n + 1)
                                pe.matmul(m.ps[:, 5 + way], cm_t[:, chunk], states[:, slot(n)], start=True,
                                          stop=True).then_inc(off_done, 1)
                        for i in range(4):
                            hh = 4 * h + i
                            mm = pe.matmul(m.ps[:, 4, hh * 64:(hh + 1) * 64], tu[:, j % MS, i * P:(i + 1) * P],
                                           xs[:, c, hh * 64:(hh + 1) * 64], start=True, stop=True)
                        mm.then_inc(y_done, 1)
                    c, h = divmod(k, 2)
                    if h == 0 and c + 1 < TT:
                        pe.wait_ge(cb_ready, g * (2 * TT) + 2 * c + 2)
                        if k >= 6:
                            pe.wait_ge(yz_ready, g * TT + (k - 4) // 2)
                        elif c >= 1:
                            pe.wait_ge(st_ready, g * NS + forward[c - 1] + 1)
                        correlate(c + 1)
                    if k < STEPS and h == 1:
                        pe.wait_ge(cb_ready, g * (2 * TT) + 2 * min(c + 2, TT))
                        if c in forward:
                            state(g, forward[c], 7)
                    if k in halves:
                        project(g, *halves[k])
                    if k >= 5 and h == 1 and (k - 5) // 2 < TT:
                        t = (k - 5) // 2
                        pe.wait_ge(off_added, g * NS + off_before[t] + len(offs[t]))
                        if c in forward:
                            pe.wait_ge(st_ready, g * NS + forward[c] + 1)
                        if k >= STEPS - 1:
                            pe.wait_ge(yz_ready, g * TT + t)
                        for i in range(4):
                            mm = pe.transpose(m.ps[:, 7, i * P:(i + 1) * P], y[:, t % 2, i * P:(i + 1) * P], ident)
                        mm.then_inc(y_turned, 1)

            groups(pe, group)


def attention_stage(m, pr, u_hi, u_lo):
    nc, d = m.nc, m.dram
    spans = [(max(b - 1, 0), min(b + 1, BLOCKS - 1) - max(b - 1, 0) + 1, P if b == 0 else 0) for b in range(BLOCKS)]
    slopes = [2.0 ** (-8.0 * (h + 1) / HEADS) for h in range(HEADS)]
    IH = HEADS // 2
    ITEMS = 2 * BLOCKS
    item = lambda it: (*spans[it // 2], it // 2, (it % 2) * IH)
    turns = [IH * spans[it // 2][1] // 4 for it in range(ITEMS)]
    turns_before = [sum(turns[:it]) for it in range(ITEMS)]
    NTURN = sum(turns)
    rep = HEADS // KVH
    with ExitStack() as ctx:
        sem = lambda n: m.semaphore(f"att_{n}")
        sb = lambda n, s, t=F32: ctx.enter_context(nc.sbuf_tensor(n, s, t))
        qs = sb("qs", [P, HEADS // 2, SEQ])
        kd = sb("kd", [P, KVH, SEQ])
        vt = sb("vt", [P, 2, SEQ])
        v = sb("v", [P, BLOCKS, KVH, 2 * HD], F32R)
        s_sb = sb("s_sb", [P, 2, IH, 3 * P])
        pt_hi, pt_lo = sb("pt_hi", [P, IH * 3, P], F32R), sb("pt_lo", [P, IH * 3, P], F32R)
        o_low = sb("o_low", [HD, 2, BANK])
        ot = sb("ot_sb", [HD, 2, IH, P])
        st = sb("att_st", [P, 2, 6, IH])
        qk_landed, q_landed, v_landed = sem("qk_landed"), sem("q_landed"), sem("v_landed")
        s_done, s_read, normed = sem("s_done"), sem("s_read"), sem("normed")
        stat, m_ready, p_ready, sink_e, den = sem("stat"), sem("m_ready"), sem("p_ready"), sem("sink_e"), sem("den")
        v_turned, v_hi_done, v_ready = sem("v_turned"), sem("v_hi_done"), sem("v_ready")
        p_turned, pt_hi_done, pt_ready = sem("p_turned"), sem("pt_hi_done"), sem("pt_ready")
        o_done, o_low_done, ot_ready = sem("o_done"), sem("o_low_done"), sem("ot_ready")
        ot_stored = [sem(f"ot_stored{r}") for r in range(2)]
        block = ctx.enter_context(nc.Block())
        units = Units(m, GATE0)
        MAX, NMAX, SINK, ESINK, SUM, RSUM = range(6)

        @block.sync
        def _(sp):
            def load_weights(u):
                sp.wait_ge(m.w_lo_ready, GATE0 + u - 1)
                load_unit(sp, m, u % 2, d["w_all"][(GATE0 + u) * P:(GATE0 + u + 1) * P, :])

            def load_qk(s):
                rows = lambda tile, n: d["proj"][tile * P:(tile + n) * P, s * SEQ:(s + 1) * SEQ]
                q = rows(Q0, 8).rearrange("(a p) t -> p a t", p=P)
                sp.dma_start(qs[:, :, 0:P], q[:, :, 0:P]).then_inc(qk_landed, 16)
                for half in range(2):
                    sp.dma_start(kd[half * 64:(half + 1) * 64], rows(K0, 2).rearrange("(a p) t -> p a t", p=HD)).then_inc(qk_landed, 16)
                sp.dma_start(qs[:, :, P:SEQ], q[:, :, P:SEQ]).then_inc(q_landed, 16)

            load_qk(0)
            for s in range(NSEQ):
                for r in range(2):
                    if s:
                        sp.wait_ge(ot_stored[r], s * (ITEMS * 8))
                sp.dma_start(vt[:], d["proj"][V0 * P:(V0 + 2) * P, s * SEQ:(s + 1) * SEQ]
                             .rearrange("(a p) t -> p a t", p=P)).then_inc(v_landed, 16)
                load_weights(s * ITEMS + 2)
                load_weights(s * ITEMS + 3)
                for it in range(ITEMS):
                    if it + 2 < ITEMS:
                        load_weights(s * ITEMS + it + 4)
                    if it == ITEMS - 1 and s + 1 < NSEQ:
                        sp.wait_ge(s_done, (s + 1) * (ITEMS * IH))
                        load_qk(s + 1)
                    b, half = divmod(it, 2)
                    sp.wait_ge(ot_ready, 2 * (s * ITEMS + it + 1))
                    sp.dma_start(d["ot"].rearrange("(h p) t -> p h t", p=HD)
                                 [:, IH * half:IH * half + IH, s * SEQ + b * P:s * SEQ + (b + 1) * P],
                                 ot[:, it % 2]).then_inc(ot_stored[it % 2], 16)
            for r in range(2):
                sp.wait_ge(ot_stored[r], NSEQ * (ITEMS * 8))

        @block.tensor
        def _(pe):
            ident = m.con[:, CON_ID:CON_ID + P]
            with pe.Fori(0, NSEQ) as s:
                def project(j, n):
                    pr.half(pe, u_hi, u_lo, s * ITEMS + (GATE0 + j), j % 2, n)

                def score(it, i):
                    k0, nk, _, b, h0 = item(it)
                    n, h = it * IH + i, h0 + i
                    if it == 2 and i == 0:
                        pe.wait_ge(q_landed, s * 16 + 16)
                    if n >= 2:
                        pe.wait_ge(s_read, s * (ITEMS * IH) + n - 1)
                    half = slice((h % 2) * 64, (h % 2) * 64 + 64)
                    pe.matmul(m.ps[:, 4 + n % 2, 0:nk * P], qs[half, h // 2, b * P:(b + 1) * P],
                              kd[half, h // rep, k0 * P:(k0 + nk) * P], start=True, stop=True).then_inc(s_done, 1)

                def turn(it, t):
                    nk = item(it)[1]
                    last_head = (4 * t + 3) // nk
                    pe.wait_ge(normed, s * (ITEMS * IH // 2) + (it * (IH // 2) + last_head // 2 + 1))
                    n = turns_before[it] + t
                    if n >= 2:
                        pe.wait_ge(pt_ready, s * NTURN + (n - 1))
                    for i in range(4):
                        h, kb = divmod(4 * t + i, nk)
                        mm = pe.transpose(m.ps[:, 6 + n % 2, i * P:(i + 1) * P],
                                          s_sb[:, it % 2, h, kb * P:(kb + 1) * P], ident)
                    mm.then_inc(p_turned, 1)

                project(0, 0)
                pe.wait_ge(qk_landed, s * 48 + 48)
                for i in range(IH):
                    score(0, i)
                project(0, 1)
                pe.wait_ge(v_landed, s * 16 + 16)
                for n in range(2):
                    for i in range(4):
                        kb, ft = divmod(4 * n + i, 2)
                        mm = pe.transpose(m.ps[:, 6 + n, i * P:(i + 1) * P], vt[:, ft, kb * P:(kb + 1) * P], ident)
                    mm.then_inc(v_turned, 1)
                for it in range(ITEMS):
                    k0, nk, _, b, h0 = item(it)
                    for i in range(IH):
                        if it + 1 < ITEMS:
                            score(it + 1, i)
                        if i == 0:
                            if it == 0:
                                pe.wait_ge(v_ready, s * 2 + 2)
                            else:
                                pe.wait_ge(ot_ready, 2 * (s * ITEMS + it))
                        if i < turns[it]:
                            turn(it, i)
                    if it + 1 < ITEMS:
                        project(it + 1, 0)
                    pe.wait_ge(pt_ready, s * NTURN + (turns_before[it] + turns[it]))
                    for j in range(2):
                        g = h0 // rep + j
                        for kb in range(nk):
                            for q, pt in enumerate((pt_hi, pt_lo)):
                                four = pt[:, 4 * j * nk:4 * (j + 1) * nk].rearrange("p (h k) t -> p h k t", k=nk)[:, :, kb]
                                mm = pe.matmul(m.ps[:, 6 + j].rearrange("p (a b) -> p a b", a=4), v[:, k0 + kb, g], four,
                                               start=kb == 0 and q == 0, stop=kb == nk - 1 and q == 1)
                        mm.then_inc(o_done, 1)
                    if it + 1 < ITEMS:
                        project(it + 1, 1)

        @block.vector
        def _(dve):
            with dve.Fori(0, NSEQ) as s:
                def read_score(it, i):
                    _, nk, c0, _, h0 = item(it)
                    if it >= 2 and i == 0:
                        dve.wait_ge(p_turned, s * NTURN + turns_before[it - 1])
                    n = it * IH + i
                    dve.wait_ge(s_done, s * (ITEMS * IH) + n + 1)
                    dve.scalar_tensor_tensor(s_sb[:, it % 2, i, 0:nk * P],
                                             m.con[:, CON_DIST + c0:CON_DIST + c0 + nk * P], -slopes[h0 + i],
                                             m.ps[:, 4 + n % 2, 0:nk * P], ALU.mult, ALU.add).then_inc(s_read, 1)

                def maxima(it):
                    _, nk, _, _, h0 = item(it)
                    t = st[:, it % 2]
                    sink = m.rows[:, R_SINK + h0:R_SINK + h0 + IH]
                    dve.wait_ge(s_read, s * (ITEMS * IH) + (it + 1) * IH)
                    dve.tensor_reduce(t[:, MAX], s_sb[:, it % 2, :, 0:nk * P], AX.X, ALU.max).then_inc(stat, 1)
                    dve.wait_ge(stat, s * (2 * ITEMS) + (2 * it + 1))
                    dve.tensor_tensor(t[:, MAX], t[:, MAX], sink, ALU.max).then_inc(stat, 1)
                    dve.wait_ge(stat, s * (2 * ITEMS) + (2 * it + 2))
                    dve.tensor_scalar(t[:, NMAX], t[:, MAX], -1.0, None, ALU.mult).then_inc(m_ready, 1)
                    dve.tensor_tensor(t[:, SINK], sink, t[:, MAX], ALU.subtract).then_inc(m_ready, 1)

                def denominator(it):
                    t = st[:, it % 2]
                    dve.wait_ge(sink_e, s * ITEMS + it + 1)
                    dve.wait_ge(p_ready, s * (ITEMS * IH) + (it + 1) * IH)
                    dve.tensor_tensor(t[:, SUM], t[:, SUM], t[:, ESINK], ALU.add).then_inc(den, 1)
                    dve.wait_ge(den, s * (2 * ITEMS) + (2 * it + 1))
                    dve.reciprocal(t[:, RSUM], t[:, SUM]).then_inc(den, 1)

                for i in range(IH):
                    read_score(0, i)
                maxima(0)
                units.lo(dve, s * ITEMS + 1, 1)
                denominator(0)
                for n in range(2):
                    dve.wait_ge(v_turned, s * 2 + n + 1)
                    turned = m.ps[:, 6 + n].rearrange("p (k g d) -> p k g d", k=2, g=KVH)
                    dve.tensor_copy(v[:, 2 * n:2 * n + 2, :, 0:HD], turned).then_inc(v_hi_done, 1)
                    dve.wait_ge(v_hi_done, s * 2 + n + 1)
                    dve.tensor_tensor(v[:, 2 * n:2 * n + 2, :, HD:2 * HD], turned,
                                      v[:, 2 * n:2 * n + 2, :, 0:HD].bitcast(F32), ALU.subtract).then_inc(v_ready, 1)
                for it in range(ITEMS):
                    for i in range(IH):
                        if it + 1 < ITEMS:
                            read_score(it + 1, i)
                        if i < turns[it]:
                            n = turns_before[it] + i
                            dve.wait_ge(pt_hi_done, s * NTURN + n + 1)
                            dve.tensor_tensor(pt_lo[:, 4 * i:4 * i + 4].rearrange("p a b -> p (a b)"), m.ps[:, 6 + n % 2],
                                              pt_hi[:, 4 * i:4 * i + 4].rearrange("p a b -> p (a b)").bitcast(F32),
                                              ALU.subtract).then_inc(pt_ready, 1)
                    if it + 1 < ITEMS:
                        maxima(it + 1)
                    if it + 2 <= ITEMS:
                        units.lo(dve, s * ITEMS + (it + 2), it % 2)
                    for j in range(2):
                        dve.wait_ge(o_low_done, 2 * (s * ITEMS + it) + j + 1)
                        if it >= 2 and j == 0:
                            dve.wait_ge(ot_stored[it % 2], s * (ITEMS * 8) + (it // 2) * 16)
                        dve.tensor_tensor(ot[:, it % 2, 4 * j:4 * j + 4].rearrange("p a b -> p (a b)"),
                                          m.ps[0:HD, 6 + j], o_low[:, j], ALU.add).then_inc(ot_ready, 1)
                    if it + 1 < ITEMS:
                        denominator(it + 1)

        @block.gpsimd
        def _(pool):
            with pool.Fori(0, NSEQ) as s:
                for it in range(ITEMS):
                    nk = item(it)[1]
                    pool.wait_ge(den, s * (2 * ITEMS) + (2 * it + 2))
                    for i in range(0, IH, 2):
                        p = s_sb[:, it % 2, i:i + 2, 0:nk * P]
                        pool.tensor_tensor(p, p, bc(st[:, it % 2, RSUM, i:i + 2], nk * P), ALU.mult).then_inc(normed, 1)

        @block.scalar
        def _(act):
            with act.Fori(0, NSEQ) as s:
                def drain(j):
                    pr.evacuate(act, s * ITEMS + (GATE0 + j), j % 2, ACT.Sigmoid)

                def exponents(it):
                    nk = item(it)[1]
                    t = st[:, it % 2]
                    act.wait_ge(m_ready, s * (2 * ITEMS) + (2 * it + 2))
                    act.activation(t[:, ESINK], t[:, SINK], ACT.Exp).then_inc(sink_e, 1)
                    for i in range(IH):
                        p = s_sb[:, it % 2, i, 0:nk * P]
                        act.activation(p, p, ACT.Exp, bias=t[:, NMAX, i:i + 1],
                                       accum_out=t[:, SUM, i:i + 1]).then_inc(p_ready, 1)

                units.hi(act, s * ITEMS + 1, 1)
                exponents(0)
                for it in range(ITEMS):
                    if it:
                        act.wait_ge(o_done, 2 * (s * ITEMS + it))
                    for i in range(turns[it]):
                        n = turns_before[it] + i
                        act.wait_ge(p_turned, s * NTURN + n + 1)
                        act.activation(pt_hi[:, 4 * i:4 * i + 4].rearrange("p a b -> p (a b)"),
                                       m.ps[:, 6 + n % 2], ACT.Copy).then_inc(pt_hi_done, 1)
                    if it + 2 <= ITEMS:
                        units.hi(act, s * ITEMS + (it + 2), it % 2)
                    drain(it)
                    if it + 1 < ITEMS:
                        exponents(it + 1)
                    for j in range(2):
                        act.wait_ge(o_done, 2 * (s * ITEMS + it) + j + 1)
                        if it:
                            act.wait_ge(ot_ready, 2 * (s * ITEMS + it - 1) + j + 1)
                        act.activation(o_low[:, j], m.ps[HD:2 * HD, 6 + j], ACT.Copy).then_inc(o_low_done, 1)
            for r in range(2):
                act.wait_ge(pr.stored[r], NPROJ * 8)


def ssm_out_stage(m, stage):
    nc, d = m.nc, m.dram
    NK = 2 * KT
    with ExitStack() as ctx:
        sem = lambda n: m.semaphore(f"wb_{n}")
        sb = lambda n, s, t=F32: ctx.enter_context(nc.sbuf_tensor(n, s, t))
        hi, lo = sb("y_hi", [P, NK, TOK], F32R), sb("y_lo", [P, NK, TOK], F32R)
        NL = 4
        y_in = lambda k: m.resid[:, 3 + k % NL]
        sq = lambda k: m.resid[:, 1 + k % 2]
        rms = m.resid[:, KT - 1]
        landed = [sem(f"landed{r}") for r in range(NL)]
        gate_landed = [sem(f"gate_landed{r}") for r in range(2)]
        sq_summed, ot_landed = sem("sq_summed"), sem("ot_landed")
        hi_done, lo_done, sq_done, sq_used, mean, root, rms_ready = (sem(n) for n in (
            "hi_done", "lo_done", "sq_done", "sq_used", "mean", "root", "rms_ready"))
        scaled, gated = sem("scaled"), sem("gated")
        block = ctx.enter_context(nc.Block())
        units = Units(m, U_WB)
        both = lambda r: m.ps[:, 2 * r:2 * r + 2].rearrange("p a b -> p (a b)")

        @block.sync
        def _(sp):
            for k in range(NK):
                if k >= NL:
                    sp.wait_ge(lo_done, k - NL + 1)
                    sp.wait_ge(sq_done, k - NL + 1)
                sp.dma_start(y_in(k), d["yt"][k * P:(k + 1) * P, :]).then_inc(landed[k % NL], 16)
            for r in range(2):
                sp.dma_start(stage[:, r], d["proj"][(GATE0 + 8 + r) * P:(GATE0 + 9 + r) * P, :]).then_inc(gate_landed[r], 16)
            for k in range(2):
                sp.dma_start(stage[:, 2 + k], d["ot"][k * P:(k + 1) * P, :]).then_inc(ot_landed, 16)
            w = d["w_all"]

            def next_units(i, r):
                for s in range(2):
                    row = sp.snap(i * (4 * P) + (U_WB + 2 + 2 * r + s) * P)
                    sp.wait_ge(m.w_lo_ready, i * 4 + (U_WB + 1 + 2 * r + s))
                    load_unit(sp, m, s, w[bass.ds(row, P), :])
            with sp.Fori(0, KT // 2 - 1) as i:
                for r in range(2):
                    next_units(i, r)
                    row = sp.snap(i * (2 * P) + (GATE0 + 8 + 2 + r) * P)
                    sp.wait_ge(gated, i * 2 + r + 1)
                    sp.dma_start(stage[:, r], d["proj"][bass.ds(row, P), :]).then_inc(gate_landed[r], 16)
            with sp.Fori(KT // 2 - 1, KT // 2) as i:
                for r in range(2):
                    next_units(i, r)
            sp.wait_ge(ot_landed, 32)

        @block.scalar
        def _(act):
            units.hi(act, 1, 1, first=True)
            for k in range(NK):
                act.wait_ge(landed[k % NL], 16 * (k // NL + 1))
                act.activation(hi[:, k], y_in(k), ACT.Copy, scale=m.gains[:, G_SSM + k:G_SSM + k + 1]).then_inc(hi_done, 1)
                if k >= 2:
                    act.wait_ge(sq_used, max(k - 2, 1))
                act.activation(sq(k), y_in(k), ACT.Square).then_inc(sq_done, 1)
            units.hi(act, 2, 0)
            units.hi(act, 3, 1)
            act.wait_ge(mean, 1)
            act.activation(rms, rms, ACT.Sqrt).then_inc(root, 1)
            with act.Fori(2, KT) as i:
                for r in range(2):
                    units.hi(act, i * 2 + r, r)
            units.hi(act, 2 * KT, 0)

        @block.vector
        def _(dve):
            units.lo(dve, 1, 1)
            for k in range(NK):
                dve.wait_ge(hi_done, k + 1)
                dve.scalar_tensor_tensor(lo[:, k], y_in(k), m.gains[:, G_SSM + k:G_SSM + k + 1],
                                         hi[:, k].bitcast(F32), ALU.mult, ALU.subtract).then_inc(lo_done, 1)
            units.lo(dve, 2, 0)
            units.lo(dve, 3, 1)
            dve.wait_ge(sq_summed, 1)
            dve.tensor_scalar(rms, m.ps[:, 4:6].rearrange("p a b -> p (a b)"), 1.0 / (2 * D), EPS,
                              ALU.mult, ALU.add).then_inc(mean, 1)
            dve.wait_ge(root, 1)
            dve.reciprocal(rms, rms).then_inc(rms_ready, 1)
            dve.wait_ge(rms_ready, 1)

            def finish(at, r):
                dst = m.resid[:, at] if isinstance(at, int) else m.resid[:, bass.ds(dve.snap(at), 1)].squeeze(1)
                dve.wait_ge(m.w_used, at * 2 + (U_WB + 2))
                dve.tensor_tensor(dst, both(r), rms, ALU.mult).then_inc(scaled, 1)
                dve.wait_ge(gate_landed[r], (at - r) * 8 + 16)
                dve.wait_ge(scaled, at + 1)
                dve.tensor_tensor(dst, dst, stage[:, r], ALU.mult).then_inc(gated, 1)

            finish(0, 0)
            units.lo(dve, 4, 0)
            units.lo(dve, 5, 1)
            finish(1, 1)
            with dve.Fori(1, KT // 2 - 1) as i:
                for r in range(2):
                    units.lo(dve, i * 4 + 2 * r + 2, 0)
                    units.lo(dve, i * 4 + 2 * r + 3, 1)
                    finish(i * 2 + r, r)
            units.lo(dve, 2 * KT - 2, 0)
            units.lo(dve, 2 * KT - 1, 1)
            finish(KT - 2, 0)
            units.lo(dve, 2 * KT, 0)
            finish(KT - 1, 1)

        @block.gpsimd
        def _(pool):
            for k in range(1, NK):
                pool.wait_ge(sq_done, k + 1)
                if k >= 2:
                    pool.wait_ge(sq_used, k - 1)
                pool.tensor_tensor(rms, sq(0) if k == 1 else rms, sq(k), ALU.add).then_inc(sq_used, 1)

        @block.tensor
        def _(pe):

            def tile(at, r, peel):
                for s in range(2):
                    units.wait(pe, at * 2 + s)
                    if s == 0 and not peel:
                        pe.wait_ge(scaled, at - 1)
                    for n in range(2):
                        c = slice(n * BANK, (n + 1) * BANK)
                        for k in range(KT):
                            if peel and r == 0 and n == 0:
                                pe.wait_ge(lo_done, s * KT + k + 1)
                            mm = products(pe, m.ps[:, 2 * r + n],
                                          [(wslice(m, s, k * P, (k + 1) * P), (hi[:, s * KT + k, c], lo[:, s * KT + k, c]))],
                                          first_of_group=s == 0 and k == 0, last_of_group=s == 1 and k == KT - 1)
                        if peel and (r, s, n) == (1, 0, 0):
                            pe.wait_ge(sq_used, NK - 1)
                            for half in range(2):
                                total = pe.matmul(m.ps[:, 4 + half], m.con[:, CON_ONES:CON_ONES + P],
                                                  rms[:, half * BANK:(half + 1) * BANK], start=True, stop=True)
                            total.then_inc(sq_summed, 1)
                    mm.then_inc(m.w_used, 1)
            for r in range(2):
                tile(r, r, True)
            with pe.Fori(1, KT // 2) as i:
                for r in range(2):
                    tile(i * 2 + r, r, False)


def attention_out_stage(m, stage, m_hi, m_lo):
    nc, d = m.nc, m.dram
    with ExitStack() as ctx:
        sem = lambda n: m.semaphore(f"wa_{n}")
        sb = lambda n, s, t=F32: ctx.enter_context(nc.sbuf_tensor(n, s, t))
        hi, lo = sb("o_hi", [P, KT, TOK], F32R), sb("o_lo", [P, KT, TOK], F32R)
        NL = 4
        o_in = lambda k: stage[:, (k + 2) % NL]
        landed = [sem(f"landed{r}") for r in range(NL)]
        gate_landed = [sem(f"gate_landed{r}") for r in range(2)]
        hi_done, lo_done, gated, summed, m_hi_done, merged = (sem(n) for n in (
            "hi_done", "lo_done", "gated", "summed", "m_hi_done", "merged"))
        x_landed = sem("x_landed")
        block = ctx.enter_context(nc.Block())
        units = Units(m, U_WA)
        both = lambda r: m.ps[:, 2 * r:2 * r + 2].rearrange("p a b -> p (a b)")

        @block.sync
        def _(sp):
            for k in range(2, KT):
                if k >= NL:
                    sp.wait_ge(lo_done, k - NL + 1)
                sp.dma_start(o_in(k), d["ot"][k * P:(k + 1) * P, :]).then_inc(landed[k % NL], 16)
            sp.wait_ge(lo_done, KT)
            for r in range(2):
                sp.dma_start(stage[:, r], d["proj"][(GATE0 + r) * P:(GATE0 + r + 1) * P, :]).then_inc(gate_landed[r], 16)
            w = d["w_all"]
            with sp.Fori(0, KT // 2 - 1) as i:
                for r in range(2):
                    row = sp.snap(i * (2 * P) + (U_WA + 2 + r) * P)
                    g_row = sp.snap(i * (2 * P) + (GATE0 + 2 + r) * P)
                    sp.wait_ge(m.w_lo_ready, i * 2 + (U_WA + 1 + r))
                    load_unit(sp, m, r, w[bass.ds(row, P), :])
                    sp.wait_ge(merged, i * 2 + r + 1)
                    sp.dma_start(stage[:, r], d["proj"][bass.ds(g_row, P), :]).then_inc(gate_landed[r], 16)
            for r in range(2):
                sp.wait_ge(m.w_lo_ready, U_WA + KT - 1 + r)
                load_unit(sp, m, r, w[(U_WA + KT + r) * P:(U_WA + KT + r + 1) * P, :])
            for t in range(TT):
                sp.wait_ge(merged, t + 1)
                sp.dma_start(m.resid[:, t], d["x"][t * P:(t + 1) * P, :]).then_inc(x_landed, 16)
            sp.wait_ge(x_landed, TT * 16)

        @block.scalar
        def _(act):
            units.hi(act, 1, 1, first=True)
            for k in range(KT):
                if k >= 2:
                    act.wait_ge(landed[k % NL], 16 * len(range(k % NL if k % NL >= 2 else k % NL + NL, k + 1, NL)))
                act.activation(hi[:, k], o_in(k), ACT.Copy).then_inc(hi_done, 1)
            with act.Fori(1, KT // 2) as i:
                for r in range(2):
                    units.hi(act, i * 2 + r, r)
            units.hi(act, KT, 0)

        @block.vector
        def _(dve):
            for k in range(KT):
                dve.wait_ge(hi_done, k + 1)
                dve.tensor_tensor(lo[:, k], o_in(k), hi[:, k].bitcast(F32), ALU.subtract).then_inc(lo_done, 1)

            def finish(at, r):
                one = (lambda t: t[:, at]) if isinstance(at, int) else (lambda t, j=dve.snap(at): t[:, bass.ds(j, 1)].squeeze(1))
                dve.wait_ge(m.w_used, at + (U_WA + 1))
                dve.wait_ge(gate_landed[r], (at - r) * 8 + 16)
                dve.tensor_tensor(stage[:, r], both(r), stage[:, r], ALU.mult).then_inc(gated, 1)
                dve.wait_ge(gated, at + 1)
                dve.tensor_tensor(one(m.resid), one(m.resid), stage[:, r], ALU.add).then_inc(summed, 1)
                dve.wait_ge(summed, at + 1)
                dve.tensor_scalar(one(m_hi), one(m.resid), 1.0, None, ALU.mult).then_inc(m_hi_done, 1)
                dve.wait_ge(m_hi_done, at + 1)
                dve.tensor_tensor(one(m_lo), one(m.resid), one(m_hi).bitcast(F32), ALU.subtract).then_inc(merged, 1)

            with dve.Fori(0, KT // 2 - 1) as i:
                units.lo(dve, i * 2 + 1, 1)
                finish(i * 2, 0)
                units.lo(dve, i * 2 + 2, 0)
                finish(i * 2 + 1, 1)
            units.lo(dve, KT - 1, 1)
            finish(KT - 2, 0)
            units.lo(dve, KT, 0)
            finish(KT - 1, 1)

        @block.tensor
        def _(pe):
            def tile(at, r, peel):
                units.wait(pe, at)
                if not peel:
                    pe.wait_ge(gated, at - 1)
                for n in range(2):
                    c = slice(n * BANK, (n + 1) * BANK)
                    for k in range(KT):
                        if peel and r == 0 and n == 0:
                            pe.wait_ge(lo_done, k + 1)
                        mm = products(pe, m.ps[:, 2 * r + n], [(wslice(m, r, k * P, (k + 1) * P), (hi[:, k, c], lo[:, k, c]))],
                                      first_of_group=k == 0, last_of_group=k == KT - 1)
                mm.then_inc(m.w_used, 1)
            for r in range(2):
                tile(r, r, True)
            with pe.Fori(1, KT // 2) as i:
                for r in range(2):
                    tile(i * 2 + r, r, False)


def residual_stage(m, name, first, hi, lo, mem_x=None):
    nc, d = m.nc, m.dram
    n_units = KT
    with ExitStack() as ctx:
        sem = lambda n: m.semaphore(f"{name}_{n}")
        part_done, added, mem_landed = sem("part_done"), sem("added"), sem("mem_landed")
        block = ctx.enter_context(nc.Block())
        units = Units(m, first)

        @block.sync
        def _(sp):
            if mem_x is not None:
                for t in range(MT):
                    sp.dma_start(mem_x[:, t], d["mem"][t * P:(t + 1) * P, :]).then_inc(mem_landed, 16)
            stream_weights(sp, m, first, n_units)
            if mem_x is not None:
                sp.wait_ge(mem_landed, 16 * MT)

        @block.scalar
        def _(act):
            units.hi(act, 1, 1, first=True)
            with act.Fori(1, n_units // 2) as i:
                for r in range(2):
                    units.hi(act, i * 2 + r, r)
            units.hi(act, n_units, 0)

        @block.vector
        def _(dve):
            def add(u):
                col = (u % 2) * BANK
                for g in range(4):
                    wait_part(dve, units, part_done, u, g)
                    dst = m.resid[:, 2 * g:2 * g + 2, col:col + BANK]
                    dve.tensor_tensor(dst, dst, m.ps[:, 2 * (g % 2):2 * (g % 2) + 2], ALU.add).then_inc(added, 1)
            for u in range(n_units):
                units.lo(dve, u + 1, (u + 1) % 2)
                add(u)

        @block.tensor
        def _(pe):
            for u in range(n_units):
                units.wait(pe, u)
                parts(pe, m, u % 2, part_done, hi, lo, 2 * (u // 2),
                      lambda g: pe.wait_ge(added, 4 * u + g - 1) if 4 * u + g >= 2 else None)


def wait_part(eng, units, part_done, u, g):
    if g < 3:
        eng.wait_ge(part_done, u * 3 + (g + 1))
    else:
        units.products_done(eng, u)


def parts(pe, m, r, part_done, hi, lo, kt, wait_bank):
    for g in range(4):
        wait_bank(g)
        for t in (2 * g, 2 * g + 1):
            s = slice(t * P, (t + 1) * P)
            mm = products(pe, m.ps[:, 2 * (g % 2) + t % 2],
                          [((hi[:, kt + i, s], lo[:, kt + i, s]), wslice(m, r, i * BANK, (i + 1) * BANK))
                           for i in range(2)])
        mm.then_inc(part_done if g < 3 else m.w_used, 1)


def memory_stage(m, mem_hi, mem_lo, k_t, v_c, c_hi, c_lo, xn):
    nc, d = m.nc, m.dram
    NU = 2 * KT
    HALF = TT // 2
    with ExitStack() as ctx:
        sem = lambda n: m.semaphore(f"kv_{n}")
        ss = ctx.enter_context(nc.sbuf_tensor("crs_ss", [P, 3, TT], F32))
        k_read, v_read = sem("k_read"), sem("v_read")
        squared, mean, root, rstd, scaled = sem("squared"), sem("mean"), sem("root"), sem("rstd"), sem("scaled")
        turned, hi_done, lo_done = sem("turned"), sem("hi_done"), sem("lo_done")
        block = ctx.enter_context(nc.Block())
        units = Units(m, U_KV)
        part = lambda t, i: t[:, i % KT, i // KT * BANK:(i // KT + 1) * BANK]
        gain = lambda i: m.gains[:, G_CROSS + i % KT:G_CROSS + i % KT + 1]

        @block.sync
        def _(sp):
            stream_weights(sp, m, U_KV, NU)

        @block.scalar
        def _(act):
            def statistics(n):
                if n:
                    act.wait_ge(turned, n * KT)
                for t in range(HALF * n, HALF * (n + 1)):
                    act.activation(xn[:, t % HALF], m.resid[:, t], ACT.Square,
                                   accum_out=ss[:, 0, t:t + 1]).then_inc(squared, 1)
                act.wait_ge(mean, n + 1)
                s = slice(HALF * n, HALF * (n + 1))
                act.activation(ss[:, 2, s], ss[:, 1, s], ACT.Sqrt).then_inc(root, 1)

            def split_group(i):
                act.wait_ge(turned, i + 1)
                act.activation(part(c_hi, i), m.ps[:, 2 + i % 2], ACT.Copy, scale=gain(i)).then_inc(hi_done, 1)

            for u in range(NU):
                units.hi(act, u + 1, (u + 1) % 2, first=u == 0)
                if u % KT == 0:
                    statistics(u // KT)
                if u >= 1:
                    split_group(u - 1)
            split_group(NU - 1)

        @block.vector
        def _(dve):
            def statistics(n):
                s = slice(HALF * n, HALF * (n + 1))
                dve.wait_ge(squared, HALF * (n + 1))
                dve.tensor_scalar(ss[:, 1, s], ss[:, 0, s], 1.0 / D, EPS, ALU.mult, ALU.add).then_inc(mean, 1)
                dve.wait_ge(root, n + 1)
                dve.reciprocal(ss[:, 0, s], ss[:, 2, s]).then_inc(rstd, 1)
                dve.wait_ge(rstd, n + 1)
                for t in range(HALF * n, HALF * (n + 1)):
                    dve.tensor_scalar(xn[:, t % HALF], m.resid[:, t], ss[:, 0, t:t + 1], None,
                                      ALU.mult).then_inc(scaled, 1)

            def low_group(i):
                dve.wait_ge(hi_done, i + 1)
                dve.scalar_tensor_tensor(part(c_lo, i), m.ps[:, 2 + i % 2], gain(i), part(c_hi, i).bitcast(F32),
                                         ALU.mult, ALU.subtract).then_inc(lo_done, 1)

            for u in range(NU):
                units.lo(dve, u + 1, (u + 1) % 2)
                if u % KT == 0:
                    statistics(u // KT)
                if u < KT:
                    units.products_done(dve, u)
                    dve.tensor_copy(k_t[:, u], m.ps[:, u % 2]).then_inc(k_read, 1)
                elif u % 4 == 3:
                    n = (u - KT) // 4
                    units.products_done(dve, u)
                    for t in range(MT):
                        dve.tensor_copy(v_c[:, t, n * BANK:(n + 1) * BANK], m.ps[:, 4 + t]).then_inc(v_read, 1)
                if u >= 1:
                    low_group(u - 1)
            low_group(NU - 1)

        @block.tensor
        def _(pe):
            def turn(i):
                if i % KT == 0:
                    pe.wait_ge(scaled, HALF * (i // KT + 1))
                if i >= 2:
                    pe.wait_ge(lo_done, i - 1)
                for t in range(HALF):
                    mm = pe.transpose(m.ps[:, 2 + i % 2, t * P:(t + 1) * P], xn[:, t, i % KT * P:(i % KT + 1) * P],
                                      m.con[:, CON_ID:CON_ID + P])
                mm.then_inc(turned, 1)

            for u in range(NU):
                units.wait(pe, u)
                if u < KT:
                    if u >= 2:
                        pe.wait_ge(k_read, u - 1)
                    mm = products(pe, m.ps[:, u % 2], [(wslice(m, u % 2, k * P, (k + 1) * P), (mem_hi[:, k], mem_lo[:, k]))
                                                       for k in range(KT)])
                else:
                    kp = u % 4
                    if u == KT + 4:
                        pe.wait_ge(v_read, MT)
                    for t in range(MT):
                        s = slice(t * P, (t + 1) * P)
                        mm = products(pe, m.ps[:, 4 + t],
                                      [((mem_hi[:, 2 * kp + i, s], mem_lo[:, 2 * kp + i, s]),
                                        wslice(m, u % 2, i * BANK, (i + 1) * BANK)) for i in range(2)],
                                      first_of_group=kp == 0, last_of_group=kp == 3)
                mm.then_inc(m.w_used, 1)
                if u >= 1:
                    turn(u - 1)
            turn(NU - 1)


def query_stage(m, u_hi, u_lo, q_t):
    nc, d = m.nc, m.dram
    with ExitStack() as ctx:
        drained = m.semaphore("q_drained")
        block = ctx.enter_context(nc.Block())
        units = Units(m, U_Q)

        @block.sync
        def _(sp):
            stream_weights(sp, m, U_Q, KT)

        @block.scalar
        def _(act):
            units.hi(act, 1, 1, first=True)
            with act.Fori(1, KT // 2) as i:
                for r in range(2):
                    units.hi(act, i * 2 + r, r)
            units.hi(act, KT, 0)

        @block.vector
        def _(dve):
            def finish(at, r):
                dst = q_t[:, at] if isinstance(at, int) else q_t[:, bass.ds(dve.snap(at), 1)].squeeze(1)
                units.products_done(dve, at)
                dve.tensor_scalar(dst, m.ps[:, 2 * r:2 * r + 2].rearrange("p a b -> p (a b)"), XHD ** -0.5, None,
                                  ALU.mult).then_inc(drained, 1)
            with dve.Fori(0, KT // 2 - 1) as i:
                units.lo(dve, i * 2 + 1, 1)
                finish(i * 2, 0)
                units.lo(dve, i * 2 + 2, 0)
                finish(i * 2 + 1, 1)
            units.lo(dve, KT - 1, 1)
            finish(KT - 2, 0)
            units.lo(dve, KT, 0)
            finish(KT - 1, 1)

        @block.tensor
        def _(pe):
            def tile(at, r, peel):
                units.wait(pe, at)
                if not peel:
                    pe.wait_ge(drained, at - 1)
                for n in range(2):
                    c = slice(n * BANK, (n + 1) * BANK)
                    mm = products(pe, m.ps[:, 2 * r + n],
                                  [(wslice(m, r, k * P, (k + 1) * P), (u_hi[:, k, c], u_lo[:, k, c])) for k in range(KT)])
                mm.then_inc(m.w_used, 1)
            for r in range(2):
                tile(r, r, True)
            with pe.Fori(1, KT // 2) as i:
                for r in range(2):
                    tile(i * 2 + r, r, False)


def cross_stage(m, q_t, k_t, v_c, o_hi, o_lo, stage):
    nc = m.nc
    with ExitStack() as ctx:
        sem = lambda n: m.semaphore(f"cr_{n}")
        sb = lambda n, s, t=F32: ctx.enter_context(nc.sbuf_tensor(n, s, t))
        p = stage[:, 0:2].rearrange("p s (h k) -> p s h k", h=XH)
        pt = stage[:, 2:4].rearrange("p s (h k) -> p s h k", h=2 * XH)
        st = sb("cr_st", [P, 2, 3, XH])
        s_done, neg_max, exp_done, inv, normed, p_turned, pt_ready, o_done, hi_done, lo_done = (sem(n) for n in (
            "s_done", "neg_max", "exp_done", "inv", "normed", "p_turned", "pt_ready", "o_done", "hi_done", "lo_done"))
        block = ctx.enter_context(nc.Block())
        scores = m.ps[:, 4:6].rearrange("p a (h k) -> p (a h) k", h=2)

        @block.tensor
        def _(pe):
            ident = m.con[:, CON_ID:CON_ID + P]

            def score(t):
                s = t // BLOCKS
                if t:
                    pe.wait_ge(exp_done, XH * t)
                for h in range(XH):
                    for i in range(2):
                        mm = pe.matmul(scores[:, h], q_t[:, 2 * h + i, t * P:(t + 1) * P],
                                       k_t[:, 2 * h + i, s * MEM:(s + 1) * MEM], start=i == 0, stop=i == 1)
                mm.then_inc(s_done, 1)

            def turn(t):
                for n in range(2):
                    pe.wait_ge(normed, XH * t + 2 * n + 2)
                    if t:
                        pe.wait_ge(pt_ready, 2 * (t - 1) + n + 1)
                    for i in range(4):
                        h, kb = divmod(4 * n + i, 2)
                        mm = pe.transpose(m.ps[:, 6 + n, i * P:(i + 1) * P], p[:, t % 2, h, kb * P:(kb + 1) * P], ident)
                    mm.then_inc(p_turned, 1)

            score(0)
            score(1)
            turn(0)
            for t in range(TT):
                s = t // BLOCKS
                if t + 2 < TT:
                    score(t + 2)
                if t + 1 < TT:
                    turn(t + 1)
                if t >= 2:
                    pe.wait_ge(lo_done, 2 * (t - 1))
                for n in range(2):
                    pe.wait_ge(pt_ready, 2 * t + n + 1)
                    for i in range(4):
                        f = 4 * n + i
                        h = f // 2
                        for kb in range(2):
                            mm = pe.matmul(m.ps[:, 2 * (t % 2) + n, i * P:(i + 1) * P], v_c[:, 2 * s + kb, f * P:(f + 1) * P],
                                           pt[:, t % 2, 2 * h + kb], start=kb == 0, stop=kb == 1)
                    mm.then_inc(o_done, 1)

        @block.vector
        def _(dve):
            def maxima(t):
                dve.wait_ge(s_done, t + 1)
                dve.tensor_reduce(st[:, t % 2, 0], scores, AX.X, ALU.max, negate=True).then_inc(neg_max, 1)

            def normalise(t):
                dve.wait_ge(exp_done, XH * (t + 1))
                dve.reciprocal(st[:, t % 2, 2], st[:, t % 2, 1]).then_inc(inv, 1)
                dve.wait_ge(inv, t + 1)
                for h in range(XH):
                    dve.tensor_scalar(p[:, t % 2, h], p[:, t % 2, h], st[:, t % 2, 2, h:h + 1], None,
                                      ALU.mult).then_inc(normed, 1)

            for t in range(2):
                maxima(t)
                normalise(t)
            for t in range(TT):
                if t + 2 < TT:
                    maxima(t + 2)
                    normalise(t + 2)
                for n in range(2):
                    dve.wait_ge(hi_done, 2 * t + n + 1)
                    dst = (slice(None), slice(4 * n, 4 * n + 4), slice(t * P, (t + 1) * P))
                    dve.tensor_tensor(o_lo[dst], m.ps[:, 2 * (t % 2) + n].rearrange("p (a b) -> p a b", a=4),
                                      o_hi[dst].bitcast(F32), ALU.subtract).then_inc(lo_done, 1)

        @block.scalar
        def _(act):
            def exponents(t):
                act.wait_ge(neg_max, t + 1)
                if t >= 2:
                    act.wait_ge(p_turned, 2 * (t - 1))
                for h in range(XH):
                    act.activation(p[:, t % 2, h], scores[:, h], ACT.Exp, bias=st[:, t % 2, 0, h:h + 1],
                                   accum_out=st[:, t % 2, 1, h:h + 1]).then_inc(exp_done, 1)

            def copy_turned(t):
                for n in range(2):
                    act.wait_ge(p_turned, 2 * t + n + 1)
                    if t >= 2:
                        act.wait_ge(o_done, 2 * (t - 1))
                    act.activation(pt[:, t % 2, 4 * n:4 * n + 4].rearrange("p a b -> p (a b)"), m.ps[:, 6 + n],
                                   ACT.Copy).then_inc(pt_ready, 1)

            exponents(0)
            exponents(1)
            copy_turned(0)
            for t in range(TT):
                if t + 2 < TT:
                    exponents(t + 2)
                if t + 1 < TT:
                    copy_turned(t + 1)
                for n in range(2):
                    act.wait_ge(o_done, 2 * t + n + 1)
                    act.activation(o_hi[:, 4 * n:4 * n + 4, t * P:(t + 1) * P],
                                   m.ps[:, 2 * (t % 2) + n].rearrange("p (a b) -> p a b", a=4), ACT.Copy).then_inc(hi_done, 1)


def ffn_stage(m, u_hi, u_lo):
    nc, d = m.nc, m.dram
    NC = HT // 2
    with ExitStack() as ctx:
        sem = lambda n: m.semaphore(f"ffn_{n}")
        sb = lambda n, s, t=F32: ctx.enter_context(nc.sbuf_tensor(n, s, t))
        g = sb("ffn_g", [P, 2, TOK])
        h_hi, h_lo = sb("h_hi", [P, 2, TOK], F32R), sb("h_lo", [P, 2, TOK], F32R)
        silu, prod, h_hi_done, h_ready, part_done, added = (sem(n) for n in (
            "silu", "prod", "h_hi_done", "h_ready", "part_done", "added"))
        block = ctx.enter_context(nc.Block())
        units = Units(m, U_FFN)
        both = lambda r: m.ps[:, 2 * r:2 * r + 2].rearrange("p a b -> p (a b)")
        at = lambda c, k: (c - 1) * 6 + (4 + k)

        @block.sync
        def _(sp):
            stream_weights(sp, m, U_FFN, 3 * HT)

        @block.scalar
        def _(act):
            def gate(u, c, r, first=False):
                if not first:
                    act.wait_ge(h_ready, c * 2 + (r - 1))
                units.products_done(act, u)
                act.activation(g[:, r], both(r), ACT.Silu).then_inc(silu, 1)

            def hidden(c, r):
                act.wait_ge(prod, c * 2 + (r + 1))
                act.activation(h_hi[:, r], g[:, r], ACT.Copy).then_inc(h_hi_done, 1)

            units.hi(act, 1, 1, first=True)
            gate(0, 0, 0, True)
            units.hi(act, 2, 0)
            gate(1, 0, 1, True)
            units.hi(act, 3, 1)
            units.hi(act, 4, 0)
            hidden(0, 0)
            units.hi(act, 5, 1)
            hidden(0, 1)
            with act.Fori(1, NC) as c:
                gate(at(c, 0), c, 0)
                units.hi(act, at(c, 2), 0)
                gate(at(c, 1), c, 1)
                units.hi(act, at(c, 3), 1)
                units.hi(act, at(c, 4), 0)
                units.hi(act, at(c, 5), 1)
                units.hi(act, at(c, 6), 0)
                hidden(c, 0)
                hidden(c, 1)
                units.hi(act, at(c, 7), 1)

        @block.vector
        def _(dve):
            def up(u, c, r):
                dve.wait_ge(silu, c * 2 + (r + 1))
                units.products_done(dve, u)
                dve.tensor_tensor(g[:, r], both(r), g[:, r], ALU.mult).then_inc(prod, 1)

            def low(c, r):
                dve.wait_ge(h_hi_done, c * 2 + (r + 1))
                dve.tensor_tensor(h_lo[:, r], g[:, r], h_hi[:, r].bitcast(F32), ALU.subtract).then_inc(h_ready, 1)

            def down(u, d_at, n):
                for k in range(4):
                    if k < 3:
                        dve.wait_ge(part_done, d_at * 3 + (k + 1))
                    else:
                        units.products_done(dve, u)
                    dst = m.resid[:, 2 * k:2 * k + 2, n * BANK:(n + 1) * BANK]
                    dve.tensor_tensor(dst, dst, m.ps[:, 2 * (k % 2):2 * (k % 2) + 2], ALU.add).then_inc(added, 1)

            for u in range(1, 4):
                units.lo(dve, u, u % 2)
            units.lo(dve, 4, 0)
            up(2, 0, 0)
            units.lo(dve, 5, 1)
            up(3, 0, 1)
            low(0, 0)
            low(0, 1)
            with dve.Fori(1, NC) as c:
                units.lo(dve, at(c, 2), 0)
                units.lo(dve, at(c, 3), 1)
                down(at(c, 2), c * 2 - 2, 0)
                units.lo(dve, at(c, 4), 0)
                down(at(c, 3), c * 2 - 1, 1)
                units.lo(dve, at(c, 5), 1)
                units.lo(dve, at(c, 6), 0)
                up(at(c, 4), c, 0)
                low(c, 0)
                up(at(c, 5), c, 1)
                low(c, 1)
                units.lo(dve, at(c, 7), 1)
            down(at(NC, 0), 2 * NC - 2, 0)
            down(at(NC, 1), 2 * NC - 1, 1)

        @block.tensor
        def _(pe):
            def tile(u, r):
                units.wait(pe, u)
                for n in range(2):
                    s = slice(n * BANK, (n + 1) * BANK)
                    mm = products(pe, m.ps[:, 2 * r + n],
                                  [(wslice(m, r, k * P, (k + 1) * P), (u_hi[:, k, s], u_lo[:, k, s])) for k in range(KT)])
                mm.then_inc(m.w_used, 1)

            def down(u, d_at, n, c):
                units.wait(pe, u)

                def bank_free(k):
                    if n == 0 and k < 2:
                        if k == 0:
                            pe.wait_ge(silu, c * 2 + 2)
                    else:
                        pe.wait_ge(added, d_at * 4 + (k - 1))
                parts(pe, m, n, part_done, h_hi, h_lo, 0, bank_free)

            tile(0, 0)
            tile(1, 1)
            pe.wait_ge(silu, 1)
            tile(2, 0)
            pe.wait_ge(silu, 2)
            tile(3, 1)
            with pe.Fori(1, NC) as c:
                pe.wait_ge(prod, c * 2 - 1)
                tile(at(c, 0), 0)
                pe.wait_ge(prod, c * 2)
                tile(at(c, 1), 1)
                pe.wait_ge(h_ready, c * 2)
                down(at(c, 2), c * 2 - 2, 0, c)
                down(at(c, 3), c * 2 - 1, 1, c)
                pe.wait_ge(added, c * 8 - 1)
                tile(at(c, 4), 0)
                pe.wait_ge(added, c * 8)
                tile(at(c, 5), 1)
            pe.wait_ge(h_ready, 2 * NC)
            pe.wait_ge(prod, 2 * NC)
            down(at(NC, 0), 2 * NC - 2, 0, NC - 1)
            down(at(NC, 1), 2 * NC - 1, 1, NC - 1)


def final_stage(m):
    nc, d = m.nc, m.dram
    with ExitStack() as ctx:
        sem = lambda n: m.semaphore(f"fin_{n}")
        sq = ctx.enter_context(nc.sbuf_tensor("fin_sq", [P, 2, D], F32))
        ss = ctx.enter_context(nc.sbuf_tensor("fin_ss", [P, 3, TT], F32))
        gain = ctx.enter_context(nc.sbuf_tensor("fin_gain", [P, D], F32))
        squared, mean, root, rstd, ready, stored, gain_landed = (sem(n) for n in (
            "squared", "mean", "root", "rstd", "ready", "stored", "gain_landed"))
        block = ctx.enter_context(nc.Block())

        @block.scalar
        def _(act):
            for n in range(TT // 2):
                for t in (2 * n, 2 * n + 1):
                    if t >= 2:
                        act.wait_ge(squared, t - 1)
                    act.activation(sq[:, t % 2], m.resid[:, t], ACT.Square, accum_out=ss[:, 0, t:t + 1]).then_inc(squared, 1)
                act.wait_ge(mean, n + 1)
                act.activation(ss[:, 2, 2 * n:2 * n + 2], ss[:, 1, 2 * n:2 * n + 2], ACT.Sqrt).then_inc(root, 1)

        @block.vector
        def _(dve):
            for n in range(TT // 2):
                pair = slice(2 * n, 2 * n + 2)
                dve.wait_ge(squared, 2 * n + 2)
                dve.tensor_scalar(ss[:, 1, pair], ss[:, 0, pair], 1.0 / D, EPS, ALU.mult, ALU.add).then_inc(mean, 1)
                dve.wait_ge(root, n + 1)
                dve.reciprocal(ss[:, 0, pair], ss[:, 2, pair]).then_inc(rstd, 1)
                dve.wait_ge(rstd, n + 1)
                if n == 0:
                    dve.wait_ge(gain_landed, 16)
                for t in (2 * n, 2 * n + 1):
                    dve.scalar_tensor_tensor(m.resid[:, t], m.resid[:, t], ss[:, 0, t:t + 1],
                                             gain[:], ALU.mult, ALU.mult).then_inc(ready, 1)

        @block.sync
        def _(sp):
            sp.dma_start(gain[:], d["g_final"].partition_broadcast(P)).then_inc(gain_landed, 16)
            for t in range(TT):
                sp.wait_ge(ready, t + 1)
                sp.dma_start(d["y"][t * P:(t + 1) * P, :], m.resid[:, t]).then_inc(stored, 16)
            sp.wait_ge(stored, 16 * TT)


def build(nc, dram):
    with ExitStack() as top:
        m = open_core(nc, top, dram)
        sb = lambda ctx, n, s, t=F32: ctx.enter_context(nc.sbuf_tensor(n, s, t))
        with ExitStack() as mix:
            m.w_dt = sb(mix, "w_dt", [P, KT * 64])
            u_hi, u_lo = sb(mix, "u_hi", [P, KT, TOK], F32R), sb(mix, "u_lo", [P, KT, TOK], F32R)
            norm_stage(m, "mix", dram["x"], G_MIX, u_hi, u_lo, TT, True, first_stage=True)
            pr = Projection(m, mix)
            first_stage(m, pr, u_hi, u_lo)
            ssd_stage(m, pr, u_hi, u_lo)
            attention_stage(m, pr, u_hi, u_lo)
        m.resid = sb(top, "resid", [P, TT, D])
        mid = top.enter_context(ExitStack())
        stage = sb(mid, "stage", [P, 4, D])
        ssm_out_stage(m, stage)
        with ExitStack() as ctx:
            m_hi, m_lo = sb(ctx, "m_hi", [P, KT, TOK], F32R), sb(ctx, "m_lo", [P, KT, TOK], F32R)
            attention_out_stage(m, stage, m_hi, m_lo)
            residual_stage(m, "out", U_OUT, m_hi, m_lo, mem_x=stage)
        m.recycle()
        with ExitStack() as ctx:
            k_t, v_c = sb(ctx, "k_t", [P, KT, NSEQ * MEM]), sb(ctx, "v_c", [P, MT, D])
            c_hi, c_lo = sb(ctx, "c_hi", [P, KT, TOK], F32R), sb(ctx, "c_lo", [P, KT, TOK], F32R)
            with ExitStack() as c2:
                mem_hi, mem_lo = (sb(c2, n, [P, KT, NSEQ * MEM], F32R) for n in ("mem_hi", "mem_lo"))
                norm_stage(m, "mem", stage, G_MEM, mem_hi, mem_lo, MT, False, xn=v_c)
                memory_stage(m, mem_hi, mem_lo, k_t, v_c, c_hi, c_lo, stage)
            q_t = sb(ctx, "q_t", [P, KT, TOK])
            query_stage(m, c_hi, c_lo, q_t)
            cross_stage(m, q_t, k_t, v_c, c_hi, c_lo, stage)
            residual_stage(m, "wo", U_O, c_hi, c_lo)
        mid.close()
        with ExitStack() as ctx:
            f_hi, f_lo = sb(ctx, "f_hi", [P, KT, TOK], F32R), sb(ctx, "f_lo", [P, KT, TOK], F32R)
            norm_stage(m, "ffn", m.resid, G_FFN, f_hi, f_lo, TT, False)
            ffn_stage(m, f_hi, f_lo)
        final_stage(m)



def tiles_a(w):
    k, n = w.shape
    return w.reshape(KT, P, n // P, P).transpose(2, 1, 0, 3).reshape(-1, 1024)


def tiles_b(w):
    k, n = w.shape
    return w.reshape(k // (2 * P), 2, P, n // BANK, BANK).transpose(0, 3, 2, 1, 4).reshape(-1, 1024)


def lay_out(i):
    a = {k: np.asarray(v) for k, v in i.items()}
    w = a["w_in"][0]
    c = 1536
    z, xbc, dtw, gates = w[:, c:c + 2048], w[:, c + 2048:c + 5120], w[:, c + 5120:c + 5184], w[:, c + 5184:]
    chans = np.concatenate([np.r_[g * GW:(g + 1) * GW, 2048 + g * P:2048 + (g + 1) * P, 2560 + g * P:2560 + (g + 1) * P]
                            for g in range(GROUPS)])
    kv = a["w_kv_cross"][0]
    v_units = kv[:, 1024:].reshape(4, 2, P, 2, BANK).transpose(3, 0, 2, 1, 4).reshape(-1, 1024)
    gu = a["w_gate_up"][0]
    gate, up = (tiles_a(gu[:, s:s + HID]).reshape(HT // 2, 2 * P, 1024) for s in (0, HID))
    down = tiles_b(a["w_down"][0]).reshape(HT // 2, 2 * P, 1024)
    ffn = [gate[0], up[0]]
    for k in range(1, HT // 2):
        ffn += [gate[k], down[k - 1], up[k]]
    ffn.append(down[-1])
    wb = a["w_br_ssm"][0].reshape(2, KT, P, KT, P).transpose(3, 0, 2, 1, 4).reshape(-1, 1024)
    groups = [tiles_a(np.concatenate([z[:, g * GW:(g + 1) * GW], xbc[:, chans[g * CT * P:(g + 1) * CT * P]]], axis=1))
              for g in range(GROUPS)]
    w_all = np.concatenate([tiles_a(w[:, 1280:1536]), *groups, tiles_a(w[:, :1280]), tiles_a(gates), wb,
                            tiles_a(a["w_br_attn"][0]), tiles_b(a["w_out"][0]), tiles_a(kv[:, :1024]), v_units,
                            tiles_a(a["w_q_cross"][0]), tiles_b(a["w_o_cross"][0]), *ffn])
    taps = np.concatenate([a["conv_w"][0], a["conv_b"][0][None]])[:, chans]
    taps = taps.reshape(TAPS + 1, GROUPS, CT, P).transpose(1, 3, 2, 0).reshape(GROUPS * P, CT * (TAPS + 1))
    col = lambda n: a[n].reshape(-1, P).T
    return {
        "x": np.concatenate([a["x_prompt"][0], a["x_sample"][0]]),
        "mem": np.concatenate([a["mem_prompt"][0], a["mem_sample"][0]]),
        "w_all": w_all,
        "w_dt": dtw.reshape(KT, P, 64).transpose(1, 0, 2).reshape(P, KT * 64),
        "taps": taps,
        "gains": np.concatenate([col(n) for n in ("norm_mix", "norm_cross", "norm_mem", "norm_ffn", "ssm_norm")], axis=1),
        "rows": np.concatenate([a["a_log"].ravel(), a["dt_bias"].ravel(), a["d_skip"].ravel(), a["attn_sink"].ravel()]),
        "g_final": a["norm_final"].ravel(),
        "con": constants(),
    }


def kernel(**inputs):
    import concourse.bacc as bacc
    from concourse.bass_utils import run_bass_kernel_spmd

    arrays = {k: np.ascontiguousarray(v) for k, v in lay_out(inputs).items()}
    nc = bacc.Bacc("TRN2", target_bir_lowering=False, num_devices=1)
    dram = {k: nc.dram_tensor(f"{k}_dram", v.shape, F32, kind="ExternalInput").ap() for k, v in arrays.items()}
    for name, tiles in (("proj", NPROJ), ("yt", 2 * KT), ("ot", KT)):
        dram[name] = nc.dram_tensor(f"{name}_dram", [tiles * P, TOK], F32, kind="Internal").ap()
    dram["steps"] = nc.dram_tensor("steps_dram", [GROUPS * P, STEPW], F32, kind="Internal").ap()
    dram["sums"] = nc.dram_tensor("sums_dram", [GROUPS * TT * 2, 2 * BANK], F32, kind="Internal").ap()
    dram["y"] = nc.dram_tensor("y_dram", [TOK, D], F32, kind="ExternalOutput").ap()
    build(nc, dram)
    y = run_bass_kernel_spmd(nc, [{f"{k}_dram": v for k, v in arrays.items()}], core_ids=[0]).results[0]["y_dram"]
    return y[:SEQ][None], y[SEQ:][None]
```
